# Optimizing a Trainium2 kernel written in Bass

```python
import jax
import jax.numpy as jnp
from jax import lax
import numpy as np
import jax, jax.numpy as jnp

D_MODEL = 2048
BATCH = 1
SEQ = 256
DEPTH = 2

MIX_WIDTH = 2048
CONV_WIDTH = 1024
CONV_KERNEL = 31
MOBA_HEADS = 8
MOBA_HEAD_DIM = 128
MOBA_WIDTH = MOBA_HEADS * MOBA_HEAD_DIM
MOBA_BLOCK = 256
MOBA_TOPK = 3
MOBA_QCHUNK = 32
EVEN_IN = 3 * CONV_WIDTH + 4 * MOBA_WIDTH
DSA_HEADS = 16
DSA_HEAD_DIM = 128
DSA_WIDTH = DSA_HEADS * DSA_HEAD_DIM
Q_LORA = 512
KV_LORA = 256
IDX_HEADS = 16
IDX_DIM = 64
DSA_TOPK_MAX = 256
DSA_QCHUNK = 128
ODD_IN = Q_LORA + KV_LORA + IDX_DIM + IDX_HEADS + DSA_WIDTH
N_EVEN = (DEPTH + 1) // 2
N_ODD = DEPTH // 2
EPS = 1e-6


def _rmsnorm(x, g):
    xf = x.astype(jnp.float32)
    y = xf * lax.rsqrt(jnp.mean(xf * xf, axis=-1, keepdims=True) + EPS)
    return (y * g.astype(jnp.float32)).astype(x.dtype)

def _layernorm(x, g, b):
    xf = x.astype(jnp.float32)
    mu = jnp.mean(xf, axis=-1, keepdims=True)
    xc = xf - mu
    y = xc * lax.rsqrt(jnp.mean(xc * xc, axis=-1, keepdims=True) + EPS)
    return (y * g.astype(jnp.float32) + b.astype(jnp.float32)).astype(x.dtype)

def _split_cols(z, sizes):
    out = []
    off = 0
    for s in sizes:
        out.append(z[..., off:off + s])
        off += s
    return out

def _conformer_conv(a_val, a_gt, w_dw, b_dw, ln_g, ln_b, w_pw, b_pw):
    u = a_val * jax.nn.sigmoid(a_gt)
    y = lax.conv_general_dilated(
        u, w_dw[:, None, :], window_strides=(1,), padding=[(CONV_KERNEL - 1, 0)],
        dimension_numbers=('NWC', 'WIO', 'NWC'), feature_group_count=CONV_WIDTH) + b_dw
    y = jax.nn.silu(_layernorm(y, ln_g, ln_b))
    return y @ w_pw + b_pw

def _moba_attention(q, k, v):
    b, t, h, dh = q.shape
    nb = -(-t // MOBA_BLOCK)
    pad = nb * MOBA_BLOCK - t
    q = q.transpose(0, 2, 1, 3)
    k = jnp.pad(k.transpose(0, 2, 1, 3), ((0, 0), (0, 0), (0, pad), (0, 0)))
    v = jnp.pad(v.transpose(0, 2, 1, 3), ((0, 0), (0, 0), (0, pad), (0, 0)))
    kb = k.reshape(b, h, nb, MOBA_BLOCK, dh)
    vb = v.reshape(b, h, nb, MOBA_BLOCK, dh)
    n_sel = min(MOBA_TOPK, nb - 1)
    scale = dh ** -0.5
    sel = None
    if n_sel > 0:
        k_mean = jnp.mean(kb, axis=3)
        gate = jnp.einsum('bhtd,bhnd->bhtn', q, k_mean)
        cur = jnp.arange(t) // MOBA_BLOCK
        fully_past = jnp.arange(nb)[None, :] < cur[:, None]
        gate = jnp.where(fully_past, gate, -jnp.inf)
        sel = lax.top_k(gate, n_sel)[1]
    bi = jnp.arange(b)[:, None, None, None]
    hi = jnp.arange(h)[None, :, None, None]

    def chunk(c):
        t0 = c * MOBA_QCHUNK
        blk = t0 // MOBA_BLOCK
        qc = lax.dynamic_slice_in_dim(q, t0, MOBA_QCHUNK, axis=2)
        k_own = lax.dynamic_index_in_dim(kb, blk, axis=2, keepdims=False)
        v_own = lax.dynamic_index_in_dim(vb, blk, axis=2, keepdims=False)
        qpos = t0 + jnp.arange(MOBA_QCHUNK)
        kpos = blk * MOBA_BLOCK + jnp.arange(MOBA_BLOCK)
        s_own = jnp.einsum('bhqd,bhsd->bhqs', qc, k_own) * scale
        s_own = jnp.where(kpos[None, :] <= qpos[:, None], s_own, -jnp.inf)
        if n_sel == 0:
            p = jax.nn.softmax(s_own.astype(jnp.float32), axis=-1).astype(v.dtype)
            return jnp.einsum('bhqs,bhsd->bhqd', p, v_own)
        sel_c = lax.dynamic_slice_in_dim(sel, t0, MOBA_QCHUNK, axis=2)
        k_sel = kb[bi, hi, sel_c]
        v_sel = vb[bi, hi, sel_c]
        s_past = jnp.einsum('bhqd,bhqksd->bhqks', qc, k_sel) * scale
        s_past = jnp.where((sel_c < blk)[..., None], s_past, -jnp.inf)
        logits = jnp.concatenate(
            [s_past.reshape(b, h, MOBA_QCHUNK, n_sel * MOBA_BLOCK), s_own], axis=-1)
        p = jax.nn.softmax(logits.astype(jnp.float32), axis=-1).astype(v.dtype)
        p_past = p[..., :n_sel * MOBA_BLOCK].reshape(b, h, MOBA_QCHUNK, n_sel, MOBA_BLOCK)
        p_own = p[..., n_sel * MOBA_BLOCK:]
        return (jnp.einsum('bhqks,bhqksd->bhqd', p_past, v_sel)
                + jnp.einsum('bhqs,bhsd->bhqd', p_own, v_own))

    out = lax.map(chunk, jnp.arange(t // MOBA_QCHUNK))
    return out.transpose(1, 0, 3, 2, 4).reshape(b, t, h * dh)

def _dsa_attention(q_lat, ckv, iq, ik, iw):
    b, t, h, c = q_lat.shape
    k_top = min(DSA_TOPK_MAX, t // 4)
    scale = DSA_HEAD_DIM ** -0.5
    bi = jnp.arange(b)[:, None, None]
    kpos = jnp.arange(t)

    def chunk(ci):
        t0 = ci * DSA_QCHUNK
        qpos = t0 + jnp.arange(DSA_QCHUNK)
        iq_c = lax.dynamic_slice_in_dim(iq, t0, DSA_QCHUNK, axis=1)
        iw_c = lax.dynamic_slice_in_dim(iw, t0, DSA_QCHUNK, axis=1)
        ql_c = lax.dynamic_slice_in_dim(q_lat, t0, DSA_QCHUNK, axis=1)
        idx = jnp.einsum('bqhd,bsd->bqhs', iq_c, ik)
        score = jnp.einsum('bqhs,bqh->bqs', jax.nn.relu(idx), iw_c)
        score = jnp.where(kpos[None, :] <= qpos[:, None], score, -jnp.inf)
        sel = lax.top_k(score, k_top)[1]
        kv = ckv[bi, sel]
        s = jnp.einsum('bqhc,bqkc->bqhk', ql_c, kv) * scale
        s = jnp.where((sel <= qpos[None, :, None])[:, :, None, :], s, -jnp.inf)
        p = jax.nn.softmax(s.astype(jnp.float32), axis=-1).astype(kv.dtype)
        return jnp.einsum('bqhk,bqkc->bqhc', p, kv)

    out = lax.map(chunk, jnp.arange(t // DSA_QCHUNK))
    return out.transpose(1, 0, 2, 3, 4).reshape(b, t, h, c)

def _even_layer(x, norm_g, w_in, b_glu, w_dw, b_dw, ln_g, ln_b, w_pw, b_pw, w_out):
    b, t, _ = x.shape
    z = _rmsnorm(x, norm_g) @ w_in
    a_val, a_gt, a_gate, q, k, v, b_gate = _split_cols(
        z, [CONV_WIDTH, CONV_WIDTH, CONV_WIDTH, MOBA_WIDTH, MOBA_WIDTH, MOBA_WIDTH, MOBA_WIDTH])
    ya = _conformer_conv(a_val + b_glu[:CONV_WIDTH], a_gt + b_glu[CONV_WIDTH:],
                         w_dw, b_dw, ln_g, ln_b, w_pw, b_pw) * jax.nn.silu(a_gate)
    shp = (b, t, MOBA_HEADS, MOBA_HEAD_DIM)
    yb = _moba_attention(q.reshape(shp), k.reshape(shp), v.reshape(shp)) * jax.nn.silu(b_gate)
    return jnp.concatenate([ya, yb], axis=-1) @ w_out

def _odd_layer(x, norm_g, w_in, q_norm, w_qb, kv_norm, w_uk, w_uv, w_iq, ik_g, ik_b, w_out):
    b, t, _ = x.shape
    z = _rmsnorm(x, norm_g) @ w_in
    cq, ckv, ik, iw, gate = _split_cols(z, [Q_LORA, KV_LORA, IDX_DIM, IDX_HEADS, DSA_WIDTH])
    cq = _rmsnorm(cq, q_norm)
    q = (cq @ w_qb).reshape(b, t, DSA_HEADS, DSA_HEAD_DIM)
    q_lat = jnp.einsum('bthd,hdc->bthc', q, w_uk)
    ckv = _rmsnorm(ckv, kv_norm)
    iq = (cq @ w_iq).reshape(b, t, IDX_HEADS, IDX_DIM)
    ik = _layernorm(ik, ik_g, ik_b)
    iw = iw * (IDX_HEADS ** -0.5 * IDX_DIM ** -0.5)
    o_lat = _dsa_attention(q_lat, ckv, iq, ik, iw)
    o = jnp.einsum('bthc,hcd->bthd', o_lat, w_uv).reshape(b, t, DSA_WIDTH)
    return (o * jax.nn.silu(gate)) @ w_out

def first_inputs(seed: int = 0) -> dict:
    key = jax.random.key(seed)
    ks = jax.random.split(key, 24)
    f32 = jnp.float32
    out_mult = (2.0 * DEPTH) ** -0.5

    def w(k, shape, fan_in, mult=1.0):
        return jax.random.normal(k, shape, f32) * (mult * fan_in ** -0.5)

    def gain(k, shape):
        return 1.0 + 0.02 * jax.random.normal(k, shape, f32)

    def bias(k, shape):
        return 0.02 * jax.random.normal(k, shape, f32)

    return {
        'x': jax.random.normal(ks[0], (BATCH, SEQ, D_MODEL), f32),
        'even_norm': gain(ks[1], (N_EVEN, D_MODEL)),
        'even_w_in': w(ks[2], (N_EVEN, D_MODEL, EVEN_IN), D_MODEL),
        'even_b_glu': bias(ks[3], (N_EVEN, 2 * CONV_WIDTH)),
        'even_w_dw': w(ks[4], (N_EVEN, CONV_KERNEL, CONV_WIDTH), CONV_KERNEL),
        'even_b_dw': bias(ks[5], (N_EVEN, CONV_WIDTH)),
        'even_conv_ln_g': gain(ks[6], (N_EVEN, CONV_WIDTH)),
        'even_conv_ln_b': bias(ks[7], (N_EVEN, CONV_WIDTH)),
        'even_w_pw': w(ks[8], (N_EVEN, CONV_WIDTH, CONV_WIDTH), CONV_WIDTH),
        'even_b_pw': bias(ks[9], (N_EVEN, CONV_WIDTH)),
        'even_w_out': w(ks[10], (N_EVEN, MIX_WIDTH, D_MODEL), MIX_WIDTH, out_mult),
        'odd_norm': gain(ks[11], (N_ODD, D_MODEL)),
        'odd_w_in': w(ks[12], (N_ODD, D_MODEL, ODD_IN), D_MODEL),
        'odd_q_norm': gain(ks[13], (N_ODD, Q_LORA)),
        'odd_w_qb': w(ks[14], (N_ODD, Q_LORA, DSA_WIDTH), Q_LORA),
        'odd_kv_norm': gain(ks[15], (N_ODD, KV_LORA)),
        'odd_w_uk': w(ks[16], (N_ODD, DSA_HEADS, DSA_HEAD_DIM, KV_LORA), DSA_HEAD_DIM),
        'odd_w_uv': w(ks[17], (N_ODD, DSA_HEADS, KV_LORA, DSA_HEAD_DIM), KV_LORA),
        'odd_w_iq': w(ks[18], (N_ODD, Q_LORA, IDX_HEADS * IDX_DIM), Q_LORA),
        'odd_ik_ln_g': gain(ks[19], (N_ODD, IDX_DIM)),
        'odd_ik_ln_b': bias(ks[20], (N_ODD, IDX_DIM)),
        'odd_w_out': w(ks[21], (N_ODD, DSA_WIDTH, D_MODEL), DSA_WIDTH, out_mult),
        'final_norm': gain(ks[22], (D_MODEL,)),
    }

def first_block(x, even_norm, even_w_in, even_b_glu, even_w_dw, even_b_dw, even_conv_ln_g,
              even_conv_ln_b, even_w_pw, even_b_pw, even_w_out, odd_norm, odd_w_in, odd_q_norm,
              odd_w_qb, odd_kv_norm, odd_w_uk, odd_w_uv, odd_w_iq, odd_ik_ln_g, odd_ik_ln_b,
              odd_w_out, final_norm):
    for layer in range(DEPTH):
        i = layer // 2
        if layer % 2 == 0:
            x = x + _even_layer(x, even_norm[i], even_w_in[i], even_b_glu[i], even_w_dw[i],
                                even_b_dw[i], even_conv_ln_g[i], even_conv_ln_b[i],
                                even_w_pw[i], even_b_pw[i], even_w_out[i])
        else:
            x = x + _odd_layer(x, odd_norm[i], odd_w_in[i], odd_q_norm[i], odd_w_qb[i],
                               odd_kv_norm[i], odd_w_uk[i], odd_w_uv[i], odd_w_iq[i],
                               odd_ik_ln_g[i], odd_ik_ln_b[i], odd_w_out[i])
    return _rmsnorm(x, final_norm)


DEPTH_2 = 1

N_DN_HEADS = 8
DN_HEAD_DIM = 128
DN_WIDTH = N_DN_HEADS * DN_HEAD_DIM
N_FOURIER_GROUPS = 8
FOURIER_GROUP_DIM = 128
FOURIER_WIDTH = N_FOURIER_GROUPS * FOURIER_GROUP_DIM
CONV_WIDTH_2 = 5
CHUNK = 64
D_FF = 4 * D_MODEL
N_BRANCHES = 2

SPLIT_SIZES = (DN_WIDTH, DN_WIDTH, DN_WIDTH, DN_WIDTH, FOURIER_WIDTH, 4 * N_DN_HEADS, N_BRANCHES * D_MODEL)
IN_WIDTH = int(sum(SPLIT_SIZES))
SPLIT_POINTS = tuple(int(s) for s in np.cumsum(SPLIT_SIZES)[:-1])


def rms_norm(x, g):
    xf = x.astype(jnp.float32)
    y = xf * lax.rsqrt(jnp.mean(xf * xf, axis=-1, keepdims=True) + EPS)
    return (y * g.astype(jnp.float32)).astype(x.dtype)

def l2_norm(x):
    return x * lax.rsqrt(jnp.sum(x * x, axis=-1, keepdims=True) + EPS)

def centred_short_conv(u, w):
    c = u.shape[-1]
    pad = (CONV_WIDTH_2 - 1) // 2
    return lax.conv_general_dilated(u, w[:, None, :].astype(u.dtype), window_strides=(1,),
                                    padding=[(pad, pad)], dimension_numbers=("NWC", "WIO", "NWC"),
                                    feature_group_count=c)

def gated_delta_rule_chunked(q, k, v, g, beta):
    b, h, t, dk = q.shape
    dv = v.shape[-1]
    n = t // CHUNK
    q = q.reshape(b, h, n, CHUNK, dk)
    k = k.reshape(b, h, n, CHUNK, dk)
    v = v.reshape(b, h, n, CHUNK, dv)
    gc = jnp.cumsum(g.reshape(b, h, n, CHUNK), axis=-1)
    beta = beta.reshape(b, h, n, CHUNK, 1)
    idx = jnp.arange(CHUNK)
    incl = idx[:, None] >= idx[None, :]
    strict = idx[:, None] > idx[None, :]
    diff = gc[..., :, None] - gc[..., None, :]
    decay = jnp.where(incl, jnp.exp(jnp.where(incl, diff, 0.0)), 0.0)
    kb = k * beta
    m = jnp.where(strict, jnp.einsum("bhnid,bhnjd->bhnij", kb, k) * decay, 0.0)
    a_mat = m + jnp.eye(CHUNK, dtype=m.dtype)
    rhs = jnp.concatenate([v * beta, kb * jnp.exp(gc)[..., None]], axis=-1)
    sol = lax.linalg.triangular_solve(a_mat, rhs, left_side=True, lower=True, unit_diagonal=True)
    u, w = sol[..., :dv], sol[..., dv:]
    qk = jnp.where(incl, jnp.einsum("bhnid,bhnjd->bhnij", q, k) * decay, 0.0)
    q_dec = q * jnp.exp(gc)[..., None]
    k_dec = k * jnp.exp(gc[..., -1:] - gc)[..., None]
    g_last = jnp.exp(gc[..., -1])
    xs = tuple(jnp.moveaxis(a, 2, 0) for a in (q_dec, k_dec, u, w, qk, g_last))

    def step(s, inp):
        qd, kd, uc, wc, qkc, gl = inp
        v_new = uc - jnp.einsum("bhck,bhkv->bhcv", wc, s)
        o = jnp.einsum("bhck,bhkv->bhcv", qd, s) + jnp.einsum("bhij,bhjv->bhiv", qkc, v_new)
        s = s * gl[..., None, None] + jnp.einsum("bhck,bhcv->bhkv", kd, v_new)
        return s, o

    s0 = jnp.zeros((b, h, dk, dv), jnp.float32)
    _, o = lax.scan(step, s0, xs)
    return jnp.moveaxis(o, 0, 2).reshape(b, h, t, dv)

def gated_deltanet_branch(q, k, v, z, scal, conv_w, a_log_f, a_log_b, dt_b_f, dt_b_b, g_head, w_up):
    b, t, _ = q.shape
    dtype = q.dtype
    qkv = jax.nn.silu(centred_short_conv(jnp.concatenate([q, k, v], axis=-1), conv_w)).astype(jnp.float32)
    q, k, v = jnp.split(qkv, 3, axis=-1)
    heads = lambda a: a.reshape(b, t, N_DN_HEADS, DN_HEAD_DIM).transpose(0, 2, 1, 3)
    q = l2_norm(heads(q)) * (DN_HEAD_DIM ** -0.5)
    k = l2_norm(heads(k))
    v = heads(v)
    scal = scal.astype(jnp.float32).transpose(0, 2, 1)
    beta_f, beta_b, a_f, a_b = jnp.split(scal, 4, axis=1)
    beta_f, beta_b = jax.nn.sigmoid(beta_f), jax.nn.sigmoid(beta_b)
    g_f = -jnp.exp(a_log_f.astype(jnp.float32))[:, None] * jax.nn.softplus(a_f + dt_b_f.astype(jnp.float32)[:, None])
    g_b = -jnp.exp(a_log_b.astype(jnp.float32))[:, None] * jax.nn.softplus(a_b + dt_b_b.astype(jnp.float32)[:, None])
    o_f = gated_delta_rule_chunked(q, k, v, g_f, beta_f)
    flip = lambda a: jnp.flip(a, axis=2)
    o_b = flip(gated_delta_rule_chunked(flip(q), flip(k), flip(v), flip(g_b), flip(beta_b)))
    o = (o_f + o_b).transpose(0, 2, 1, 3)
    o = o * lax.rsqrt(jnp.mean(o * o, axis=-1, keepdims=True) + EPS) * g_head.astype(jnp.float32)
    o = o * jax.nn.silu(z.astype(jnp.float32).reshape(b, t, N_DN_HEADS, DN_HEAD_DIM))
    return o.reshape(b, t, DN_WIDTH).astype(dtype) @ w_up

def fourier_branch(f, w_lin):
    b, t, _ = f.shape
    fg = f.astype(jnp.float32).reshape(b, t, N_FOURIER_GROUPS, FOURIER_GROUP_DIM)
    fr = jnp.real(jnp.fft.fft2(fg, axes=(1, 3), norm="ortho"))
    return fr.reshape(b, t, FOURIER_WIDTH).astype(f.dtype) @ w_lin

def second_inputs(seed: int = 0) -> dict:
    key = jax.random.key(seed)
    ks = jax.random.split(key, 20)
    nrm = lambda k, shape, fan_in: jax.random.normal(k, shape, jnp.float32) * (fan_in ** -0.5)
    gain = lambda k, shape: 1.0 + 0.02 * jax.random.normal(k, shape, jnp.float32)
    a_log = lambda k: jnp.log(jax.random.uniform(k, (DEPTH_2, N_DN_HEADS), jnp.float32, 1.0, 16.0))

    def dt_bias(k):
        dt = jnp.exp(jax.random.uniform(k, (DEPTH_2, N_DN_HEADS), jnp.float32, np.log(1e-3), np.log(1e-1)))
        return dt + jnp.log(-jnp.expm1(-dt))

    return {
        "x": jax.random.normal(ks[0], (BATCH, SEQ, D_MODEL), jnp.float32),
        "g_mix": gain(ks[1], (DEPTH_2, D_MODEL)),
        "w_in": nrm(ks[2], (DEPTH_2, D_MODEL, IN_WIDTH), D_MODEL),
        "conv_w": nrm(ks[3], (DEPTH_2, CONV_WIDTH_2, 3 * DN_WIDTH), CONV_WIDTH_2),
        "a_log_fwd": a_log(ks[4]),
        "a_log_bwd": a_log(ks[5]),
        "dt_bias_fwd": dt_bias(ks[6]),
        "dt_bias_bwd": dt_bias(ks[7]),
        "g_dn_head": gain(ks[8], (DEPTH_2, DN_HEAD_DIM)),
        "w_dn_up": nrm(ks[9], (DEPTH_2, DN_WIDTH, D_MODEL), DN_WIDTH),
        "w_fourier": nrm(ks[10], (DEPTH_2, FOURIER_WIDTH, D_MODEL), FOURIER_WIDTH),
        "w_o": nrm(ks[11], (DEPTH_2, D_MODEL, D_MODEL), D_MODEL),
        "g_mlp": gain(ks[12], (DEPTH_2, D_MODEL)),
        "w_mlp_up": nrm(ks[13], (DEPTH_2, D_MODEL, D_FF), D_MODEL),
        "w_mlp_down": nrm(ks[14], (DEPTH_2, D_FF, D_MODEL), D_FF),
        "g_final": gain(ks[15], (D_MODEL,)),
    }

def second_block(x, g_mix, w_in, conv_w, a_log_fwd, a_log_bwd, dt_bias_fwd, dt_bias_bwd, g_dn_head,
              w_dn_up, w_fourier, w_o, g_mlp, w_mlp_up, w_mlp_down, g_final):
    for l in range(DEPTH_2):
        h = rms_norm(x, g_mix[l])
        proj = h @ w_in[l]
        q, k, v, z, f, scal, gates = jnp.split(proj, SPLIT_POINTS, axis=-1)
        y_a = gated_deltanet_branch(q, k, v, z, scal, conv_w[l], a_log_fwd[l], a_log_bwd[l],
                                    dt_bias_fwd[l], dt_bias_bwd[l], g_dn_head[l], w_dn_up[l])
        y_f = fourier_branch(f, w_fourier[l])
        gate_a, gate_f = jnp.split(jax.nn.sigmoid(gates), N_BRANCHES, axis=-1)
        x = x + (gate_a * y_a + gate_f * y_f) @ w_o[l]
        h = rms_norm(x, g_mlp[l])
        x = x + jnp.square(jax.nn.relu(h @ w_mlp_up[l])) @ w_mlp_down[l]
    return rms_norm(x, g_final)


def setup_inputs(seed=0):
    out = dict(first_inputs(seed))
    for name, value in second_inputs(seed + 1).items():
        if name != "x":
            out[name + "_2"] = value
    return out


def reference(
    x, even_norm, even_w_in, even_b_glu, even_w_dw, even_b_dw, even_conv_ln_g, even_conv_ln_b,
    even_w_pw, even_b_pw, even_w_out, odd_norm, odd_w_in, odd_q_norm, odd_w_qb, odd_kv_norm,
    odd_w_uk, odd_w_uv, odd_w_iq, odd_ik_ln_g, odd_ik_ln_b, odd_w_out, final_norm, g_mix_2,
    w_in_2, conv_w_2, a_log_fwd_2, a_log_bwd_2, dt_bias_fwd_2, dt_bias_bwd_2, g_dn_head_2,
    w_dn_up_2, w_fourier_2, w_o_2, g_mlp_2, w_mlp_up_2, w_mlp_down_2, g_final_2,
):
    x = first_block(
        x, even_norm, even_w_in, even_b_glu, even_w_dw, even_b_dw, even_conv_ln_g,
        even_conv_ln_b, even_w_pw, even_b_pw, even_w_out, odd_norm, odd_w_in, odd_q_norm,
        odd_w_qb, odd_kv_norm, odd_w_uk, odd_w_uv, odd_w_iq, odd_ik_ln_g, odd_ik_ln_b,
        odd_w_out, final_norm,
    )
    return second_block(
        x, g_mix_2, w_in_2, conv_w_2, a_log_fwd_2, a_log_bwd_2, dt_bias_fwd_2, dt_bias_bwd_2,
        g_dn_head_2, w_dn_up_2, w_fourier_2, w_o_2, g_mlp_2, w_mlp_up_2, w_mlp_down_2,
        g_final_2,
    )


_drawn_inputs = setup_inputs


def setup_inputs(seed=0):
    import zlib

    import numpy as np

    out = dict(_drawn_inputs(seed))
    spreads = {}
    factors = {'even_norm': 7.755,
     'even_b_glu': 8.0,
     'even_b_dw': 6.25,
     'even_conv_ln_g': 8.0,
     'even_conv_ln_b': 8.0,
     'even_b_pw': 7.255,
     'odd_norm': 4.294,
     'odd_q_norm': 5.846,
     'odd_kv_norm': 8.0,
     'odd_ik_ln_g': 5.805,
     'odd_ik_ln_b': 6.809,
     'g_mix_2': 4.341,
     'g_dn_head_2': 22.498,
     'g_mlp_2': 12.021,
     'g_final_2': 8.425}
    for name, (base, spread) in spreads.items():
        noise = np.random.default_rng([zlib.crc32(name.encode()), seed]).standard_normal(out[name].shape)
        drawn = base * np.exp(spread * noise) if base else spread * noise
        out[name] = jnp.asarray(drawn.astype(out[name].dtype))
    for name, factor in factors.items():
        out[name] = (out[name] * factor).astype(out[name].dtype)
    return out
```

```python
from contextlib import ExitStack

import numpy as np

import concourse.bass as bass
from concourse import mybir

F32 = mybir.dt.float32
F32R = mybir.dt.float32r
BF16 = mybir.dt.bfloat16
ALU = mybir.AluOpType
ACT = mybir.ActivationFunctionType
AX = mybir.AxisListType

P = 128
T = 256
TT = T // P
D = 2048
DC = D // P
EPS = 1e-6
CW = 1024
TAPS = 31
HE, DH = 8, 128
HO = 16
QL, KVL = 512, 256
IH, ID = 16, 64
TOPK = 64
HN = 8
NT = 5
FG = 8
DFF = 8192
LEVELS = 7

UK, UN = 4, 256
SLOTS = 4
GROUP = 2

ROWS = {}


def _rows():
    at = 0
    for name, n in (("even_norm", 16), ("odd_norm", 16), ("g_mix_2", 16), ("g_mlp_2", 16), ("g_final_2", 16),
                    ("even_b_glu", 16), ("even_b_dw", 8), ("even_conv_ln_g", 8), ("even_conv_ln_b", 8),
                    ("even_b_pw", 8), ("even_w_dw", 248), ("odd_q_norm", 4), ("odd_kv_norm", 2), ("g_dn_head_2", 1),
                    ("conv_w_2", 120), ("ik_g", 1), ("ik_b", 1), ("final_norm", 16)):
        ROWS[name] = at
        at += n
    return at


N_ROWS = _rows()
N_PACKS = -(-N_ROWS // P)

ZB = 56
Z_AVAL, Z_AGT, Z_AGATE, Z_Q, Z_K, Z_V, Z_BGATE = (8 * n for n in range(7))
Z_OGATE, Z_QLAT, Z_CQ, Z_CKV, Z_IQ = 0, 16, 48, 52, 16
Z_DQ, Z_DK, Z_DV, Z_DZ, Z_F, Z_DN, Z_DFT = 0, 8, 16, 24, 32, 40, 40

LINEARS = (("even_w_in", 112), ("even_w_pw", 8), ("even_w_out", 32), ("odd_w_in", 44), ("odd_w_iq", 4),
           ("odd_w_qb", 8), ("odd_w_uk", 4), ("odd_w_uv", 4), ("odd_w_out", 32), ("w_in_2", 80),
           ("gates", 64), ("mix", 32), ("w_o_2", 32), ("mlp", 256))
UNIT0 = {}
_at = 0
for _name, _n in LINEARS:
    UNIT0[_name] = _at
    _at += _n
UNITS = _at
GROUPS = (("even_w_in", 28), ("even_w_pw", 4), ("even_w_out", 8), ("odd_w_in", 11), ("odd_w_iq", 4),
          ("odd_w_qb", 8), ("odd_w_uk", 16), ("odd_w_uv", 8), ("odd_w_out", 8), ("w_in_2", 20),
          ("gates", 16), ("mix", 16), ("w_o_2", 8), ("mlp", 160))
GROUP0 = {}
_at = 0
for _name, _n in GROUPS:
    GROUP0[_name] = _at
    _at += _n


class Steps:

    def __init__(self, sem, names, first=0):
        self.sem = sem
        self.first = first
        self.names = list(names)
        self.n = len(self.names)
        self.index = {name: i for i, name in enumerate(self.names)}
        assert len(self.index) == self.n

    def at(self, name, r=0):
        return r * self.n + (self.index[name] + 1 + self.first)

    def done(self, r):
        return r * self.n + self.first


def four1(v):
    return v.rearrange("p (n i) -> p n i", n=4)


def flat(v):
    return v.rearrange("p d c h -> p (d c h)")


NORMS = ("even_norm", "odd_norm", "final_norm", "g_mix_2", "g_mlp_2", "g_final_2")
SPLIT_ROUND = (0, 1, None, 2, 3, 4)
XB = (0, 8, 16, 24, 32, 64)
KUS = {"even_w_in": 4, "even_w_pw": 2, "even_w_out": 4, "odd_w_in": 4, "odd_w_iq": 1, "odd_w_qb": 1,
       "odd_w_out": 4, "w_in_2": 4, "w_o_2": 4, "mlp": 4}
A_FREE = (0, UNIT0["even_w_out"], None, UNIT0["odd_w_out"], UNIT0["mlp"])


def build(nc, t, out):
    ctx = ExitStack()
    with ctx:
        def sb(name, shape, dt=F32):
            return ctx.enter_context(nc.sbuf_tensor(name, shape, dt))

        def sem(name):
            return ctx.enter_context(nc.semaphore(name))

        opened = []

        def steps(name, names):
            return Steps(sem(name), names)

        def rounds(name, names):
            opened.append(Steps(sem(name), names, first=1))
            return opened[-1]

        raw = sb("raw", [P, SLOTS, UK * UN])
        w_hi = sb("w_hi", [P, SLOTS, UK * UN], F32R)
        w_lo = sb("w_lo", [P, SLOTS, UK * UN], F32R)
        x = sb("x", [P, DC, T])
        a = sb("a", [P, DC, 2, T], F32R)
        b = sb("b", [P, DC, 2, T], F32R)
        z = sb("z", [P, ZB, T])
        scr = sb("scr", [P, 4, 512])
        rstd = sb("rstd", [P, T])
        vec = sb("vec", [P, N_PACKS * P])
        ident = sb("ident", [P, P])
        ones = sb("ones", [P, P])
        eps = sb("eps", [P, 1])
        one = sb("one", [P, 1])
        tri = sb("tri", [P, 4, P])
        causal = sb("causal", [P, TT, T], BF16)
        dmask = sb("dmask", [P, 4, P], BF16)
        stat = sb("stat", [P, 64])
        dsc = sb("dsc", [P, 8, 2, TT, HN])
        opening = sb("opening", [P, 16])
        iw = sb("iw", [P, TT, IH])
        own5 = sb("own5", [P, 5, T])
        ckvn, ckvt, ikt = own5[:, 0:2, :], own5[:, 2:4, :], own5[:, 4, :]

        lmask = own5[:, 0:4, :].rearrange("p a b -> p (a b)").bitcast(BF16)[:, 0:LEVELS * 2 * P].rearrange(
            "p (l d i) -> p l d i", l=LEVELS, d=2)
        scw = z[:, 50:52, :].rearrange("p a b -> p (a b)")

        lin_ps = ctx.enter_context(nc.psum_tensor("lin_ps", [P, 4, 512], F32))
        ps = ctx.enter_context(nc.psum_tensor("ps", [P, 4, 512], F32))

        raw_in = [sem(f"raw_in{s}") for s in range(SLOTS)]
        hi_done = sem("hi_done")
        lo_done = sem("lo_done")
        unit_used = sem("unit_used")
        part_done = sem("part_done")
        group_free = sem("group_free")
        x_done = sem("x_done")
        consts_in = sem("consts_in")
        x_in = sem("x_in")
        small_in = sem("small_in")
        table_in = sem("table_in")
        out_done = sem("out_done")

        ev = steps("ev", ["sum", "use"])
        bld = sem("bld")
        tp_pe = sem("tp_pe")
        tp_ev = sem("tp_ev")

        nr_act = steps("nr_act", [f"sq{s}" for s in range(8)] + ["root"])
        nr_pe = steps("nr_pe", [f"sum{s}" for s in range(8)])
        nr_rs = steps("nr_rs", ["rstd"])
        nr_n = steps("nr_n", [f"{s}" for s in range(8)])
        nr_hi = steps("nr_hi", [f"{s}" for s in range(8)])
        nr_lo = steps("nr_lo", [f"{s}" for s in range(8)])

        even_act = steps("even_act", ["qs", "vs", "p0", "p1"])
        cv_act = steps("cv_act", ["sig"])
        cv_dve = steps("cv_dve", ["glu"] + [f"tap{k}" for k in range(TAPS)])
        ln_act = steps("ln_act", [f"sq{s}" for s in range(4)] + ["root"] + [y for s in range(4) for y in (f"silu{s}a", f"silu{s}b")]
                       + [f"hi{s}" for s in range(4)] + ["agate", "bgate"])
        ln_pe = steps("ln_pe", ["mean"] + [f"var{s}" for s in range(4)])
        ln_dve = steps("ln_dve", [f"c{s}" for s in range(4)] + ["rstd"] + [f"n{s}" for s in range(4)] + [f"lo{s}" for s in range(4)])
        at_pe = steps("at_pe", ["vt", "s", "pt", "o"])
        at_dve = rounds("at_dve", ["vtok", "mask", "max", "neg", "rsum", "n0", "n1", "ptc", "o", "hi", "lo"])
        at_act = even_act
        pw_dve = steps("pw_dve", ["g0", "g1", "hi", "lo"])

        od_pe = steps("od_pe", ["ik", "cqs", "kvs", "kvt", "ikt"])
        od_act = steps("od_act", ["cqsq", "cqroot", "kvsq", "kvroot", "cqhi", "ogate", "ikroot"])
        od_dve = steps("od_dve", ["cqr", "cq0", "cq1", "cq2", "cq3", "cqlo", "kvr", "kv0", "kv1", "kvt",
                                  "bn0", "bn1", "ag0", "ag1", "ikr", "ikn0", "ikn1", "ikn2", "ikn3", "ikt", "iw", "zero"])
        ix_act = rounds("ix_act", ["stage", "relu"])
        ix_pe = rounds("ix_pe", ["idx"])
        ix_dve = rounds("ix_dve", ["s0", "s1", "s2", "s3"])
        tk_dve = steps("tk_dve", ["fill"] + [f"{y}{r}{q}" for r in range(8) for y in ("max", "rep") for q in range(2)] + ["sel", "am"])
        qb_dve = steps("qb_dve", ["hi", "lo"])
        da_act = steps("da_act", ["stage", "p0", "p1", "ohi"])
        da_pe = rounds("da_pe", ["s", "pt", "o"])
        da_dve = rounds("da_dve", ["mask", "max", "neg", "rsum", "n0", "n1", "ptc", "olo"])
        uv_dve = steps("uv_dve", ["gate", "hi", "lo"])

        sc_pe = steps("sc_pe", ["scal", "cum"])
        sc_act = steps("sc_act", ["b0", "b1", "e", "ln", "ea", "eg", "er"])
        sc_dve = steps("sc_dve", ["a0", "a1", "neg", "abs", "pos", "sp", "nea", "g0", "g1", "gc", "rem", "ne"])
        fo_act = steps("fo_act", ["stage", "ab", "hi"])
        fo_pe = rounds("fo_pe", ["ab", "o"])
        fo_dve = rounds("fo_dve", ["lo"])
        dn_dve = [rounds(f"dn_dve{w}", [f"cv{y}{k}" for k in range(NT) for y in range(3)]
                         + ["rn", "qn", "kn", "gb", "dsub", "dmin", "mt1", "mt2", "qk", "t0", "u0", "mm0"]
                         + [y for l in range(LEVELS - 1) for y in (f"mm{l + 1}", f"t{l + 1}", f"u{l + 1}")]
                         + [f"u{LEVELS}", "vn1a", "vn1b", "vka", "vkb", "r2a", "r2b", "vn2a", "vn2b", "o", "orn",
                            "on0", "on1", "ot", "hi", "lo"]) for w in range(2)]
        dn_act = [rounds(f"dn_act{w}", ["sl0", "sl1", "sl2", "sq", "root", "tok", "dexp"] + [f"x{l}" for l in range(LEVELS)]
                         + ["s", "qs0", "qs1", "os0", "os1", "oroot", "sz"]) for w in range(2)]
        dn_pe = [steps(f"dn_pe{w}", ["l2", "tok", "gc", "gram"] + [y for l in range(LEVELS) for y in (f"x{l}", f"tu{l}")]
                       + ["y1", "s", "ks", "qs", "y2", "o", "ot"]) for w in range(2)]
        mx_act = steps("mx_act", ["siga", "sigb", "sigc", "sigd"])
        mx_dve = steps("mx_dve", ["dng", "frg", "sum", "hi", "lo"])
        ml_dve = rounds("ml_dve", ["sq", "hi", "lo"])
        gate_half = sem("gate_half")
        sw_in = sem("sw_in")
        fin_pe = sem("fin_pe")
        fin_dve = sem("fin_dve")

        e_q, e_v, e_vt = z[:, 0, :], z[:, 1, :], z[:, 2, :]
        e_s, e_p, e_pt = (z[:, n:n + 2, :] for n in (3, 5, 16))
        o_q = scr[:, 0, :]
        o_s, o_p, o_pt = (z[:, n:n + 2, :] for n in (48, 50, 54))
        score = z[:, 24:26, :]
        work = z[:, 26:28, :]
        relu = z[:, 28:32, :]
        iq_st = z[:, 32, :]
        small = z[:, 36:41, :]
        small_w = small.rearrange("p a b -> p (a b)")
        addm = dmask[:].rearrange("p a b -> p (a b)").rearrange("p (q k) -> p q k", q=TT)
        ikn = z[:, 33, :]
        def four(v):
            return v.rearrange("p a (c i) -> p (a c) i", c=2)

        class Way:

            def __init__(self, w, two):
                self.w = w
                self.x_ps, self.y_ps = ps[:, 2 * w, :], ps[:, 2 * w + 1, :]
                self.qk_feat = two[0]
                self.tok = four(two[1])
                self.m = self.v_new = four(two[2])
                self.qk = four(two[3])
                self.t = self.gate = self.v_dec = four(two[4])
                self.u = four(two[5])
                self.x = self.decay = four(two[6])
                self.sq = self.root = two[6]
                self.mm = self.r = four(two[7])
                self.v_feat = two[7][:, 0, :]
                self.norm = stat[:, 32 + 8 * w:40 + 8 * w]

        ways = [Way(0, [z[:, 40 + 2 * n:42 + 2 * n, :] for n in range(8)]),
                Way(1, [z[:, 32 + 2 * n:34 + 2 * n, :] for n in range(4)]
                    + [scr[:, n, :].rearrange("p (a b) -> p a b", a=2) for n in range(4)])]
        BETA, GG, GC, EG, REM, ER, NEG, AA = range(8)
        dtb = sb("dtb", [P, 2, 16])

        pk = z[:, 32:35, :].rearrange("p a b -> p (a b)")
        consts = [(ident[:], t["c_ident"]), (tri[:], t["c_tri"]), (causal[:], t["c_causal"].bitcast(BF16))]

        def pack(name, src, c0=0, w=P):
            r, done, rows = ROWS[name], 0, src.shape[0]
            while done < rows:
                k, at = divmod(r + done, P)
                n = min(rows - done, P - at)
                consts.append((pk[at:at + n, k * P + c0:k * P + c0 + w], src[done:done + n, :]))
                done += n

        for name in ("even_norm", "odd_norm", "final_norm", "g_mix_2", "g_mlp_2", "g_final_2", "even_b_glu", "even_b_dw",
                     "even_conv_ln_g", "even_conv_ln_b", "even_b_pw", "even_w_dw", "odd_q_norm", "odd_kv_norm",
                     "g_dn_head_2", "conv_w_2"):
            v = t[name]
            pack(name, v.rearrange("(c p) -> c p", p=P) if len(v.shape) == 1 else v.rearrange("k (c p) -> (k c) p", p=P))
        for name, src in (("ik_g", "odd_ik_ln_g"), ("ik_b", "odd_ik_ln_b")):
            for c0 in (0, ID):
                pack(name, t[src].rearrange("(a p) -> a p", a=1), c0, ID)
        N_CONST = len(consts)

        block = ctx.enter_context(nc.Block())

        def units(v3):
            return v3.rearrange("p (k n) -> p k n", k=UK)

        @block.sync
        def _(sp):
            def load(u, slot, src):
                if not (isinstance(u, int) and u < SLOTS):
                    sp.wait_ge(lo_done, u - SLOTS + 1)
                sp.dma_start(units(raw[:, slot]), src).then_inc(raw_in[slot], 16)

            def stream(name, u0, groups, kus, col0=0, row0=0, per=2):
                v = t[name].rearrange("(k p) n -> p k n", p=P)

                def turn(g0, base):
                    col = g0 * UN if isinstance(g0, int) else sp.snap(g0 * UN)
                    for g in range(per):
                        for q in range(kus):
                            j = g * kus + q
                            k0 = row0 + q * UK
                            load(base + j, (u0 + j) % SLOTS,
                                 v[:, k0:k0 + UK, bass.ds(col + (col0 + g * UN), UN)])

                turn(0, u0)
                if groups > per:
                    with sp.Fori(1, groups // per) as i:
                        turn(i * per, i * (per * kus) + u0)

            stream("even_w_in", UNIT0["even_w_in"], 28, 4)
            COL = t["odd_w_in"].rearrange("(k p) n -> p k n", p=P)[:, :, QL + KVL:QL + KVL + ID + IH]
            stream("even_w_pw", UNIT0["even_w_pw"], 4, 2, per=4)
            stream("even_w_out", UNIT0["even_w_out"], 8, 4)
            sp.wait_ge(at_dve.sem, at_dve.at("lo", HE - 1))
            sp.dma_start(small_w.rearrange("p (k n) -> p k n", k=DC), COL).then_inc(sw_in, 16)
            stream("odd_w_in", UNIT0["odd_w_in"], 3, 4, per=3)
            stream("odd_w_in", UNIT0["odd_w_in"] + 12, 8, 4, col0=QL + KVL + ID + IH)
            stream("odd_w_iq", UNIT0["odd_w_iq"], 4, 1, per=4)
            stream("odd_w_qb", UNIT0["odd_w_qb"], 8, 1, per=4)
            uk = t["odd_w_uk"].rearrange("h d c -> d h c")
            uv = t["odd_w_uv"].rearrange("h (k c) d -> c (h k) d", c=P)
            for n in range(4):
                load(UNIT0["odd_w_uk"] + n, n, uk[:, 4 * n:4 * n + 4, :])
            for n in range(4):
                u = UNIT0["odd_w_uv"] + n
                sp.wait_ge(lo_done, u - SLOTS + 1)
                sp.dma_start(raw[:, n].rearrange("p (h d) -> p h d", h=8), uv[:, 8 * n:8 * n + 8, :]).then_inc(raw_in[n], 16)
            stream("odd_w_out", UNIT0["odd_w_out"], 8, 4)
            sp.wait_ge(da_dve.sem, da_dve.at("olo", HO - 1))
            sp.dma_start(lmask, t["c_lmask"].bitcast(BF16)).then_inc(table_in, 16)
            sp.dma_start(dmask[:], t["c_dmask"].bitcast(BF16)).then_inc(table_in, 16)
            sp.dma_start(z[:, Z_DFT:Z_DFT + 5, :], t["c_dft"]).then_inc(table_in, 16)
            sp.dma_start(scw.rearrange("p (k n) -> p k n", k=DC),
                         t["w_in_2"].rearrange("(k p) n -> p k n", p=P)[:, :, 5120:5152]).then_inc(table_in, 16)
            stream("w_in_2", UNIT0["w_in_2"], 20, 4)
            u0 = UNIT0["gates"]
            gates = t["w_in_2"].rearrange("(k p) n -> p k n", p=P)
            with sp.Fori(0, 4) as i:
                col = sp.snap(i * (2 * UN))
                for n, col0 in enumerate((0, D, UN, D + UN)):
                    for q in range(4):
                        load(i * 16 + (u0 + 4 * n + q), q, gates[:, q * UK:(q + 1) * UK, bass.ds(col + (5152 + col0), UN)])
            u0 = UNIT0["mix"]
            dn_up = t["w_dn_up_2"].rearrange("(k p) n -> p k n", p=P)
            four_up = t["w_fourier_2"].rearrange("(k p) n -> p k n", p=P)
            with sp.Fori(1, 9) as g:
                for n, (v, q) in enumerate(((dn_up, 0), (dn_up, 1), (four_up, 0), (four_up, 1))):
                    load(g * 4 + (u0 - 4 + n), n, v[:, q * UK:(q + 1) * UK, bass.ds(g * UN - UN, UN)])
            stream("w_o_2", UNIT0["w_o_2"], 8, 4)
            for ph in range(4):
                stream("w_mlp_up_2", UNIT0["mlp"] + 64 * ph, 8, 4, col0=ph * D)
                stream("w_mlp_down_2", UNIT0["mlp"] + 64 * ph + 32, 8, 4, row0=ph * DC)
            ov = out.rearrange("(q p) (s n) -> p s q n", p=P, n=T)
            for s in range(8):
                sp.wait_ge(fin_dve, s + 1)
                sp.dma_start(ov[:, s], z[:, 16 + 2 * s:18 + 2 * s, :]).then_inc(out_done, 16)
            sp.wait_ge(out_done, 16 * 8)

        @block.gpsimd
        def _(pool):
            def lo(u, slot, first=False):
                pool.wait_ge(hi_done, u + 1)
                if not first:
                    pool.wait_ge(unit_used, u - SLOTS + 1)
                nc.gpsimd.tensor_tensor(w_lo[:, slot], raw[:, slot], w_hi[:, slot].bitcast(F32),
                                        ALU.subtract).then_inc(lo_done, 1)

            for n, steps_ in enumerate(opened):
                nc.gpsimd.memset(opening[:, n:n + 1], 0.0).then_inc(steps_.sem, 1)
            n_units = UNITS
            for u in range(SLOTS):
                lo(u, u, first=True)
            with pool.Fori(1, n_units // SLOTS) as i:
                for s in range(SLOTS):
                    lo(i * SLOTS + s, s)

        @block.scalar
        def _(act):
            for dst, src in consts:
                act.dma_start(dst, src).then_inc(consts_in, 16)
            for k, names in enumerate((("dt_bias_fwd_2", "dt_bias_bwd_2"), ("a_log_fwd_2", "a_log_bwd_2"))):
                for d, name in enumerate(names):
                    act.dma_start(dtb[:, k, d * HN:(d + 1) * HN],
                                  t[name].rearrange("(a n) -> a n", a=1).broadcast_to([P, HN])).then_inc(small_in, 16)
            for tt in range(TT):
                act.dma_start(z[:, 8 * tt:8 * tt + 8, :].rearrange("p a b -> p (a b)"),
                              t["x"][tt * P:(tt + 1) * P, :]).then_inc(x_in, 16)

            def hi(u, slot, first=False):
                act.wait_ge(raw_in[slot], 16 * (u // SLOTS + 1))
                if not first:
                    act.wait_ge(unit_used, u - SLOTS + 1)
                nc.scalar.activation(w_hi[:, slot], raw[:, slot], ACT.Copy).then_inc(hi_done, 1)

            def his(u0, n):
                s0 = u0 % SLOTS
                assert n % SLOTS == 0
                with act.Fori(0, n // SLOTS) as i:
                    for s in range(SLOTS):
                        slot = (s0 + s) % SLOTS
                        act.wait_ge(raw_in[slot], i * 16 + 16 * ((u0 + s) // SLOTS + 1))
                        act.wait_ge(unit_used, i * SLOTS + (u0 + s - SLOTS + 1))
                        nc.scalar.activation(w_hi[:, slot], raw[:, slot], ACT.Copy).then_inc(hi_done, 1)

            def ahead(u0):
                for s in range(SLOTS):
                    hi(u0 + s, (u0 + s) % SLOTS, first=u0 == 0)

            def norm_squares(r):
                for s in range(8):
                    act.wait_ge(x_done, XB[r] + s + 1)
                    if s >= 2:
                        act.wait_ge(nr_pe.sem, nr_pe.at(f"sum{s - 2}", r))
                    nc.scalar.activation(scr[:, s % 2].rearrange("p (k n) -> p k n", k=2), x[:, 2 * s:2 * s + 2, :],
                                         ACT.Square).then_inc(nr_act.sem, 1)
                act.wait_ge(nr_pe.sem, nr_pe.at("sum7", r))
                act.wait_ge(bld, 3)
                nc.scalar.activation(scr[:, 0, 0:T], ps[:, 0, 0:T], ACT.Sqrt, bias=eps[:, 0:1],
                                     scale=1.0 / D).then_inc(nr_act.sem, 1)

            def norm_hi(r):
                for s in range(8):
                    act.wait_ge(nr_n.sem, nr_n.at(f"{s}", SPLIT_ROUND[r]))
                    if s == 0 and r:
                        act.wait_ge(unit_used, A_FREE[r])
                    nc.scalar.activation(a[:, 2 * s:2 * s + 2, 0, :],
                                         scr[:, 2 + s % 2].rearrange("p (k n) -> p k n", k=2),
                                         ACT.Copy).then_inc(nr_hi.sem, 1)

            ahead(0)
            norm_squares(0)
            norm_hi(0)
            his(4, 112 - 4)
            ahead_n = UNIT0["even_w_pw"]
            with act.Fori(0, 8) as c:
                act.wait_ge(group_free, 28)
                nc.scalar.activation(z[:, bass.ds(c + Z_AGT, 1), :], z[:, bass.ds(c + Z_AGT, 1), :], ACT.Sigmoid,
                                     bias=vec[:, bass.ds(c + ROWS["even_b_glu"] + 8, 1)]).then_inc(cv_act.sem, 1)
            for s in range(4):
                act.wait_ge(ln_dve.sem, ln_dve.at(f"c{s}"))
                if s >= 2:
                    act.wait_ge(ln_pe.sem, ln_pe.at(f"var{s - 2}"))
                nc.scalar.activation(scr[:, s % 2].rearrange("p (k n) -> p k n", k=2),
                                     z[:, Z_AGT + 2 * s:Z_AGT + 2 * s + 2, :], ACT.Square).then_inc(ln_act.sem, 1)
            act.wait_ge(ln_pe.sem, ln_pe.at("var3"))
            nc.scalar.activation(scr[:, 2, 0:T], ps[:, 1, 0:T], ACT.Sqrt, bias=eps[:, 0:1],
                                 scale=1.0 / CW).then_inc(ln_act.sem, 1)
            for s in range(4):
                act.wait_ge(ln_dve.sem, ln_dve.at(f"n{s}"))
                for k in range(2):
                    c = 2 * s + k
                    nc.scalar.activation(z[:, Z_AGT + c, :], z[:, Z_AGT + c, :], ACT.Silu,
                                         bias=vec[:, ROWS["even_conv_ln_b"] + c:ROWS["even_conv_ln_b"] + c + 1],
                                         scale=vec[:, ROWS["even_conv_ln_g"] + c:ROWS["even_conv_ln_g"] + c + 1]
                                         ).then_inc(ln_act.sem, 1)
            for s in range(4):
                act.wait_ge(ln_act.sem, ln_act.at(f"silu{s}b"))
                nc.scalar.activation(a[:, 2 * s:2 * s + 2, 0, :], z[:, Z_AGT + 2 * s:Z_AGT + 2 * s + 2, :],
                                     ACT.Copy).then_inc(ln_act.sem, 1)
            nc.scalar.activation(z[:, Z_AGATE:Z_AGATE + 8, :], z[:, Z_AGATE:Z_AGATE + 8, :],
                                 ACT.Silu).then_inc(ln_act.sem, 1)
            nc.scalar.activation(z[:, Z_BGATE:Z_BGATE + 8, :], z[:, Z_BGATE:Z_BGATE + 8, :],
                                 ACT.Silu).then_inc(ln_act.sem, 1)
            his(UNIT0["even_w_pw"], 8)
            ahead(UNIT0["even_w_out"])
            with act.Fori(0, HE) as h:
                act.wait_ge(at_dve.sem, at_dve.done(h))
                nc.scalar.mul(e_q, z[:, bass.ds(h + Z_Q, 1), :].rearrange("p a n -> p (a n)"), DH ** -0.5).then_inc(at_act.sem, 1)
                nc.scalar.copy(e_v, z[:, bass.ds(h + Z_V, 1), :].rearrange("p a n -> p (a n)")).then_inc(at_act.sem, 1)
                act.wait_ge(at_dve.sem, at_dve.at("neg", h))
                for q in range(TT):
                    nc.scalar.activation(e_p[:, q, :], e_s[:, q, :], ACT.Exp, bias=stat[:, 2 + q:3 + q],
                                         accum_out=stat[:, 4 + q:5 + q]).then_inc(at_act.sem, 1)
            his(UNIT0["even_w_out"] + 4, 28)
            norm_squares(1)
            norm_hi(1)
            his(UNIT0["odd_w_in"], 44)
            ahead(UNIT0["odd_w_iq"])
            act.wait_ge(group_free, GROUP0["odd_w_in"] + 11)
            nc.scalar.activation(scr[:, 0:2, :].rearrange("p a (k n) -> p (a k) n", k=2), z[:, Z_CQ:Z_CQ + 4, :],
                                 ACT.Square).then_inc(od_act.sem, 1)
            act.wait_ge(od_pe.sem, od_pe.at("cqs"))
            nc.scalar.activation(scr[:, 2, 0:T], ps[:, 0, 0:T], ACT.Sqrt, bias=eps[:, 0:1],
                                 scale=1.0 / QL).then_inc(od_act.sem, 1)
            nc.scalar.activation(scr[:, 0, :].rearrange("p (k n) -> p k n", k=2), z[:, Z_CKV:Z_CKV + 2, :],
                                 ACT.Square).then_inc(od_act.sem, 1)
            act.wait_ge(od_pe.sem, od_pe.at("kvs"))
            nc.scalar.activation(scr[:, 3, 0:T], ps[:, 1, 0:T], ACT.Sqrt, bias=eps[:, 0:1],
                                 scale=1.0 / KVL).then_inc(od_act.sem, 1)
            act.wait_ge(od_dve.sem, od_dve.at("cq3"))
            nc.scalar.activation(b[:, 0:4, 0, :], z[:, Z_CQ:Z_CQ + 4, :], ACT.Copy).then_inc(od_act.sem, 1)
            nc.scalar.activation(z[:, Z_OGATE:Z_OGATE + 16, :], z[:, Z_OGATE:Z_OGATE + 16, :],
                                 ACT.Silu).then_inc(od_act.sem, 1)
            act.wait_ge(od_dve.sem, od_dve.at("ag1"))
            nc.scalar.activation(stat[:, 20:22], stat[:, 16:20].rearrange("p (q s) -> p s q", s=2)[:, 1, :], ACT.Sqrt,
                                 bias=eps[:, 0:1]).then_inc(od_act.sem, 1)
            with act.Fori(0, 8) as c:
                act.wait_ge(group_free, GROUP0["odd_w_iq"] + 4)
                act.wait_ge(ix_pe.sem, ix_pe.done(c))
                nc.scalar.copy(iq_st, z[:, bass.ds(c + Z_IQ, 1), :].rearrange("p a n -> p (a n)")).then_inc(ix_act.sem, 1)
                act.wait_ge(ix_pe.sem, ix_pe.at("idx", c))
                act.wait_ge(ix_dve.sem, ix_dve.done(c))
                nc.scalar.activation(relu.rearrange("p a n -> p (a n)"), ps[:, 0:2, :].rearrange("p a n -> p (a n)"),
                                     ACT.Relu).then_inc(ix_act.sem, 1)
            his(UNIT0["odd_w_qb"], 8)
            his(UNIT0["odd_w_uk"], 4)
            ahead(UNIT0["odd_w_uv"])
            for half in range(2):
                with act.Fori(0, 8) as h8:
                    h = h8 + 8 * half
                    if half == 0:
                        act.wait_ge(group_free, GROUP0["odd_w_uk"] + 16)
                    act.wait_ge(da_pe.sem, da_pe.done(h))
                    nc.scalar.mul(o_q.rearrange("p (k n) -> p k n", k=2), z[:, bass.ds(h * 2 + Z_QLAT, 2), :],
                                  DH ** -0.5).then_inc(da_act.sem, 1)
                    act.wait_ge(da_dve.sem, da_dve.at("neg", h))
                    for q in range(TT):
                        nc.scalar.activation(o_p[:, q, :], o_s[:, q, :], ACT.Exp, bias=stat[:, 2 + q:3 + q],
                                             accum_out=stat[:, 4 + q:5 + q]).then_inc(da_act.sem, 1)
                    act.wait_ge(da_pe.sem, da_pe.at("o", h))
                    if half == 1:
                        act.wait_ge(unit_used, UNIT0["odd_w_uv"] + 2)
                    else:
                        act.wait_ge(unit_used, UNIT0["odd_w_uk"] + 4)
                    nc.scalar.activation(a[:, bass.ds(h8 * 2, 2), 0, :], ps[:, 2, :].rearrange("p (k n) -> p k n", k=2),
                                         ACT.Copy).then_inc(da_act.sem, 1)
            his(UNIT0["odd_w_out"], 32)
            norm_squares(2)
            norm_squares(3)
            norm_hi(3)
            his(UNIT0["w_in_2"], 80)
            act.wait_ge(sc_pe.sem, sc_pe.at("scal"))
            act.wait_ge(sc_dve.sem, sc_dve.at("a1"))
            for c in range(TT):
                nc.scalar.activation(dsc[:, BETA, :, c, :],
                                     ps[:, 0, c * 32:c * 32 + 16].rearrange("p (d h) -> p d h", d=2),
                                     ACT.Sigmoid).then_inc(sc_act.sem, 1)
            act.wait_ge(sc_dve.sem, sc_dve.at("abs"))
            nc.scalar.activation(stat[:, 0:32], stat[:, 0:32], ACT.Exp, scale=-1.0).then_inc(sc_act.sem, 1)
            act.wait_ge(sc_act.sem, sc_act.at("e"))
            nc.scalar.activation(stat[:, 0:32], stat[:, 0:32], ACT.Ln, bias=one[:, 0:1]).then_inc(sc_act.sem, 1)
            act.wait_ge(small_in, 16 * 4)
            nc.scalar.activation(dtb[:, 1, :], dtb[:, 1, :], ACT.Exp).then_inc(sc_act.sem, 1)
            act.wait_ge(sc_dve.sem, sc_dve.at("rem"))
            nc.scalar.activation(flat(dsc[:, EG]), flat(dsc[:, GC]), ACT.Exp).then_inc(sc_act.sem, 1)
            nc.scalar.activation(flat(dsc[:, ER]), flat(dsc[:, REM]), ACT.Exp).then_inc(sc_act.sem, 1)
            with act.Fori(0, FG) as g:
                act.wait_ge(group_free, GROUP0["w_in_2"] + 20)
                act.wait_ge(fo_pe.sem, fo_pe.done(g))
                nc.scalar.copy(z[:, 46, :], z[:, bass.ds(g + Z_F, 1), :].rearrange("p a n -> p (a n)")).then_inc(fo_act.sem, 1)
                act.wait_ge(fo_pe.sem, fo_pe.at("ab", g))
                nc.scalar.activation(z[:, 48:50, :], ps[:, 2, :].rearrange("p (a n) -> p a n", a=2), ACT.Copy).then_inc(fo_act.sem, 1)
                act.wait_ge(fo_pe.sem, fo_pe.at("o", g))
                nc.scalar.activation(b[:, bass.ds(g + 8, 1), 0, :].rearrange("p a n -> p (a n)"), ps[:, 3, 0:T],
                                     ACT.Copy).then_inc(fo_act.sem, 1)
            u0 = UNIT0["gates"]
            for n in range(2):
                hi(u0 + n, n)
            with act.Fori(0, HN // 2) as i:
                def fill(n):
                    u, slot = u0 + n + 2, (n + 2) % SLOTS
                    act.wait_ge(raw_in[slot], i * 64 + 16 * (u // SLOTS + 1))
                    act.wait_ge(unit_used, i * 16 + (u - SLOTS + 1))
                    nc.scalar.activation(w_hi[:, slot], raw[:, slot], ACT.Copy).then_inc(hi_done, 1)

                for w in ways:
                    own, dve_sem = dn_act[w.w], dn_dve[w.w]
                    for y, v in enumerate((w.qk_feat[:, 0, :], w.qk_feat[:, 1, :], w.v_feat)):
                        act.wait_ge(dve_sem.sem, dve_sem.at(f"cv{y}{NT - 1}", i))
                        nc.scalar.activation(v, v, ACT.Silu).then_inc(own.sem, 1)
                    act.wait_ge(own.sem, own.at("sl1", i))
                    nc.scalar.activation(w.sq, w.qk_feat, ACT.Square).then_inc(own.sem, 1)
                    fill(w.w)
                fill(2)
                for w in ways:
                    own, pe_sem = dn_act[w.w], dn_pe[w.w]
                    act.wait_ge(pe_sem.sem, pe_sem.at("l2", i))
                    nc.scalar.activation(w.root, w.x_ps.rearrange("p (a n) -> p a n", a=2), ACT.Sqrt,
                                         bias=eps[:, 0:1]).then_inc(own.sem, 1)
                fill(3)
                for w in ways:
                    own, pe_sem = dn_act[w.w], dn_pe[w.w]
                    act.wait_ge(pe_sem.sem, pe_sem.at("tok", i))
                    nc.scalar.activation(w.tok, four1(w.y_ps), ACT.Copy).then_inc(own.sem, 1)
                fill(4)
                for w in ways:
                    own, dve_sem = dn_act[w.w], dn_dve[w.w]
                    act.wait_ge(dve_sem.sem, dve_sem.at("dmin", i))
                    nc.scalar.activation(w.decay, w.decay, ACT.Exp).then_inc(own.sem, 1)
                fill(5)
                for l in range(LEVELS):
                    for w in ways:
                        own, pe_sem = dn_act[w.w], dn_pe[w.w]
                        act.wait_ge(pe_sem.sem, pe_sem.at(f"x{l}", i))
                        nc.scalar.activation(w.x, four1(w.x_ps), ACT.Copy).then_inc(own.sem, 1)
                    fill(6 + l)
                fill(13)
                for w in ways:
                    own, pe_sem = dn_act[w.w], dn_pe[w.w]
                    act.wait_ge(pe_sem.sem, pe_sem.at("s", i))
                    nc.scalar.activation(w.x[:, 0:2, :], four1(w.y_ps)[:, 0:2, :], ACT.Copy).then_inc(own.sem, 1)
                fill(14)
                for w in ways:
                    own, pe_sem = dn_act[w.w], dn_pe[w.w]
                    act.wait_ge(pe_sem.sem, pe_sem.at("qs", i))
                    for d in range(2):
                        nc.scalar.activation(w.x[:, 2 + 1 - d, :], four1(w.y_ps)[:, d, :], ACT.Copy,
                                             scale=dsc[:, EG, d, 1 - d, bass.ds(i * 2 + w.w, 1)]).then_inc(own.sem, 1)
                fill(15)
                for w in ways:
                    own, dve_sem = dn_act[w.w], dn_dve[w.w]
                    act.wait_ge(dve_sem.sem, dve_sem.at("o", i))
                    for c in range(TT):
                        nc.scalar.activation(w.v_dec[:, c, :], w.u[:, c, :], ACT.Square,
                                             accum_out=w.norm[:, c:c + 1]).then_inc(own.sem, 1)
                    act.wait_ge(own.sem, own.at("os1", i))
                    nc.scalar.activation(w.norm[:, 2:4], w.norm[:, 0:2], ACT.Sqrt, bias=eps[:, 0:1],
                                         scale=1.0 / P).then_inc(own.sem, 1)
                for w in ways:
                    nc.scalar.activation(w.x[:, 0:2, :].rearrange("p a n -> p (a n)"),
                                         z[:, bass.ds(i * 2 + (Z_DZ + w.w), 1), :].rearrange("p a n -> p (a n)"),
                                         ACT.Silu).then_inc(dn_act[w.w].sem, 1)
            act.wait_ge(group_free, GROUP0["gates"] + 16)
            for n in range(4):
                gate = z[:, 8 * n:8 * n + 8, :]
                nc.scalar.activation(gate, gate, ACT.Sigmoid).then_inc(mx_act.sem, 1)
            for n in (2, 3):
                hi(UNIT0["mix"] + n, n)
            his(UNIT0["mix"] + 4, 28)
            his(UNIT0["w_o_2"], 32)
            norm_squares(4)
            norm_hi(4)
            his(UNIT0["mlp"], 256)
            norm_squares(5)

        @block.vector
        def _(dve):
            nc.vector.memset(ones[:], 1.0).then_inc(bld, 1)
            nc.vector.memset(eps[:], EPS).then_inc(bld, 1)
            nc.vector.memset(one[:], 1.0).then_inc(bld, 1)
            dve.wait_ge(tp_pe, 1)
            nc.vector.tensor_copy(vec[:, 0:4 * P], ps[:, 0, :]).then_inc(tp_ev, 1)
            nc.vector.tensor_copy(vec[:, 4 * P:N_ROWS], lin_ps[:, 0, 0:N_ROWS - 4 * P]).then_inc(tp_ev, 1)
            for s in range(8):
                dve.wait_ge(tp_pe, 2 + s)
                nc.vector.tensor_copy(x[:, 2 * s:2 * s + 2, :],
                                      ps[:, 1 + s % 3, :].rearrange("p (k n) -> p k n", k=2)).then_inc(x_done, 1)

            def norm(r, last=False):
                g0 = ROWS[NORMS[r]]
                dve.wait_ge(nr_act.sem, nr_act.at("root", r))
                dve.wait_ge(x_done, XB[r] + 8)
                dve.wait_ge(tp_ev, 2)
                nc.vector.reciprocal(rstd[:], scr[:, 0, 0:T]).then_inc(nr_rs.sem, 1)
                dve.wait_ge(nr_rs.sem, nr_rs.at("rstd", r))
                R = SPLIT_ROUND[r]
                for s in range(8):
                    pair = x[:, 2 * s:2 * s + 2, :]
                    t2 = pair if R is None else scr[:, 2 + s % 2].rearrange("p (k n) -> p k n", k=2)
                    if R is not None and s >= 2:
                        dve.wait_ge(nr_lo.sem, nr_lo.at(f"{s - 2}", R))
                    for k in range(2):
                        c = 2 * s + k
                        m = nc.vector.scalar_tensor_tensor(out=t2[:, k, :], in0=x[:, c, :], scalar=vec[:, g0 + c:g0 + c + 1],
                                                           in1=rstd[:], op0=ALU.mult, op1=ALU.mult)
                    if R is None:
                        m.then_inc(x_done, 1)
                        continue
                    m.then_inc(nr_n.sem, 1)
                    if last:
                        dve.wait_ge(nr_n.sem, nr_n.at(f"{s}", R))
                        nc.vector.tensor_copy(z[:, 2 * s:2 * s + 2, :], t2).then_inc(nr_lo.sem, 1)
                    else:
                        dve.wait_ge(nr_hi.sem, nr_hi.at(f"{s}", R))
                        nc.vector.tensor_tensor(a[:, 2 * s:2 * s + 2, 1, :], t2, a[:, 2 * s:2 * s + 2, 0, :].bitcast(F32),
                                                ALU.subtract).then_inc(nr_lo.sem, 1)

            def halves(parity):
                return lin_ps[:, 2 * parity:2 * parity + 2, :].rearrange("p m (s n) -> p m n s", s=2)

            def to_z(name, n, z0, per=2, u=0, g=0):
                kus, u0, g0 = KUS[name], UNIT0[name] + u, GROUP0[name] + g

                def turn(used, zb):
                    for k in range(per):
                        dve.wait_ge(unit_used, used + (k + 1) * kus)
                        nc.vector.tensor_reduce(z[:, bass.ds(zb + 2 * k, 2), :], halves((g0 + k) % 2), AX.X,
                                                ALU.add).then_inc(group_free, 1)
                if n <= per:
                    turn(u0, z0)
                else:
                    with dve.Fori(0, n // per) as i:
                        turn(i * (per * kus) + u0, i * (2 * per) + z0)

            def to_x(name, u=0, g=0):
                u0, g0 = UNIT0[name] + u, GROUP0[name] + g
                with dve.Fori(0, 4) as i:
                    for k in range(2):
                        dve.wait_ge(unit_used, i * 8 + (u0 + 4 * (k + 1)))
                        tmp = scr[:, 2 + k].rearrange("p (m n) -> p m n", m=2)
                        nc.vector.tensor_reduce(tmp, halves((g0 + k) % 2), AX.X, ALU.add).then_inc(group_free, 1)
                        dve.wait_ge(group_free, i * 2 + (g0 + k + 1))
                        xs = x[:, bass.ds(i * 4 + 2 * k, 2), :]
                        nc.vector.tensor_tensor(xs, xs, tmp, ALU.add).then_inc(x_done, 1)

            norm(0)
            to_z("even_w_in", 28, 0)
            with dve.Fori(0, 8) as c:
                dve.wait_ge(cv_act.sem, cv_act.at("sig", c))
                dve.wait_ge(group_free, 28)
                u = z[:, bass.ds(c + Z_AVAL, 1), :]
                y = z[:, bass.ds(c + Z_AGT, 1), :]
                nc.vector.scalar_tensor_tensor(out=u, in0=u, scalar=vec[:, bass.ds(c + ROWS["even_b_glu"], 1)], in1=y,
                                               op0=ALU.add, op1=ALU.mult).then_inc(cv_dve.sem, 1)
                dve.wait_ge(cv_dve.sem, cv_dve.at("glu", c))
                w = ROWS["even_w_dw"]
                nc.vector.tensor_scalar(y, u, vec[:, bass.ds(c + (w + 8 * (TAPS - 1)), 1)],
                                        vec[:, bass.ds(c + ROWS["even_b_dw"], 1)], ALU.mult, ALU.add).then_inc(cv_dve.sem, 1)
                for k in range(1, TAPS):
                    dve.wait_ge(cv_dve.sem, cv_dve.at(f"tap{k - 1}", c))
                    nc.vector.scalar_tensor_tensor(out=y[:, :, k:T], in0=u[:, :, 0:T - k],
                                                   scalar=vec[:, bass.ds(c + (w + 8 * (TAPS - 1 - k)), 1)], in1=y[:, :, k:T],
                                                   op0=ALU.mult, op1=ALU.add).then_inc(cv_dve.sem, 1)
            mean = ps[:, 0, 0:T].unsqueeze(1).broadcast_to([P, 2, T])
            dve.wait_ge(ln_pe.sem, ln_pe.at("mean"))
            dve.wait_ge(cv_dve.sem, cv_dve.at(f"tap{TAPS - 1}", 7))
            for s in range(4):
                yy = z[:, Z_AGT + 2 * s:Z_AGT + 2 * s + 2, :]
                nc.vector.scalar_tensor_tensor(out=yy, in0=mean, scalar=-1.0 / CW, in1=yy,
                                               op0=ALU.mult, op1=ALU.add).then_inc(ln_dve.sem, 1)
            dve.wait_ge(ln_act.sem, ln_act.at("root"))
            nc.vector.reciprocal(scr[:, 3, 0:T], scr[:, 2, 0:T]).then_inc(ln_dve.sem, 1)
            dve.wait_ge(ln_dve.sem, ln_dve.at("rstd"))
            for s in range(4):
                yy = z[:, Z_AGT + 2 * s:Z_AGT + 2 * s + 2, :]
                nc.vector.tensor_tensor(yy, yy, scr[:, 3, 0:T].unsqueeze(1).broadcast_to([P, 2, T]),
                                        ALU.mult).then_inc(ln_dve.sem, 1)
            for s in range(4):
                dve.wait_ge(ln_act.sem, ln_act.at(f"hi{s}"))
                nc.vector.tensor_tensor(a[:, 2 * s:2 * s + 2, 1, :], z[:, Z_AGT + 2 * s:Z_AGT + 2 * s + 2, :],
                                        a[:, 2 * s:2 * s + 2, 0, :].bitcast(F32), ALU.subtract).then_inc(ln_dve.sem, 1)
            for g in range(4):
                G = GROUP0["even_w_pw"] + g
                dve.wait_ge(unit_used, UNIT0["even_w_pw"] + 2 * g + 2)
                dve.wait_ge(ln_act.sem, ln_act.at("agate"))
                if g >= 1:
                    dve.wait_ge(pw_dve.sem, pw_dve.at("lo", g - 1))
                tmp = scr[:, 0].rearrange("p (m n) -> p m n", m=2)
                nc.vector.tensor_reduce(tmp, halves(G % 2), AX.X, ALU.add).then_inc(group_free, 1)
                dve.wait_ge(group_free, G + 1)
                for k in range(2):
                    c = 2 * g + k
                    nc.vector.scalar_tensor_tensor(out=tmp[:, k, :], in0=tmp[:, k, :],
                                                   scalar=vec[:, ROWS["even_b_pw"] + c:ROWS["even_b_pw"] + c + 1],
                                                   in1=z[:, Z_AGATE + c, :], op0=ALU.add, op1=ALU.mult).then_inc(pw_dve.sem, 1)
                dve.wait_ge(pw_dve.sem, pw_dve.at("g1", g))
                nc.vector.tensor_copy(b[:, 2 * g:2 * g + 2, 0, :], tmp).then_inc(pw_dve.sem, 1)
                dve.wait_ge(pw_dve.sem, pw_dve.at("hi", g))
                nc.vector.tensor_tensor(b[:, 2 * g:2 * g + 2, 1, :], tmp, b[:, 2 * g:2 * g + 2, 0, :].bitcast(F32),
                                        ALU.subtract).then_inc(pw_dve.sem, 1)
            with dve.Fori(0, HE) as h:
                dve.wait_ge(at_pe.sem, at_pe.at("vt", h))
                nc.vector.tensor_copy(e_vt, ps[:, 0, 0:T]).then_inc(at_dve.sem, 1)
                dve.wait_ge(at_pe.sem, at_pe.at("s", h))
                nc.vector.tensor_tensor(e_s, ps[:, 1, :].rearrange("p (q n) -> p q n", q=2), causal[:], ALU.add).then_inc(at_dve.sem, 1)
                dve.wait_ge(at_dve.sem, at_dve.at("mask", h))
                nc.vector.tensor_reduce(stat[:, 0:2], e_s, AX.X, ALU.max).then_inc(at_dve.sem, 1)
                dve.wait_ge(at_dve.sem, at_dve.at("max", h))
                nc.vector.tensor_scalar(stat[:, 2:4], stat[:, 0:2], -1.0, None, ALU.mult).then_inc(at_dve.sem, 1)
                dve.wait_ge(at_act.sem, at_act.at("p1", h))
                nc.vector.reciprocal(stat[:, 6:8], stat[:, 4:6]).then_inc(at_dve.sem, 1)
                dve.wait_ge(at_dve.sem, at_dve.at("rsum", h))
                for q in range(TT):
                    nc.vector.tensor_scalar(e_p[:, q, :], e_p[:, q, :], stat[:, 6 + q:7 + q], None, ALU.mult).then_inc(at_dve.sem, 1)
                dve.wait_ge(at_pe.sem, at_pe.at("pt", h))
                nc.vector.tensor_copy(e_pt, ps[:, 2, :].rearrange("p (q n) -> p q n", q=2)).then_inc(at_dve.sem, 1)
                dve.wait_ge(at_pe.sem, at_pe.at("o", h))
                tmp = scr[:, 1, 0:T]
                nc.vector.tensor_tensor(tmp, ps[:, 3, 0:T], z[:, bass.ds(h + Z_BGATE, 1), :].rearrange("p a n -> p (a n)"),
                                        ALU.mult).then_inc(at_dve.sem, 1)
                dve.wait_ge(at_dve.sem, at_dve.at("o", h))
                bh = b[:, bass.ds(h + 8, 1), :, :].rearrange("p a s n -> p (a s) n")
                nc.vector.tensor_copy(bh[:, 0, :], tmp).then_inc(at_dve.sem, 1)
                dve.wait_ge(at_dve.sem, at_dve.at("hi", h))
                nc.vector.tensor_tensor(bh[:, 1, :], tmp, bh[:, 0, :].bitcast(F32), ALU.subtract).then_inc(at_dve.sem, 1)
            to_x("even_w_out")
            norm(1)
            to_z("odd_w_in", 3, Z_CQ, per=3)
            to_z("odd_w_in", 8, Z_OGATE, u=12, g=3)
            rg = lambda c: vec[:, c:c + 1]
            dve.wait_ge(od_act.sem, od_act.at("cqroot"))
            dve.wait_ge(group_free, GROUP0["odd_w_in"] + 11)
            nc.vector.reciprocal(scr[:, 2, T:2 * T], scr[:, 2, 0:T]).then_inc(od_dve.sem, 1)
            dve.wait_ge(od_dve.sem, od_dve.at("cqr"))
            for c in range(4):
                nc.vector.scalar_tensor_tensor(out=z[:, Z_CQ + c, :], in0=z[:, Z_CQ + c, :], scalar=rg(ROWS["odd_q_norm"] + c),
                                               in1=scr[:, 2, T:2 * T], op0=ALU.mult, op1=ALU.mult).then_inc(od_dve.sem, 1)
            dve.wait_ge(od_act.sem, od_act.at("cqhi"))
            nc.vector.tensor_tensor(b[:, 0:4, 1, :], z[:, Z_CQ:Z_CQ + 4, :], b[:, 0:4, 0, :].bitcast(F32),
                                    ALU.subtract).then_inc(od_dve.sem, 1)
            nc.vector.reciprocal(scr[:, 3, T:2 * T], scr[:, 3, 0:T]).then_inc(od_dve.sem, 1)
            dve.wait_ge(od_dve.sem, od_dve.at("kvr"))
            for c in range(2):
                nc.vector.scalar_tensor_tensor(out=ckvn[:, c, :], in0=z[:, Z_CKV + c, :], scalar=rg(ROWS["odd_kv_norm"] + c),
                                               in1=scr[:, 3, T:2 * T], op0=ALU.mult, op1=ALU.mult).then_inc(od_dve.sem, 1)
            dve.wait_ge(od_pe.sem, od_pe.at("kvt"))
            nc.vector.tensor_copy(ckvt[:], ps[:, 2, :].rearrange("p (a n) -> p a n", a=2)).then_inc(od_dve.sem, 1)
            dve.wait_ge(od_pe.sem, od_pe.at("ik"))
            for q in range(TT):
                nc.vector.bn_stats(stat[:, 24 + 6 * q:30 + 6 * q], ps[:, 3, P * q:P * q + ID]).then_inc(od_dve.sem, 1)
            for q in range(TT):
                dve.wait_ge(od_dve.sem, od_dve.at(f"bn{q}"))
                nc.vector.bn_aggr(stat[:, 16 + 2 * q:18 + 2 * q], stat[:, 24 + 6 * q:30 + 6 * q]).then_inc(od_dve.sem, 1)
            dve.wait_ge(od_act.sem, od_act.at("ikroot"))
            nc.vector.reciprocal(stat[:, 22:24], stat[:, 20:22]).then_inc(od_dve.sem, 1)
            dve.wait_ge(od_dve.sem, od_dve.at("ikr"))
            for q in range(TT):
                for k in range(2):
                    nc.vector.tensor_scalar(ikn[:, P * q + ID * k:P * q + ID * k + ID], ps[:, 3, P * q:P * q + ID],
                                            stat[:, 16 + 2 * q:17 + 2 * q], stat[:, 22 + q:23 + q],
                                            ALU.subtract, ALU.mult).then_inc(od_dve.sem, 1)
            dve.wait_ge(od_pe.sem, od_pe.at("ikt"))
            nc.vector.tensor_scalar(ikt[:], ps[:, 0, 0:T], rg(ROWS["ik_g"]), rg(ROWS["ik_b"]), ALU.mult, ALU.add).then_inc(od_dve.sem, 1)
            nc.vector.tensor_scalar(iw[:], ps[:, 3, 0:2 * P].rearrange("p (q n) -> p q n", q=2)[:, :, ID:ID + IH],
                                    IH ** -0.5 * ID ** -0.5, None, ALU.mult).then_inc(od_dve.sem, 1)
            to_z("odd_w_iq", 4, Z_IQ, per=4)
            dve.wait_ge(od_pe.sem, od_pe.at("ik"))
            nc.vector.memset(score, 0.0).then_inc(od_dve.sem, 1)
            with dve.Fori(0, 8) as c:
                dve.wait_ge(ix_act.sem, ix_act.at("relu", c))
                dve.wait_ge(od_dve.sem, od_dve.at("zero"))
                for k in range(2):
                    for q in range(TT):
                        if k == 0:
                            dve.wait_ge(ix_dve.sem, ix_dve.done(c))
                        else:
                            dve.wait_ge(ix_dve.sem, ix_dve.at(f"s{q}", c))
                        nc.vector.scalar_tensor_tensor(out=score[:, q, :], in0=relu[:, 2 * k + q, :],
                                                       scalar=iw[:, q, bass.ds(c * 2 + k, 1)], in1=score[:, q, :],
                                                       op0=ALU.mult, op1=ALU.add).then_inc(ix_dve.sem, 1)
            dve.wait_ge(ix_dve.sem, ix_dve.done(8))
            nc.vector.scalar_tensor_tensor(out=work, in0=causal[:], scalar=3.0e8, in1=score, op0=ALU.mult, op1=ALU.add).then_inc(tk_dve.sem, 1)
            prev = ["fill", "fill"]
            for r in range(8):
                for q in range(TT):
                    dve.wait_ge(tk_dve.sem, tk_dve.at(prev[q]))
                    nc.vector.max(stat[:, 40 + 8 * q:48 + 8 * q], work[:, q, :]).then_inc(tk_dve.sem, 1)
                for q in range(TT):
                    dve.wait_ge(tk_dve.sem, tk_dve.at(f"max{r}{q}"))
                    nc.vector.match_replace(work[:, q, :], stat[:, 40 + 8 * q:48 + 8 * q], work[:, q, :],
                                            -3.4e38).then_inc(tk_dve.sem, 1)
                    prev[q] = f"rep{r}{q}"
            dve.wait_ge(tk_dve.sem, tk_dve.at("rep71"))
            nc.vector.tensor_scalar(work, work, -3.2e38, -1.0e30, ALU.is_ge, ALU.mult).then_inc(tk_dve.sem, 1)
            dve.wait_ge(tk_dve.sem, tk_dve.at("sel"))
            nc.vector.tensor_tensor(addm, work, causal[:], ALU.add).then_inc(tk_dve.sem, 1)
            with dve.Fori(0, 4) as i:
                for k in range(2):
                    g = i * 2 + k
                    G = g + GROUP0["odd_w_qb"]
                    dve.wait_ge(unit_used, g + (UNIT0["odd_w_qb"] + 1))
                    tmp = scr[:, 2 + k].rearrange("p (m n) -> p m n", m=2)
                    nc.vector.tensor_reduce(tmp, halves((GROUP0["odd_w_qb"] + k) % 2), AX.X, ALU.add).then_inc(group_free, 1)
                    dve.wait_ge(group_free, G + 1)
                    nc.vector.tensor_copy(a[:, bass.ds(i * 4 + 2 * k, 2), 0, :], tmp).then_inc(qb_dve.sem, 1)
                    dve.wait_ge(qb_dve.sem, qb_dve.at("hi", g))
                    nc.vector.tensor_tensor(a[:, bass.ds(i * 4 + 2 * k, 2), 1, :], tmp,
                                            a[:, bass.ds(i * 4 + 2 * k, 2), 0, :].bitcast(F32), ALU.subtract).then_inc(qb_dve.sem, 1)
            with dve.Fori(0, 4) as i:
                for k in range(4):
                    if k < 3:
                        dve.wait_ge(part_done, i * 3 + (k + 1))
                    else:
                        dve.wait_ge(unit_used, i + (UNIT0["odd_w_uk"] + 1))
                    nc.vector.tensor_reduce(z[:, bass.ds(i * 8 + (Z_QLAT + 2 * k), 2), :],
                                            halves((GROUP0["odd_w_uk"] + k) % 2), AX.X, ALU.add).then_inc(group_free, 1)
            for half in range(2):
                with dve.Fori(0, 8) as h8:
                    h = h8 + 8 * half
                    dve.wait_ge(da_pe.sem, da_pe.at("s", h))
                    dve.wait_ge(tk_dve.sem, tk_dve.at("am"))
                    nc.vector.tensor_tensor(o_s, ps[:, 0, :].rearrange("p (q n) -> p q n", q=2), addm, ALU.add).then_inc(da_dve.sem, 1)
                    dve.wait_ge(da_dve.sem, da_dve.at("mask", h))
                    nc.vector.tensor_reduce(stat[:, 0:2], o_s, AX.X, ALU.max).then_inc(da_dve.sem, 1)
                    dve.wait_ge(da_dve.sem, da_dve.at("max", h))
                    nc.vector.tensor_scalar(stat[:, 2:4], stat[:, 0:2], -1.0, None, ALU.mult).then_inc(da_dve.sem, 1)
                    dve.wait_ge(da_act.sem, da_act.at("p1", h))
                    nc.vector.reciprocal(stat[:, 6:8], stat[:, 4:6]).then_inc(da_dve.sem, 1)
                    dve.wait_ge(da_dve.sem, da_dve.at("rsum", h))
                    for q in range(TT):
                        nc.vector.tensor_scalar(o_p[:, q, :], o_p[:, q, :], stat[:, 6 + q:7 + q], None, ALU.mult).then_inc(da_dve.sem, 1)
                    dve.wait_ge(da_pe.sem, da_pe.at("pt", h))
                    nc.vector.tensor_copy(o_pt, ps[:, 1, :].rearrange("p (q n) -> p q n", q=2)).then_inc(da_dve.sem, 1)
                    dve.wait_ge(da_act.sem, da_act.at("ohi", h))
                    ah = a[:, bass.ds(h8 * 2, 2), :, :]
                    nc.vector.tensor_tensor(ah[:, :, 1, :], ps[:, 2, :].rearrange("p (k n) -> p k n", k=2),
                                            ah[:, :, 0, :].bitcast(F32), ALU.subtract).then_inc(da_dve.sem, 1)
                for g4 in range(4):
                    g = 4 * half + g4
                    G = GROUP0["odd_w_uv"] + g
                    if g % 2 == 0:
                        dve.wait_ge(part_done, 12 + g // 2 + 1)
                    else:
                        dve.wait_ge(unit_used, UNIT0["odd_w_uv"] + g // 2 + 1)
                    if g:
                        dve.wait_ge(uv_dve.sem, uv_dve.at("lo", g - 1))
                    tmp = scr[:, 2].rearrange("p (m n) -> p m n", m=2)
                    nc.vector.tensor_reduce(tmp, halves(G % 2), AX.X, ALU.add).then_inc(group_free, 1)
                    dve.wait_ge(group_free, G + 1)
                    dve.wait_ge(od_act.sem, od_act.at("ogate"))
                    nc.vector.tensor_tensor(tmp, tmp, z[:, Z_OGATE + 2 * g:Z_OGATE + 2 * g + 2, :], ALU.mult).then_inc(uv_dve.sem, 1)
                    dve.wait_ge(uv_dve.sem, uv_dve.at("gate", g))
                    nc.vector.tensor_copy(b[:, 2 * g:2 * g + 2, 0, :], tmp).then_inc(uv_dve.sem, 1)
                    dve.wait_ge(uv_dve.sem, uv_dve.at("hi", g))
                    nc.vector.tensor_tensor(b[:, 2 * g:2 * g + 2, 1, :], tmp, b[:, 2 * g:2 * g + 2, 0, :].bitcast(F32),
                                            ALU.subtract).then_inc(uv_dve.sem, 1)
            to_x("odd_w_out")
            norm(2)
            norm(3)
            to_z("w_in_2", 20, 0)
            S = lambda n: stat[:, 0:32]
            dve.wait_ge(sc_pe.sem, sc_pe.at("scal"))
            dve.wait_ge(small_in, 16 * 4)
            aa = flat(dsc[:, AA])
            for c in range(TT):
                nc.vector.tensor_tensor(aa[:, 16 * c:16 * c + 16], ps[:, 0, c * 32 + 16:c * 32 + 32], dtb[:, 0, :], ALU.add).then_inc(sc_dve.sem, 1)
            dve.wait_ge(sc_dve.sem, sc_dve.at("a1"))
            nc.vector.tensor_scalar(flat(dsc[:, NEG]), aa, -1.0, None, ALU.mult).then_inc(sc_dve.sem, 1)
            dve.wait_ge(sc_dve.sem, sc_dve.at("neg"))
            nc.vector.tensor_tensor(S(0), flat(dsc[:, NEG]), aa, ALU.max).then_inc(sc_dve.sem, 1)
            nc.vector.tensor_scalar(aa, aa, 0.0, None, ALU.max).then_inc(sc_dve.sem, 1)
            dve.wait_ge(sc_act.sem, sc_act.at("ea"))
            dve.wait_ge(sc_dve.sem, sc_dve.at("pos"))
            nc.vector.tensor_tensor(aa, aa, S(0), ALU.add).then_inc(sc_dve.sem, 1)
            dve.wait_ge(sc_dve.sem, sc_dve.at("sp"))
            nc.vector.tensor_scalar(dtb[:, 1, :], dtb[:, 1, :], -1.0, None, ALU.mult).then_inc(sc_dve.sem, 1)
            dve.wait_ge(sc_dve.sem, sc_dve.at("nea"))
            for c in range(TT):
                nc.vector.tensor_tensor(dsc[:, GG, :, c, :], aa[:, 16 * c:16 * c + 16].rearrange("p (d h) -> p d h", d=2),
                                        dtb[:, 1, :].rearrange("p (d h) -> p d h", d=2), ALU.mult).then_inc(sc_dve.sem, 1)
            dve.wait_ge(sc_pe.sem, sc_pe.at("cum"))
            nc.vector.tensor_copy(flat(dsc[:, GC]), ps[:, 1, 0:32]).then_inc(sc_dve.sem, 1)
            nc.vector.tensor_copy(flat(dsc[:, REM]), ps[:, 1, 32:64]).then_inc(sc_dve.sem, 1)
            dve.wait_ge(sc_act.sem, sc_act.at("er"))
            nc.vector.tensor_scalar(flat(dsc[:, NEG]), flat(dsc[:, EG]), -1.0, None, ALU.mult).then_inc(sc_dve.sem, 1)
            with dve.Fori(0, FG) as g:
                dve.wait_ge(fo_act.sem, fo_act.at("hi", g))
                bg = b[:, bass.ds(g + 8, 1), :, :].rearrange("p a s n -> p (a s) n")
                nc.vector.tensor_tensor(bg[:, 1, :], ps[:, 3, 0:T], bg[:, 0, :].bitcast(F32), ALU.subtract).then_inc(fo_dve.sem, 1)
            two = lambda v: v.rearrange("p (c i) -> p c i", c=2).unsqueeze(1).broadcast_to([P, 2, 2, P])
            dc = lambda v: v.rearrange("p (d c) i -> p d c i", d=2)
            idb = ident[:].unsqueeze(1).broadcast_to([P, 4, P])
            with dve.Fori(0, HN // 2) as i:
                h = [i * 2 + w.w for w in ways]

                def per(n, w):
                    return dsc[:, n, :, :, bass.ds(h[w.w], 1)].rearrange("p d c h -> p (d c) h").broadcast_to([P, 4, P])

                def col(n, d, c, w):
                    return dsc[:, n, d, c, bass.ds(h[w.w], 1)]

                def gates_out(n):
                    G = GROUP0["gates"] + n
                    dve.wait_ge(unit_used, i * 16 + (UNIT0["gates"] + 4 * n + 4))
                    place, parts = z[:, bass.ds(i * 2 + 8 * n, 2), :], halves(G % 2)
                    nc.vector.tensor_scalar(place, parts[:, :, :, 0], 0.0, None, ALU.add).then_inc(gate_half, 1)
                    dve.wait_ge(gate_half, i * 4 + (n + 1))
                    nc.vector.tensor_tensor(place, place, parts[:, :, :, 1], ALU.add).then_inc(group_free, 1)

                for w in ways:
                    own = dn_dve[w.w]
                    if w.w == 0:
                        dve.wait_ge(group_free, i * 4 + (GROUP0["w_in_2"] + 20))
                        dve.wait_ge(fo_dve.sem, fo_dve.done(FG))
                    dve.wait_ge(own.sem, own.done(i))
                    dve.wait_ge(dn_act[w.w].sem, dn_act[w.w].done(i))
                    src = [z[:, bass.ds(h[w.w] + 8 * y, 1), :].rearrange("p a n -> p (a n)") for y in range(3)]
                    dst = (w.qk_feat[:, 0, :], w.qk_feat[:, 1, :], w.v_feat)
                    tap = lambda k, y: vec[:, bass.ds(h[w.w] + (ROWS["conv_w_2"] + 24 * k + 8 * y), 1)]
                    for y in range(3):
                        nc.vector.tensor_scalar(dst[y], src[y], tap(2, y), None, ALU.mult).then_inc(own.sem, 1)
                    for n, (k, o0, i0, m) in enumerate(((0, 2, 0, T - 2), (1, 1, 0, T - 1), (3, 0, 1, T - 1), (4, 0, 2, T - 2))):
                        for y in range(3):
                            dve.wait_ge(own.sem, own.at(f"cv{y}{n}", i))
                            nc.vector.scalar_tensor_tensor(out=dst[y][:, o0:o0 + m], in0=src[y][:, i0:i0 + m], scalar=tap(k, y),
                                                           in1=dst[y][:, o0:o0 + m], op0=ALU.mult, op1=ALU.add).then_inc(own.sem, 1)
                for w in ways:
                    own = dn_dve[w.w]
                    dve.wait_ge(dn_act[w.w].sem, dn_act[w.w].at("root", i))
                    nc.vector.reciprocal(w.root, w.root).then_inc(own.sem, 1)
                    dve.wait_ge(own.sem, own.at("rn", i))
                    nc.vector.scalar_tensor_tensor(out=w.qk_feat[:, 0, :], in0=w.qk_feat[:, 0, :], scalar=DH ** -0.5,
                                                   in1=w.root[:, 0, :], op0=ALU.mult, op1=ALU.mult).then_inc(own.sem, 1)
                    nc.vector.tensor_tensor(w.qk_feat[:, 1, :], w.qk_feat[:, 1, :], w.root[:, 1, :], ALU.mult).then_inc(own.sem, 1)
                    nc.vector.tensor_copy(w.gate, per(GG, w)).then_inc(own.sem, 1)
                for w in ways:
                    own = dn_dve[w.w]
                    dve.wait_ge(dn_pe[w.w].sem, dn_pe[w.w].at("gc", i))
                    dve.wait_ge(own.sem, own.at("kn", i))
                    nc.vector.tensor_tensor(w.decay, four1(w.x_ps), per(GC, w), ALU.subtract).then_inc(own.sem, 1)
                    dve.wait_ge(own.sem, own.at("dsub", i))
                    nc.vector.scalar_tensor_tensor(out=w.decay, in0=w.decay, scalar=0.0, in1=dmask[:], op0=ALU.min,
                                                   op1=ALU.add).then_inc(own.sem, 1)
                for w in ways:
                    own = dn_dve[w.w]
                    dve.wait_ge(dn_act[w.w].sem, dn_act[w.w].at("dexp", i))
                    dve.wait_ge(dn_pe[w.w].sem, dn_pe[w.w].at("gram", i))
                    nc.vector.tensor_tensor(dc(w.m), two(w.y_ps[:, 0:T]), dc(w.decay), ALU.mult).then_inc(own.sem, 1)
                    dve.wait_ge(own.sem, own.at("mt1", i))
                    nc.vector.tensor_tensor(w.m, w.m, per(BETA, w), ALU.mult).then_inc(own.sem, 1)
                    nc.vector.tensor_tensor(dc(w.qk), two(w.y_ps[:, T:2 * T]), dc(w.decay), ALU.mult).then_inc(own.sem, 1)
                    nc.vector.tensor_copy(w.t, idb).then_inc(own.sem, 1)
                    nc.vector.tensor_copy(w.u, idb).then_inc(own.sem, 1)
                    dve.wait_ge(own.sem, own.at("mt2", i))
                    nc.vector.tensor_tensor(dc(w.mm), dc(w.m), lmask[:, 0, :, :].unsqueeze(2).broadcast_to([P, 2, 2, P]),
                                            ALU.mult).then_inc(own.sem, 1)
                gates_out(0)
                for l in range(LEVELS):
                    if l < LEVELS - 1:
                        for w in ways:
                            dve.wait_ge(dn_pe[w.w].sem, dn_pe[w.w].at(f"x{l}", i))
                            nc.vector.tensor_tensor(dc(w.mm), dc(w.m), lmask[:, l + 1, :, :].unsqueeze(2).broadcast_to([P, 2, 2, P]),
                                                    ALU.mult).then_inc(dn_dve[w.w].sem, 1)
                    if l in (2, 6):
                        gates_out(l // 4 + 1)
                    for w in ways:
                        own = dn_dve[w.w]
                        dve.wait_ge(dn_pe[w.w].sem, dn_pe[w.w].at(f"tu{l}", i))
                        dve.wait_ge(own.sem, own.at(f"u{l}", i))
                        if l < LEVELS - 1:
                            nc.vector.tensor_tensor(w.t, w.t, four1(w.x_ps), ALU.subtract).then_inc(own.sem, 1)
                        nc.vector.tensor_tensor(w.u, w.u, four1(w.y_ps), ALU.subtract).then_inc(own.sem, 1)
                for w in ways:
                    own = dn_dve[w.w]
                    dve.wait_ge(dn_pe[w.w].sem, dn_pe[w.w].at("y1", i))
                    for d in range(2):
                        nc.vector.tensor_scalar(w.v_new[:, 2 * d + d, :], four1(w.x_ps)[:, d, :], col(BETA, d, d, w), None, ALU.mult).then_inc(own.sem, 1)
                    for d in range(2):
                        dve.wait_ge(own.sem, own.at(("vn1a", "vn1b")[d], i))
                        nc.vector.tensor_scalar(w.v_dec[:, d, :], w.v_new[:, 2 * d + d, :], col(ER, d, d, w), None, ALU.mult).then_inc(own.sem, 1)
                for w in ways:
                    own = dn_dve[w.w]
                    dve.wait_ge(dn_pe[w.w].sem, dn_pe[w.w].at("ks", i))
                    for d in range(2):
                        nc.vector.scalar_tensor_tensor(out=w.r[:, d, :], in0=four1(w.x_ps)[:, d, :], scalar=col(NEG, d, 1 - d, w),
                                                       in1=w.tok[:, 2 + 1 - d, :], op0=ALU.mult, op1=ALU.add).then_inc(own.sem, 1)
                for w in ways:
                    own = dn_dve[w.w]
                    dve.wait_ge(dn_pe[w.w].sem, dn_pe[w.w].at("y2", i))
                    for d in range(2):
                        nc.vector.tensor_scalar(w.v_new[:, 2 * d + 1 - d, :], four1(w.x_ps)[:, d, :], col(BETA, d, 1 - d, w), None, ALU.mult).then_inc(own.sem, 1)
                for w in ways:
                    own = dn_dve[w.w]
                    dve.wait_ge(dn_pe[w.w].sem, dn_pe[w.w].at("o", i))
                    dve.wait_ge(dn_act[w.w].sem, dn_act[w.w].at("qs1", i))
                    nc.vector.tensor_tensor(w.u[:, 0:2, :], four1(w.y_ps)[:, 0:2, :], w.x[:, 2:4, :], ALU.add).then_inc(own.sem, 1)
                for w in ways:
                    own = dn_dve[w.w]
                    dve.wait_ge(dn_act[w.w].sem, dn_act[w.w].at("oroot", i))
                    nc.vector.reciprocal(w.norm[:, 4:6], w.norm[:, 2:4]).then_inc(own.sem, 1)
                    dve.wait_ge(own.sem, own.at("orn", i))
                    for c in range(TT):
                        nc.vector.tensor_scalar(w.u[:, c, :], w.u[:, c, :], w.norm[:, 4 + c:5 + c], None, ALU.mult).then_inc(own.sem, 1)
                for w in ways:
                    own = dn_dve[w.w]
                    dve.wait_ge(dn_pe[w.w].sem, dn_pe[w.w].at("ot", i))
                    dve.wait_ge(dn_act[w.w].sem, dn_act[w.w].at("sz", i))
                    tmp = w.v_dec[:, 2:4, :].rearrange("p a n -> p (a n)")
                    nc.vector.scalar_tensor_tensor(out=tmp, in0=w.x_ps[:, 0:T], scalar=vec[:, ROWS["g_dn_head_2"]:ROWS["g_dn_head_2"] + 1],
                                                   in1=w.x[:, 0:2, :].rearrange("p a n -> p (a n)"), op0=ALU.mult, op1=ALU.mult).then_inc(own.sem, 1)
                    dve.wait_ge(own.sem, own.at("ot", i))
                    bh = b[:, bass.ds(h[w.w], 1), :, :].rearrange("p a s n -> p (a s) n")
                    nc.vector.tensor_copy(bh[:, 0, :], tmp).then_inc(own.sem, 1)
                    dve.wait_ge(own.sem, own.at("hi", i))
                    nc.vector.tensor_tensor(bh[:, 1, :], tmp, bh[:, 0, :].bitcast(F32), ALU.subtract).then_inc(own.sem, 1)
                gates_out(3)
            own, at = mx_dve.sem, mx_dve.at
            with dve.Fori(0, 4) as i:
                for k in range(2):
                    r = i * 2 + k
                    up, fr = (scr[:, 2 * k + n].rearrange("p (m n) -> p m n", m=2) for n in range(2))
                    for n, (v, y) in enumerate(((up, "dn"), (fr, "fr"))):
                        dve.wait_ge(unit_used, i * 8 + (UNIT0["mix"] + 4 * k + 2 * n + 2))
                        if k == 0 and n == 0:
                            dve.wait_ge(mx_act.sem, mx_act.at("sigd"))
                            dve.wait_ge(dn_dve[1].sem, dn_dve[1].done(HN // 2))
                        nc.vector.tensor_reduce(v, halves((GROUP0["mix"] + n) % 2), AX.X, ALU.add).then_inc(group_free, 1)
                        dve.wait_ge(group_free, i * 4 + (GROUP0["mix"] + 2 * k + n + 1))
                        nc.vector.tensor_tensor(v, v, z[:, bass.ds(i * 2 + (16 * k + 8 * n), 2), :], ALU.mult).then_inc(own, 1)
                    dve.wait_ge(own, at("frg", r))
                    nc.vector.tensor_tensor(fr, up, fr, ALU.add).then_inc(own, 1)
                    dve.wait_ge(own, at("sum", r))
                    aa = a[:, bass.ds(i * 4 + 2 * k, 2), :, :]
                    nc.vector.tensor_copy(aa[:, :, 0, :], fr).then_inc(own, 1)
                    dve.wait_ge(own, at("hi", r))
                    nc.vector.tensor_tensor(aa[:, :, 1, :], fr, aa[:, :, 0, :].bitcast(F32), ALU.subtract).then_inc(own, 1)
            to_x("w_o_2")
            norm(4)
            for ph in range(4):
                g0 = GROUP0["mlp"] + 16 * ph
                with dve.Fori(0, 4) as i:
                    for k in range(2):
                        r = i * 2 + (k + 8 * ph)
                        dve.wait_ge(unit_used, i * 8 + (UNIT0["mlp"] + 64 * ph + 4 * (k + 1)))
                        tmp = scr[:, 2 * k].rearrange("p (m n) -> p m n", m=2)
                        tm2 = scr[:, 2 * k + 1].rearrange("p (m n) -> p m n", m=2)
                        bb = b[:, bass.ds(i * 4 + 2 * k, 2), :, :]
                        if k == 0:
                            dve.wait_ge(ml_dve.sem, ml_dve.done(r))
                        nc.vector.tensor_reduce(tmp, halves((g0 + k) % 2), AX.X, ALU.add).then_inc(group_free, 1)
                        dve.wait_ge(group_free, i * 2 + (g0 + k + 1))
                        nc.vector.scalar_tensor_tensor(out=tm2, in0=tmp, scalar=0.0, in1=tmp, op0=ALU.max, op1=ALU.mult).then_inc(ml_dve.sem, 1)
                        dve.wait_ge(ml_dve.sem, ml_dve.at("sq", r))
                        nc.vector.tensor_copy(bb[:, :, 0, :], tm2).then_inc(ml_dve.sem, 1)
                        dve.wait_ge(ml_dve.sem, ml_dve.at("hi", r))
                        nc.vector.tensor_tensor(bb[:, :, 1, :], tm2, bb[:, :, 0, :].bitcast(F32), ALU.subtract).then_inc(ml_dve.sem, 1)
                to_x("mlp", u=64 * ph + 32, g=16 * ph + 8)
            norm(5, last=True)
            for s in range(8):
                dve.wait_ge(fin_pe, s + 1)
                nc.vector.tensor_copy(z[:, 16 + 2 * s:18 + 2 * s, :], ps[:, 2 + s % 2, :].rearrange("p (q n) -> p q n", q=2)).then_inc(fin_dve, 1)

        @block.tensor
        def _(pe):
            pe.wait_ge(consts_in, 16 * N_CONST)
            for k in range(N_PACKS):
                rows = min(P, N_ROWS - k * P)
                dst = (ps, lin_ps)[k // 4][:, 0, (k % 4) * P:(k % 4) * P + rows]
                m = nc.tensor.transpose(dst, pk[0:rows, k * P:(k + 1) * P], ident[0:rows, 0:rows])
            m.then_inc(tp_pe, 1)
            pe.wait_ge(x_in, 32)
            for s in range(8):
                if s >= 3:
                    pe.wait_ge(x_done, s - 2)
                for k in range(2):
                    for tt in range(TT):
                        c = 2 * s + k
                        m = nc.tensor.transpose(ps[:, 1 + s % 3, k * T + tt * P:k * T + (tt + 1) * P],
                                                z[:, 8 * tt:8 * tt + 8, :].rearrange("p a b -> p (a b)")[:, c * P:(c + 1) * P],
                                                ident[:])
                m.then_inc(tp_pe, 1)
            pe.wait_ge(tp_ev, 2)
            pe.wait_ge(bld, 3)

            def norm_sums(r):
                for s in range(8):
                    pe.wait_ge(nr_act.sem, nr_act.at(f"sq{s}", r))
                    for k in range(2):
                        m = nc.tensor.matmul(ps[:, 0, 0:T], ones[:], scr[:, s % 2, k * T:(k + 1) * T],
                                             start=(s == 0 and k == 0), stop=(s == 7 and k == 1))
                    m.then_inc(nr_pe.sem, 1)

            def linear(u0, g0, n, kus, src, k0=0, waits=None, per=2):
                slots = lambda j: [(u0 + j * kus + q) % SLOTS for q in range(kus)]

                def turn(u, g, w=None, first=False):
                    for j in range(per):
                        run(u + j * kus, slots(j), g + j, (g0 + j) % 2, src, k0, w if j == 0 else None, not (first and g0 == 0))

                turn(u0, g0, waits, first=True)
                if n > per:
                    with pe.Fori(1, n // per) as i:
                        turn(i * (per * kus) + u0, i * per + g0)

            def product(u, g, parity, q, n, slot, src, k0, wait, free):
                if q == 0 and free:
                    pe.wait_ge(group_free, g - 1)
                pe.wait_ge(lo_done, u + 1)
                hi = w_hi[:, slot].rearrange("p (k n) -> p k n", k=UK)
                lo = w_lo[:, slot].rearrange("p (k n) -> p k n", k=UK)
                for k in range(UK):
                    kk = k0 + q * UK + k
                    if wait:
                        wait(q * UK + k)
                    for m in range(2):
                        acc = lin_ps[:, 2 * parity + m, :]
                        nc.tensor.matmul(acc, hi[:, k, m * P:(m + 1) * P], src[:, kk].rearrange("p s n -> p (s n)"),
                                         start=(q == 0 and k == 0), stop=False)
                        last = nc.tensor.matmul(acc[:, 0:T], lo[:, k, m * P:(m + 1) * P], src[:, kk, 0, :],
                                                start=False, stop=(q == n - 1 and k == UK - 1))
                last.then_inc(unit_used, 1)

            def run(u, slots, g, parity, src, k0, wait, free):
                for q, slot in enumerate(slots):
                    product(u + q, g, parity, q, len(slots), slot, src, k0, wait, free)

            def normed(r):
                def wait(c):
                    if c % 2 == 0:
                        pe.wait_ge(nr_lo.sem, nr_lo.at(f"{c // 2}", SPLIT_ROUND[r]))
                return wait

            norm_sums(0)
            linear(0, 0, 28, 4, a, waits=normed(0))
            for c in range(8):
                pe.wait_ge(cv_dve.sem, cv_dve.at(f"tap{TAPS - 1}", c))
                m = nc.tensor.matmul(ps[:, 0, 0:T], ones[:], z[:, Z_AGT + c, :], start=(c == 0), stop=(c == 7))
            m.then_inc(ln_pe.sem, 1)
            for s in range(4):
                pe.wait_ge(ln_act.sem, ln_act.at(f"sq{s}"))
                for k in range(2):
                    m = nc.tensor.matmul(ps[:, 1, 0:T], ones[:], scr[:, s % 2, k * T:(k + 1) * T],
                                         start=(s == 0 and k == 0), stop=(s == 3 and k == 1))
                m.then_inc(ln_pe.sem, 1)
            def ln_ready(c):
                if c % 2 == 0:
                    pe.wait_ge(ln_dve.sem, ln_dve.at(f"lo{c // 2}"))
            linear(UNIT0["even_w_pw"], GROUP0["even_w_pw"], 4, 2, a, waits=ln_ready, per=4)
            with pe.Fori(0, HE) as h:
                pe.wait_ge(at_act.sem, at_act.at("vs", h))
                for c in range(TT):
                    m = nc.tensor.transpose(ps[:, 0, c * P:(c + 1) * P], e_v[:, c * P:(c + 1) * P], ident[:])
                m.then_inc(at_pe.sem, 1)
                for q in range(TT):
                    m = nc.tensor.matmul(ps[:, 1, q * T:(q + 1) * T], e_q[:, q * P:(q + 1) * P],
                                         z[:, bass.ds(h + Z_K, 1), :].rearrange("p a n -> p (a n)"), start=True, stop=True)
                m.then_inc(at_pe.sem, 1)
                pe.wait_ge(at_dve.sem, at_dve.at("n1", h))
                for kt in range(TT):
                    for q in range(TT):
                        m = nc.tensor.transpose(ps[:, 2, kt * T + q * P:kt * T + (q + 1) * P], e_p[:, q, kt * P:(kt + 1) * P], ident[:])
                m.then_inc(at_pe.sem, 1)
                pe.wait_ge(at_dve.sem, at_dve.at("ptc", h))
                for kt in range(TT):
                    m = nc.tensor.matmul(ps[:, 3, 0:T], e_vt[:, kt * P:(kt + 1) * P], e_pt[:, kt, :],
                                         start=(kt == 0), stop=(kt == TT - 1))
                m.then_inc(at_pe.sem, 1)

            def cat_ready(c):
                if c == 0:
                    pe.wait_ge(pw_dve.sem, pw_dve.at("lo", 3))
                if c >= 8:
                    pe.wait_ge(at_dve.sem, at_dve.at("lo", c - 8))
            linear(UNIT0["even_w_out"], GROUP0["even_w_out"], 8, 4, b, waits=cat_ready)
            norm_sums(1)
            linear(UNIT0["odd_w_in"], GROUP0["odd_w_in"], 3, 4, a, waits=normed(1), per=3)
            linear(UNIT0["odd_w_in"] + 12, GROUP0["odd_w_in"] + 3, 8, 4, a)
            pe.wait_ge(sw_in, 16)
            for q in range(TT):
                for c in range(DC):
                    for s in range(2):
                        m = nc.tensor.matmul(ps[:, 3, q * P:q * P + ID + IH], a[:, c, s, q * P:(q + 1) * P].bitcast(F32),
                                             small_w[:, c * (ID + IH):(c + 1) * (ID + IH)],
                                             start=(c == 0 and s == 0), stop=(c == DC - 1 and s == 1))
            m.then_inc(od_pe.sem, 1)
            pe.wait_ge(od_act.sem, od_act.at("cqsq"))
            for c in range(4):
                m = nc.tensor.matmul(ps[:, 0, 0:T], ones[:], scr[:, 0:2, :].rearrange("p a (k n) -> p (a k) n", k=2)[:, c, :],
                                     start=(c == 0), stop=(c == 3))
            m.then_inc(od_pe.sem, 1)
            pe.wait_ge(od_act.sem, od_act.at("kvsq"))
            for c in range(2):
                m = nc.tensor.matmul(ps[:, 1, 0:T], ones[:], scr[:, 0, c * T:(c + 1) * T], start=(c == 0), stop=(c == 1))
            m.then_inc(od_pe.sem, 1)
            pe.wait_ge(od_dve.sem, od_dve.at("kv1"))
            for q in range(TT):
                for c in range(2):
                    m = nc.tensor.transpose(ps[:, 2, q * T + c * P:q * T + (c + 1) * P], ckvn[:, c, q * P:(q + 1) * P], ident[:])
            m.then_inc(od_pe.sem, 1)
            pe.wait_ge(od_dve.sem, od_dve.at("ikn3"))
            for q in range(TT):
                m = nc.tensor.transpose(ps[:, 0, q * P:(q + 1) * P], ikn[:, q * P:(q + 1) * P], ident[:])
            m.then_inc(od_pe.sem, 1)

            def cq_ready(c):
                if c == 0:
                    pe.wait_ge(od_dve.sem, od_dve.at("cqlo"))
            linear(UNIT0["odd_w_iq"], GROUP0["odd_w_iq"], 4, 1, b, waits=cq_ready, per=4)
            with pe.Fori(0, 8) as c:
                pe.wait_ge(ix_act.sem, ix_act.at("stage", c))
                pe.wait_ge(od_dve.sem, od_dve.at("iw"))
                pe.wait_ge(ix_act.sem, ix_act.done(c))
                for k in range(2):
                    for q in range(TT):
                        m = nc.tensor.matmul(ps[:, k, q * T:(q + 1) * T], iq_st[ID * k:ID * k + ID, q * P:(q + 1) * P],
                                             ikt[ID * k:ID * k + ID, :], start=True, stop=True)
                m.then_inc(ix_pe.sem, 1)
            linear(UNIT0["odd_w_qb"], GROUP0["odd_w_qb"], 8, 1, b, per=4)
            for n in range(4):
                u = UNIT0["odd_w_uk"] + n
                hi = w_hi[:, n].rearrange("p (k n) -> p k n", k=UK)
                lo = w_lo[:, n].rearrange("p (k n) -> p k n", k=UK)
                pe.wait_ge(lo_done, u + 1)
                for j in range(4):
                    h = 4 * n + j
                    G = GROUP0["odd_w_uk"] + h
                    pe.wait_ge(group_free, G - 1)
                    pe.wait_ge(qb_dve.sem, qb_dve.at("lo", h // 2))
                    for m in range(2):
                        acc = lin_ps[:, 2 * (G % 2) + m, :]
                        nc.tensor.matmul(acc, hi[:, j, m * P:(m + 1) * P], a[:, h].rearrange("p s n -> p (s n)"), start=True, stop=False)
                        last = nc.tensor.matmul(acc[:, 0:T], lo[:, j, m * P:(m + 1) * P], a[:, h, 0, :], start=False, stop=True)
                    last.then_inc(unit_used if j == 3 else part_done, 1)
            for half in range(2):
                with pe.Fori(0, 8) as h8:
                    h = h8 + 8 * half
                    pe.wait_ge(da_act.sem, da_act.at("stage", h))
                    pe.wait_ge(da_dve.sem, da_dve.done(h))
                    for q in range(TT):
                        for c in range(2):
                            m = nc.tensor.matmul(ps[:, 0, q * T:(q + 1) * T], o_q[:, c * T + q * P:c * T + (q + 1) * P], ckvn[:, c, :],
                                                 start=(c == 0), stop=(c == 1))
                    m.then_inc(da_pe.sem, 1)
                    pe.wait_ge(da_dve.sem, da_dve.at("n1", h))
                    for kt in range(TT):
                        for q in range(TT):
                            m = nc.tensor.transpose(ps[:, 1, kt * T + q * P:kt * T + (q + 1) * P], o_p[:, q, kt * P:(kt + 1) * P], ident[:])
                    m.then_inc(da_pe.sem, 1)
                    pe.wait_ge(da_dve.sem, da_dve.at("ptc", h))
                    for c in range(2):
                        for kt in range(TT):
                            m = nc.tensor.matmul(ps[:, 2, c * T:(c + 1) * T], ckvt[:, kt, c * P:(c + 1) * P], o_pt[:, kt, :],
                                                 start=(kt == 0), stop=(kt == TT - 1))
                    m.then_inc(da_pe.sem, 1)
                for n in range(2 * half, 2 * half + 2):
                    u = UNIT0["odd_w_uv"] + n
                    hi = w_hi[:, n].rearrange("p (k n) -> p k n", k=UK)
                    lo = w_lo[:, n].rearrange("p (k n) -> p k n", k=UK)
                    pe.wait_ge(lo_done, u + 1)
                    pe.wait_ge(da_dve.sem, da_dve.at("olo", 8 * half + 7))
                    for j in range(2):
                        G = GROUP0["odd_w_uv"] + 2 * n + j
                        pe.wait_ge(group_free, G - 1)
                        for m in range(2):
                            h = 2 * j + m
                            acc = lin_ps[:, 2 * (G % 2) + m, :]
                            for k in range(2):
                                src = a[:, 2 * (4 * (n % 2) + h) + k]
                                nc.tensor.matmul(acc, hi[:, h, k * P:(k + 1) * P], src.rearrange("p s n -> p (s n)"), start=(k == 0), stop=False)
                                last = nc.tensor.matmul(acc[:, 0:T], lo[:, h, k * P:(k + 1) * P], src[:, 0, :], start=False, stop=(k == 1))
                        last.then_inc(unit_used if j == 1 else part_done, 1)

            def o_ready(c):
                if c == 0:
                    pe.wait_ge(uv_dve.sem, uv_dve.at("lo", 7))
            linear(UNIT0["odd_w_out"], GROUP0["odd_w_out"], 8, 4, b, waits=o_ready)
            norm_sums(2)
            norm_sums(3)
            linear(UNIT0["w_in_2"], GROUP0["w_in_2"], 20, 4, a, waits=normed(3))
            pe.wait_ge(table_in, 64)
            for q in range(TT):
                for c in range(DC):
                    for s in range(2):
                        m = nc.tensor.matmul(ps[:, 0, q * 32:q * 32 + 32], a[:, c, s, q * P:(q + 1) * P].bitcast(F32),
                                             scw[:, c * 32:c * 32 + 32], start=(c == 0 and s == 0), stop=(c == DC - 1 and s == 1))
            m.then_inc(sc_pe.sem, 1)
            pe.wait_ge(sc_dve.sem, sc_dve.at("g1"))
            for n in range(4):
                d = n % 2
                m = nc.tensor.matmul(ps[:, 1, 16 * n:16 * n + 16], tri[:, n, :], flat(dsc[:, GG])[:, 16 * d:16 * d + 16], start=True, stop=True)
            m.then_inc(sc_pe.sem, 1)
            with pe.Fori(0, FG) as g:
                pe.wait_ge(fo_act.sem, fo_act.at("stage", g))
                for q in range(TT):
                    m = nc.tensor.matmul(ps[:, 2, q * T:(q + 1) * T], z[:, 46, q * P:(q + 1) * P], z[:, 40, :], start=True, stop=True)
                m.then_inc(fo_pe.sem, 1)
                pe.wait_ge(fo_act.sem, fo_act.at("ab", g))
                pe.wait_ge(fo_dve.sem, fo_dve.done(g))
                for q in range(TT):
                    for s in range(2):
                        m = nc.tensor.matmul(ps[:, 3, 0:T], z[:, 48 + q, s * P:(s + 1) * P], z[:, 41 + 2 * s + q, :],
                                             start=(q == 0 and s == 0), stop=(q == 1 and s == 1))
                m.then_inc(fo_pe.sem, 1)
            with pe.Fori(0, HN // 2) as i:
                def fill(n):
                    g, q = n // 4, n % 4
                    product(i * 16 + (UNIT0["gates"] + n), i * 4 + (GROUP0["gates"] + g), (GROUP0["gates"] + g) % 2,
                            q, 4, q, a, 0, None, True)

                def after(w, engine, name):
                    st = (dn_act if engine == "act" else dn_dve)[w.w]
                    pe.wait_ge(st.sem, st.at(name, i))

                blk = lambda v, n: v[:, n * P:(n + 1) * P]
                for n in range(3):
                    fill(n)
                for w in ways:
                    after(w, "act", "sq")
                    nc.tensor.matmul(w.x_ps, ones[:], w.sq.rearrange("p a n -> p (a n)"), start=True, stop=True).then_inc(dn_pe[w.w].sem, 1)
                fill(3)
                for w in ways:
                    after(w, "dve", "kn")
                    after(w, "act", "sl2")
                    for n in range(4):
                        src = w.qk_feat[:, 1, :] if n < 2 else w.v_feat
                        m = nc.tensor.transpose(blk(w.y_ps, n), blk(src, n % 2), ident[:])
                    m.then_inc(dn_pe[w.w].sem, 1)
                    after(w, "dve", "gb")
                    for n in range(4):
                        m = nc.tensor.matmul(blk(w.x_ps, n), w.gate[:, n, :], tri[:, n // 2, :], start=True, stop=True)
                    m.then_inc(dn_pe[w.w].sem, 1)
                fill(4)
                for w in ways:
                    after(w, "act", "tok")
                    for y in (1, 0):
                        for c in range(TT):
                            m = nc.tensor.matmul(blk(w.y_ps, 2 * (1 - y) + c), blk(w.qk_feat[:, 1, :], c), blk(w.qk_feat[:, y, :], c),
                                                 start=True, stop=True)
                    m.then_inc(dn_pe[w.w].sem, 1)
                fill(5)
                for l in range(LEVELS):
                    fill(6 + l)
                    for w in ways:
                        after(w, "dve", f"u{l}" if l else "mm0")
                        for n in range(4):
                            m = nc.tensor.matmul(blk(w.x_ps, n), w.mm[:, n, :], w.t[:, n, :], start=True, stop=True)
                        m.then_inc(dn_pe[w.w].sem, 1)
                    for w in ways:
                        after(w, "act", f"x{l}")
                        for n in range(4):
                            if l < LEVELS - 1:
                                nc.tensor.matmul(blk(w.x_ps, n), w.u[:, n, :], w.x[:, n, :], start=True, stop=True)
                            m = nc.tensor.matmul(blk(w.y_ps, n), w.x[:, n, :], w.u[:, n, :], start=True, stop=True)
                        m.then_inc(dn_pe[w.w].sem, 1)
                fill(13)
                for w in ways:
                    after(w, "dve", f"u{LEVELS}")
                    for d in range(2):
                        m = nc.tensor.matmul(blk(w.x_ps, d), w.u[:, 3 * d, :], w.tok[:, 2 + d, :], start=True, stop=True)
                    m.then_inc(dn_pe[w.w].sem, 1)
                for w in ways:
                    after(w, "dve", "vkb")
                    for d in range(2):
                        m = nc.tensor.matmul(blk(w.y_ps, d), w.tok[:, d, :], w.v_dec[:, d, :], start=True, stop=True)
                    m.then_inc(dn_pe[w.w].sem, 1)
                fill(14)
                for w in ways:
                    after(w, "act", "s")
                    for y, bank in ((1, w.x_ps), (0, w.y_ps)):
                        for d in range(2):
                            m = nc.tensor.matmul(blk(bank, d), blk(w.qk_feat[:, y, :], 1 - d), w.x[:, d, :], start=True, stop=True)
                        m.then_inc(dn_pe[w.w].sem, 1)
                for w in ways:
                    after(w, "dve", "r2b")
                    for d in range(2):
                        m = nc.tensor.matmul(blk(w.x_ps, d), w.u[:, 2 * d + 1 - d, :], w.r[:, d, :], start=True, stop=True)
                    m.then_inc(dn_pe[w.w].sem, 1)
                fill(15)
                for w in ways:
                    after(w, "dve", "vn2b")
                    after(w, "act", "qs1")
                    for c in range(TT):
                        for d in range(2):
                            m = nc.tensor.matmul(blk(w.y_ps, c), w.qk[:, 2 * d + c, :], w.v_new[:, 2 * d + c, :], start=(d == 0), stop=(d == 1))
                    m.then_inc(dn_pe[w.w].sem, 1)
                for w in ways:
                    after(w, "dve", "on1")
                    for c in range(TT):
                        m = nc.tensor.transpose(blk(w.x_ps, c), w.u[:, c, :], ident[:])
                    m.then_inc(dn_pe[w.w].sem, 1)
            u0, g0 = UNIT0["mix"], GROUP0["mix"]
            for w in range(2):
                pe.wait_ge(dn_dve[w].sem, dn_dve[w].done(HN // 2))
            pe.wait_ge(fo_dve.sem, fo_dve.done(FG))
            with pe.Fori(0, 8) as g:
                run(g * 4 + u0, [0, 1], g * 2 + g0, g0 % 2, b, 0, None, True)
                run(g * 4 + (u0 + 2), [2, 3], g * 2 + (g0 + 1), (g0 + 1) % 2, b, 8, None, True)

            def mix_ready(c):
                if c % 2 == 0:
                    pe.wait_ge(mx_dve.sem, mx_dve.at("lo", c // 2))
            linear(UNIT0["w_o_2"], GROUP0["w_o_2"], 8, 4, a, waits=mix_ready)
            norm_sums(4)
            for ph in range(4):
                def hid_ready(c):
                    if c % 2 == 0:
                        pe.wait_ge(ml_dve.sem, ml_dve.at("lo", 8 * ph + c // 2))
                linear(UNIT0["mlp"] + 64 * ph, GROUP0["mlp"] + 16 * ph, 8, 4, a, waits=normed(4) if ph == 0 else None)
                linear(UNIT0["mlp"] + 64 * ph + 32, GROUP0["mlp"] + 16 * ph + 8, 8, 4, b, waits=hid_ready)
            norm_sums(5)
            for s in range(8):
                pe.wait_ge(nr_lo.sem, nr_lo.at(f"{s}", SPLIT_ROUND[5]))
                if s >= 2:
                    pe.wait_ge(fin_dve, s - 1)
                for q in range(TT):
                    for k in range(2):
                        m = nc.tensor.transpose(ps[:, 2 + s % 2, q * T + k * P:q * T + (k + 1) * P], z[:, 2 * s + k, q * P:(q + 1) * P], ident[:])
                m.then_inc(fin_pe, 1)


def _bfloat16(v):
    return (v.astype(np.float32).view(np.uint32) >> 16).astype(np.uint16)


def _tables():
    i = np.arange(P)
    upto = (i[:, None] <= i[None, :])
    tri = np.stack([upto, upto.T, i[:, None] > i[None, :], i[:, None] < i[None, :]], 1).astype(np.float32)
    q = np.arange(T).reshape(TT, P)
    causal = np.where(np.arange(T)[None, None, :] <= q.T[:, :, None], 0.0, -1.0e30)
    dm = np.where(upto, 0.0, -1.0e30)
    dmask = np.stack([dm, dm, dm.T, dm.T], 1)
    lmask = np.zeros((P, LEVELS, 2, P), np.float32)
    for level in range(LEVELS):
        w = 2 ** level
        same = (i[:, None] // (2 * w)) == (i[None, :] // (2 * w))
        low = same & (i[:, None] // w % 2 == 0) & (i[None, :] // w % 2 == 1)
        lmask[:, level, 0] = low
        lmask[:, level, 1] = low.T
    scale = (T * P) ** -0.5
    ang = 2 * np.pi * np.outer(i, i) / P
    angt = 2 * np.pi * (np.outer(np.arange(T), np.arange(T)) % T) / T
    dft = np.zeros((P, 5, T))
    dft[:, 0, 0:P], dft[:, 0, P:] = np.cos(ang), np.sin(ang)
    for k in range(TT):
        dft[:, 1 + k] = scale * np.cos(angt[k * P:(k + 1) * P])
        dft[:, 3 + k] = -scale * np.sin(angt[k * P:(k + 1) * P])
    return {"c_ident": np.eye(P, dtype=np.float32), "c_tri": tri, "c_causal": _bfloat16(causal), "c_dmask": _bfloat16(dmask),
            "c_lmask": _bfloat16(lmask), "c_dft": dft.astype(np.float32)}


def kernel(**inputs):
    import concourse.bacc as bacc
    from concourse.bass_utils import run_bass_kernel_spmd

    nc = bacc.Bacc("TRN2", target_bir_lowering=False, num_devices=1)
    arrays, t = {}, {}
    for name, a in {**inputs, **_tables()}.items():
        a = np.ascontiguousarray(a)
        if a.shape[0] == 1:
            a = a[0]
        arrays[f"in_{name}"] = a
        t[name] = nc.dram_tensor(f"in_{name}", a.shape, mybir.dt.from_np(a.dtype), kind="ExternalInput").ap()
    out = nc.dram_tensor("out_x", (T, D), F32, kind="ExternalOutput").ap()
    build(nc, t, out)
    r = run_bass_kernel_spmd(nc, [arrays], core_ids=[0])
    return r.results[0]["out_x"].reshape(1, T, D)
```

```python
from contextlib import ExitStack

import numpy as np

import concourse.bass as bass
from concourse import mybir

F32 = mybir.dt.float32
F32R = mybir.dt.float32r
BF16 = mybir.dt.bfloat16
ALU = mybir.AluOpType
ACT = mybir.ActivationFunctionType
AX = mybir.AxisListType

P = 128
T = 256
TT = T // P
D = 2048
DC = D // P
EPS = 1e-6
CW = 1024
TAPS = 31
HE, DH = 8, 128
HO = 16
QL, KVL = 512, 256
IH, ID = 16, 64
TOPK = 64
HN = 8
NT = 5
FG = 8
DFF = 8192
LEVELS = 7

UK, UN = 4, 256
SLOTS = 4
GROUP = 2

ROWS = {}


def _rows():
    at = 0
    for name, n in (("even_norm", 16), ("odd_norm", 16), ("g_mix_2", 16), ("g_mlp_2", 16), ("g_final_2", 16),
                    ("even_b_glu", 16), ("even_b_dw", 8), ("even_conv_ln_g", 8), ("even_conv_ln_b", 8),
                    ("even_b_pw", 8), ("even_w_dw", 248), ("odd_q_norm", 4), ("odd_kv_norm", 2), ("g_dn_head_2", 1),
                    ("conv_w_2", 120), ("ik_g", 1), ("ik_b", 1), ("final_norm", 16)):
        ROWS[name] = at
        at += n
    return at


N_ROWS = _rows()
N_PACKS = -(-N_ROWS // P)

ZB = 56
Z_AVAL, Z_AGT, Z_AGATE, Z_Q, Z_K, Z_V, Z_BGATE = (8 * n for n in range(7))
Z_OGATE, Z_QLAT, Z_CQ, Z_CKV, Z_IQ = 0, 16, 48, 52, 16
Z_DQ, Z_DK, Z_DV, Z_DZ, Z_F, Z_DN, Z_DFT = 0, 8, 16, 24, 32, 40, 40

LINEARS = (("even_w_in", 112), ("even_w_pw", 8), ("even_w_out", 32), ("odd_w_in", 20), ("odd_w_iq", 4), ("odd_gate", 24),
           ("odd_w_qb", 8), ("odd_w_uk", 4), ("odd_w_uv", 4), ("odd_w_out", 32), ("w_in_2", 80),
           ("gates", 64), ("mix", 32), ("w_o_2", 32), ("mlp", 256))
UNIT0 = {}
_at = 0
for _name, _n in LINEARS:
    UNIT0[_name] = _at
    _at += _n
UNITS = _at
GROUPS = (("even_w_in", 28), ("even_w_pw", 4), ("even_w_out", 8), ("odd_w_in", 5), ("odd_w_iq", 4), ("odd_gate", 6),
          ("odd_w_qb", 8), ("odd_w_uk", 16), ("odd_w_uv", 8), ("odd_w_out", 8), ("w_in_2", 20),
          ("gates", 16), ("mix", 16), ("w_o_2", 8), ("mlp", 160))
GROUP0 = {}
_at = 0
for _name, _n in GROUPS:
    GROUP0[_name] = _at
    _at += _n


class Steps:

    def __init__(self, sem, names, first=0):
        self.sem = sem
        self.first = first
        self.names = list(names)
        self.n = len(self.names)
        self.index = {name: i for i, name in enumerate(self.names)}
        assert len(self.index) == self.n

    def at(self, name, r=0):
        return r * self.n + (self.index[name] + 1 + self.first)

    def done(self, r):
        return r * self.n + self.first


def four1(v):
    return v.rearrange("p (n i) -> p n i", n=4)


def flat(v):
    return v.rearrange("p d c h -> p (d c h)")


NORMS = ("even_norm", "odd_norm", "final_norm", "g_mix_2", "g_mlp_2", "g_final_2")
SPLIT_ROUND = (0, 1, None, 2, 3, 4)
XB = (0, 8, 16, 24, 32, 64)
KUS = {"even_w_in": 4, "even_w_pw": 2, "even_w_out": 4, "odd_w_in": 4, "odd_gate": 4, "odd_w_iq": 1, "odd_w_qb": 1,
       "odd_w_out": 4, "w_in_2": 4, "w_o_2": 4, "mlp": 4}
A_FREE = (0, UNIT0["even_w_out"], None, UNIT0["odd_w_out"], UNIT0["mlp"])


def build(nc, t, out):
    ctx = ExitStack()
    with ctx:
        def sb(name, shape, dt=F32):
            return ctx.enter_context(nc.sbuf_tensor(name, shape, dt))

        def sem(name):
            return ctx.enter_context(nc.semaphore(name))

        opened = []

        def steps(name, names):
            return Steps(sem(name), names)

        def rounds(name, names):
            opened.append(Steps(sem(name), names, first=1))
            return opened[-1]

        raw = sb("raw", [P, SLOTS, UK * UN])
        w_hi = sb("w_hi", [P, SLOTS, UK * UN], F32R)
        w_lo = sb("w_lo", [P, SLOTS, UK * UN], F32R)
        x = sb("x", [P, DC, T])
        a = sb("a", [P, DC, 2, T], F32R)
        b = sb("b", [P, DC, 2, T], F32R)
        z = sb("z", [P, ZB, T])
        scr = sb("scr", [P, 4, 512])
        rstd = sb("rstd", [P, T])
        vec = sb("vec", [P, N_PACKS * P])
        ident = sb("ident", [P, P])
        ones = sb("ones", [P, P])
        eps = sb("eps", [P, 1])
        one = sb("one", [P, 1])
        tri = sb("tri", [P, 4, P])
        causal = sb("causal", [P, TT, T], BF16)
        dmask = sb("dmask", [P, 4, P], BF16)
        stat = sb("stat", [P, 64])
        dsc = sb("dsc", [P, 8, 2, TT, HN])
        opening = sb("opening", [P, 20])
        iw = sb("iw", [P, TT, IH])
        own5 = sb("own5", [P, 5, T])
        ckvn, ckvt, ikt = own5[:, 0:2, :], own5[:, 2:4, :], own5[:, 4, :]

        lmask = own5[:, 0:4, :].rearrange("p a b -> p (a b)").bitcast(BF16)[:, 0:LEVELS * 2 * P].rearrange(
            "p (l d i) -> p l d i", l=LEVELS, d=2)
        scw = z[:, 50:52, :].rearrange("p a b -> p (a b)")

        lin_ps = ctx.enter_context(nc.psum_tensor("lin_ps", [P, 4, 512], F32))
        ps = ctx.enter_context(nc.psum_tensor("ps", [P, 4, 512], F32))

        raw_in = [sem(f"raw_in{s}") for s in range(SLOTS)]
        hi_done = sem("hi_done")
        lo_done = sem("lo_done")
        unit_used = sem("unit_used")
        part_done = sem("part_done")
        group_free = sem("group_free")
        x_done = sem("x_done")
        consts_in = sem("consts_in")
        x_in = sem("x_in")
        small_in = sem("small_in")
        table_in = sem("table_in")
        out_done = sem("out_done")

        bld = sem("bld")
        tp_pe = sem("tp_pe")
        tp_ev = sem("tp_ev")

        nr_act = steps("nr_act", [f"sq{s}" for s in range(8)] + ["root"])
        nr_pe = steps("nr_pe", [f"sum{s}" for s in range(8)])
        nr_rs = steps("nr_rs", ["rstd"])
        nr_n = steps("nr_n", [f"{s}" for s in range(8)])
        nr_hi = steps("nr_hi", [f"{s}" for s in range(8)])
        nr_lo = steps("nr_lo", [f"{s}" for s in range(8)])

        cv_act = steps("cv_act", ["sig0", "sig1"])
        cv_dve = steps("cv_dve", ["glu0", "glu1"] + [f"tap{k}{y}" for k in range(TAPS) for y in range(2)])
        ln_act = steps("ln_act", [f"sq{s}" for s in range(4)] + ["root"] + [y for s in range(4) for y in (f"silu{s}a", f"silu{s}b")]
                       + [f"hi{s}" for s in range(4)] + ["agate", "bgate"])
        ln_pe = steps("ln_pe", ["mean"] + [f"var{s}" for s in range(4)])
        ln_dve = steps("ln_dve", [f"c{s}" for s in range(4)] + ["rstd"] + [f"n{s}" for s in range(4)] + [f"lo{s}" for s in range(4)])
        at_pe = [steps(f"at_pe{w}", ["vt", "s", "pt", "o"]) for w in range(2)]
        at_dve = [rounds(f"at_dve{w}", ["vtok", "mask", "max", "neg", "rsum", "n0", "n1", "ptc", "o", "hi", "lo"]) for w in range(2)]
        at_act = [steps(f"at_act{w}", ["qs", "vs", "p0", "p1"]) for w in range(2)]
        pw_dve = steps("pw_dve", ["g0", "g1", "hi", "lo"])

        od_pe = steps("od_pe", ["ik", "cqs", "kvs", "kvt", "ikt"])
        od_act = steps("od_act", ["cqsq", "kvsq", "cqroot", "kvroot", "cqhi", "ikroot", "ogate"])
        od_dve = steps("od_dve", ["cqr", "cq0", "cq1", "cq2", "cq3", "cqlo", "kvr", "kv0", "kv1", "bn0", "bn1", "ag0", "ag1",
                                  "ikr", "ikn0", "ikn1", "ikn2", "ikn3", "kvt", "ikt", "iw", "zero"])
        ix_act = rounds("ix_act", ["stage", "relu"])
        ix_pe = rounds("ix_pe", ["idx"])
        ix_dve = rounds("ix_dve", ["s0", "s1", "s2", "s3"])
        tk_dve = steps("tk_dve", ["fill"] + [f"{y}{r}{q}" for r in range(8) for y in ("max", "rep") for q in range(2)] + ["sel", "am"])
        qb_dve = steps("qb_dve", ["hi", "lo"])
        da_act = [steps(f"da_act{w}", ["stage", "p0", "p1", "ohi"]) for w in range(2)]
        da_pe = [rounds(f"da_pe{w}", ["s", "pt", "o"]) for w in range(2)]
        da_dve = [rounds(f"da_dve{w}", ["mask", "max", "neg", "rsum", "n0", "n1", "ptc", "olo"]) for w in range(2)]
        uv_dve = steps("uv_dve", ["gate", "hi", "lo"])

        sc_pe = steps("sc_pe", ["scal", "cum"])
        sc_act = steps("sc_act", ["b0", "b1", "e", "ln", "ea", "eg", "er"])
        sc_dve = steps("sc_dve", ["a0", "a1", "neg", "abs", "pos", "sp", "nea", "g0", "g1", "gc", "rem", "ne"])
        fo_act = steps("fo_act", ["stage", "ab", "hi"])
        fo_pe = rounds("fo_pe", ["ab", "o"])
        fo_dve = rounds("fo_dve", ["lo"])
        dn_dve = [rounds(f"dn_dve{w}", [f"cv{y}{k}" for k in range(NT) for y in range(3)]
                         + ["rn", "qn", "kn", "gb", "dsub", "dmin", "mt1", "mt2", "qk", "t0", "u0", "mm0"]
                         + [y for l in range(LEVELS - 1) for y in (f"mm{l + 1}", f"t{l + 1}", f"u{l + 1}")]
                         + [f"u{LEVELS}", "vn1a", "vn1b", "vka", "vkb", "r2a", "r2b", "vn2a", "vn2b", "o", "orn",
                            "on0", "on1", "ot", "hi", "lo"]) for w in range(2)]
        dn_act = [rounds(f"dn_act{w}", ["sl0", "sl1", "sl2", "sq", "root", "tok", "dexp"] + [f"x{l}" for l in range(LEVELS)]
                         + ["s", "qs0", "qs1", "os0", "os1", "oroot", "sz"]) for w in range(2)]
        dn_pe = [steps(f"dn_pe{w}", ["l2", "tok", "gc", "gram"] + [y for l in range(LEVELS) for y in (f"x{l}", f"tu{l}")]
                       + ["y1", "s", "ks", "qs", "y2", "o", "ot"]) for w in range(2)]
        mx_act = steps("mx_act", ["siga", "sigb", "sigc", "sigd"])
        mx_dve = steps("mx_dve", ["dng", "frg", "sum", "hi", "lo"])
        ml_dve = rounds("ml_dve", ["sq", "hi", "lo"])
        gate_half = sem("gate_half")
        sw_in = sem("sw_in")
        fin_pe = sem("fin_pe")
        fin_dve = sem("fin_dve")

        e_q, e_v, e_vt = ([z[:, 8 * w + n, :] for w in range(2)] for n in range(3))
        e_s, e_pt = ([z[:, 8 * w + n:8 * w + n + 2, :] for w in range(2)] for n in (3, 5))
        o_q = [scr[:, w, :] for w in range(2)]
        o_s, o_pt = ([z[:, 4 * w + n:4 * w + n + 2, :] for w in range(2)] for n in (48, 50))
        score = z[:, 24:26, :]
        work = z[:, 26:28, :]
        relu = z[:, 28:32, :]
        iq_st = z[:, 32, :]
        small = z[:, 36:41, :]
        small_w = small.rearrange("p a b -> p (a b)")
        addm = dmask[:].rearrange("p a b -> p (a b)").rearrange("p (q k) -> p q k", q=TT)
        ikn = z[:, 33, :]
        def four(v):
            return v.rearrange("p a (c i) -> p (a c) i", c=2)

        class Way:

            def __init__(self, w, two):
                self.w = w
                self.x_ps, self.y_ps = ps[:, 2 * w, :], ps[:, 2 * w + 1, :]
                self.qk_feat = two[0]
                self.tok = four(two[1])
                self.m = self.v_new = four(two[2])
                self.qk = four(two[3])
                self.t = self.gate = self.v_dec = four(two[4])
                self.u = four(two[5])
                self.x = self.decay = four(two[6])
                self.sq = self.root = two[6]
                self.mm = self.r = four(two[7])
                self.v_feat = two[7][:, 0, :]
                self.norm = stat[:, 32 + 8 * w:40 + 8 * w]

        ways = [Way(0, [z[:, 40 + 2 * n:42 + 2 * n, :] for n in range(8)]),
                Way(1, [z[:, 32 + 2 * n:34 + 2 * n, :] for n in range(4)]
                    + [scr[:, n, :].rearrange("p (a b) -> p a b", a=2) for n in range(4)])]
        BETA, GG, GC, EG, REM, ER, NEG, AA = range(8)
        dtb = sb("dtb", [P, 2, 16])

        pk = z[:, 32:35, :].rearrange("p a b -> p (a b)")
        consts = [(tri[:], t["c_tri"]), (causal[:], t["c_causal"].bitcast(BF16))]

        def pack(name, src, c0=0, w=P):
            r, done, rows = ROWS[name], 0, src.shape[0]
            while done < rows:
                k, at = divmod(r + done, P)
                n = min(rows - done, P - at)
                consts.append((pk[at:at + n, k * P + c0:k * P + c0 + w], src[done:done + n, :]))
                done += n

        for name in ("even_norm", "odd_norm", "final_norm", "g_mix_2", "g_mlp_2", "g_final_2", "even_b_glu", "even_b_dw",
                     "even_conv_ln_g", "even_conv_ln_b", "even_b_pw", "even_w_dw", "odd_q_norm", "odd_kv_norm",
                     "g_dn_head_2", "conv_w_2"):
            v = t[name]
            pack(name, v.rearrange("(c p) -> c p", p=P) if len(v.shape) == 1 else v.rearrange("k (c p) -> (k c) p", p=P))
        for name, src in (("ik_g", "odd_ik_ln_g"), ("ik_b", "odd_ik_ln_b")):
            for c0 in (0, ID):
                pack(name, t[src].rearrange("(a p) -> a p", a=1), c0, ID)
        N_CONST = len(consts)

        block = ctx.enter_context(nc.Block())

        def units(v3):
            return v3.rearrange("p (k n) -> p k n", k=UK)

        @block.sync
        def _(sp):
            def load(u, slot, src):
                if not (isinstance(u, int) and u < SLOTS):
                    sp.wait_ge(lo_done, u - SLOTS + 1)
                sp.dma_start(units(raw[:, slot]), src).then_inc(raw_in[slot], 16)

            def stream(name, u0, groups, kus, col0=0, row0=0, per=2):
                v = t[name].rearrange("(k p) n -> p k n", p=P)

                def turn(g0, base):
                    col = g0 * UN if isinstance(g0, int) else sp.snap(g0 * UN)
                    for g in range(per):
                        for q in range(kus):
                            j = g * kus + q
                            k0 = row0 + q * UK
                            load(base + j, (u0 + j) % SLOTS,
                                 v[:, k0:k0 + UK, bass.ds(col + (col0 + g * UN), UN)])

                turn(0, u0)
                if groups > per:
                    with sp.Fori(1, groups // per) as i:
                        turn(i * per, i * (per * kus) + u0)

            stream("even_w_in", UNIT0["even_w_in"], 28, 4)
            small_cols = t["odd_w_in"].rearrange("(k p) n -> p k n", p=P)[:, :, QL + KVL:QL + KVL + ID + IH]
            stream("even_w_pw", UNIT0["even_w_pw"], 4, 2, per=4)
            stream("even_w_out", UNIT0["even_w_out"], 8, 4)
            for w in range(2):
                sp.wait_ge(at_dve[w].sem, at_dve[w].at("lo", HE // 2 - 1))
            sp.dma_start(small_w.rearrange("p (k n) -> p k n", k=DC), small_cols).then_inc(sw_in, 16)
            stream("odd_w_in", UNIT0["odd_w_in"], 3, 4, per=3)
            gate0 = QL + KVL + ID + IH
            stream("odd_w_in", UNIT0["odd_w_in"] + 12, 2, 4, col0=gate0)
            stream("odd_w_iq", UNIT0["odd_w_iq"], 4, 1, per=4)
            stream("odd_w_in", UNIT0["odd_gate"], 6, 4, col0=gate0 + 2 * UN)
            stream("odd_w_qb", UNIT0["odd_w_qb"], 8, 1, per=4)
            uk = t["odd_w_uk"].rearrange("h d c -> d h c")
            uv = t["odd_w_uv"].rearrange("h (k c) d -> c (h k) d", c=P)
            for n in range(4):
                load(UNIT0["odd_w_uk"] + n, n, uk[:, 4 * n:4 * n + 4, :])
            for n in range(4):
                u = UNIT0["odd_w_uv"] + n
                sp.wait_ge(lo_done, u - SLOTS + 1)
                sp.dma_start(raw[:, n].rearrange("p (h d) -> p h d", h=8), uv[:, 8 * n:8 * n + 8, :]).then_inc(raw_in[n], 16)
            stream("odd_w_out", UNIT0["odd_w_out"], 8, 4)
            for w in range(2):
                sp.wait_ge(da_dve[w].sem, da_dve[w].at("olo", HO // 2 - 1))
            sp.dma_start(lmask, t["c_lmask"].bitcast(BF16)).then_inc(table_in, 16)
            sp.dma_start(dmask[:], t["c_dmask"].bitcast(BF16)).then_inc(table_in, 16)
            sp.dma_start(z[:, Z_DFT:Z_DFT + 5, :], t["c_dft"]).then_inc(table_in, 16)
            sp.dma_start(scw.rearrange("p (k n) -> p k n", k=DC),
                         t["w_in_2"].rearrange("(k p) n -> p k n", p=P)[:, :, 5120:5152]).then_inc(table_in, 16)
            stream("w_in_2", UNIT0["w_in_2"], 4, 4, col0=4096)
            stream("w_in_2", UNIT0["w_in_2"] + 16, 16, 4)
            u0 = UNIT0["gates"]
            gates = t["w_in_2"].rearrange("(k p) n -> p k n", p=P)
            with sp.Fori(0, 4) as i:
                col = sp.snap(i * (2 * UN))
                for n, col0 in enumerate((0, D, UN, D + UN)):
                    for q in range(4):
                        load(i * 16 + (u0 + 4 * n + q), q, gates[:, q * UK:(q + 1) * UK, bass.ds(col + (5152 + col0), UN)])
            u0 = UNIT0["mix"]
            dn_up = t["w_dn_up_2"].rearrange("(k p) n -> p k n", p=P)
            four_up = t["w_fourier_2"].rearrange("(k p) n -> p k n", p=P)
            with sp.Fori(1, 9) as g:
                for n, (v, q) in enumerate(((dn_up, 0), (dn_up, 1), (four_up, 0), (four_up, 1))):
                    load(g * 4 + (u0 - 4 + n), n, v[:, q * UK:(q + 1) * UK, bass.ds(g * UN - UN, UN)])
            stream("w_o_2", UNIT0["w_o_2"], 8, 4)
            for ph in range(4):
                stream("w_mlp_up_2", UNIT0["mlp"] + 64 * ph, 8, 4, col0=ph * D)
                stream("w_mlp_down_2", UNIT0["mlp"] + 64 * ph + 32, 8, 4, row0=ph * DC)
            ov = out.rearrange("(q p) (s n) -> p s q n", p=P, n=T)
            for s in range(8):
                sp.wait_ge(fin_dve, s + 1)
                sp.dma_start(ov[:, s], z[:, 16 + 2 * s:18 + 2 * s, :]).then_inc(out_done, 16)
            sp.wait_ge(out_done, 16 * 8)

        @block.gpsimd
        def _(pool):
            def lo(u, slot, first=False):
                pool.wait_ge(hi_done, u + 1)
                if not first:
                    pool.wait_ge(unit_used, u - SLOTS + 1)
                nc.gpsimd.tensor_tensor(w_lo[:, slot], raw[:, slot], w_hi[:, slot].bitcast(F32),
                                        ALU.subtract).then_inc(lo_done, 1)

            for n, steps_ in enumerate(opened):
                nc.gpsimd.memset(opening[:, n:n + 1], 0.0).then_inc(steps_.sem, 1)
            n_units = UNITS
            for u in range(SLOTS):
                lo(u, u, first=True)
            with pool.Fori(1, n_units // SLOTS) as i:
                for s in range(SLOTS):
                    lo(i * SLOTS + s, s)

        @block.scalar
        def _(act):
            act.dma_start(ident[:], t["c_ident"]).then_inc(x_in, 16)
            for tt in range(TT):
                act.dma_start(z[:, 8 * tt:8 * tt + 8, :].rearrange("p a b -> p (a b)"),
                              t["x"][tt * P:(tt + 1) * P, :]).then_inc(x_in, 16)
            for dst, src in consts:
                act.dma_start(dst, src).then_inc(consts_in, 16)
            for k, names in enumerate((("dt_bias_fwd_2", "dt_bias_bwd_2"), ("a_log_fwd_2", "a_log_bwd_2"))):
                for d, name in enumerate(names):
                    act.dma_start(dtb[:, k, d * HN:(d + 1) * HN],
                                  t[name].rearrange("(a n) -> a n", a=1).broadcast_to([P, HN])).then_inc(small_in, 16)

            def hi(u, slot, first=False):
                act.wait_ge(raw_in[slot], 16 * (u // SLOTS + 1))
                if not first:
                    act.wait_ge(unit_used, u - SLOTS + 1)
                nc.scalar.activation(w_hi[:, slot], raw[:, slot], ACT.Copy).then_inc(hi_done, 1)

            def his(u0, n):
                s0 = u0 % SLOTS
                assert n % SLOTS == 0
                with act.Fori(0, n // SLOTS) as i:
                    for s in range(SLOTS):
                        slot = (s0 + s) % SLOTS
                        act.wait_ge(raw_in[slot], i * 16 + 16 * ((u0 + s) // SLOTS + 1))
                        act.wait_ge(unit_used, i * SLOTS + (u0 + s - SLOTS + 1))
                        nc.scalar.activation(w_hi[:, slot], raw[:, slot], ACT.Copy).then_inc(hi_done, 1)

            def ahead(u0):
                for s in range(SLOTS):
                    hi(u0 + s, (u0 + s) % SLOTS, first=u0 == 0)

            def norm_squares(r, u0=None):
                for s in range(8):
                    if u0 and s == 6:
                        for n in range(3):
                            hi(u0 + n, (u0 + n) % SLOTS)
                    act.wait_ge(x_done, XB[r] + s + 1)
                    if s >= 2:
                        act.wait_ge(nr_pe.sem, nr_pe.at(f"sum{s - 2}", r))
                    nc.scalar.activation(scr[:, s % 2].rearrange("p (k n) -> p k n", k=2), x[:, 2 * s:2 * s + 2, :],
                                         ACT.Square).then_inc(nr_act.sem, 1)
                if u0:
                    hi(u0 + 3, (u0 + 3) % SLOTS)
                act.wait_ge(nr_pe.sem, nr_pe.at("sum7", r))
                act.wait_ge(bld, 3)
                nc.scalar.activation(scr[:, 0, 0:T], ps[:, 0, 0:T], ACT.Sqrt, bias=eps[:, 0:1],
                                     scale=1.0 / D).then_inc(nr_act.sem, 1)

            def norm_hi(r):
                for s in range(8):
                    act.wait_ge(nr_n.sem, nr_n.at(f"{s}", SPLIT_ROUND[r]))
                    if s == 0 and r:
                        act.wait_ge(unit_used, A_FREE[r])
                    nc.scalar.activation(a[:, 2 * s:2 * s + 2, 0, :],
                                         scr[:, 2 + s % 2].rearrange("p (k n) -> p k n", k=2),
                                         ACT.Copy).then_inc(nr_hi.sem, 1)

            ahead(0)
            norm_squares(0)
            norm_hi(0)
            his(4, 28)
            with act.Fori(0, 4) as i:
                for n in range(16):
                    slot = n % SLOTS
                    act.wait_ge(raw_in[slot], i * 64 + 16 * ((32 + n) // SLOTS + 1))
                    act.wait_ge(unit_used, i * 16 + (32 + n - SLOTS + 1))
                    nc.scalar.activation(w_hi[:, slot], raw[:, slot], ACT.Copy).then_inc(hi_done, 1)
                    if n == 3:
                        act.wait_ge(group_free, 8)
                        for y in range(2):
                            gate = z[:, bass.ds(i * 2 + (Z_AGT + y), 1), :]
                            nc.scalar.activation(gate, gate, ACT.Sigmoid,
                                                 bias=vec[:, bass.ds(i * 2 + (ROWS["even_b_glu"] + 8 + y), 1)]).then_inc(cv_act.sem, 1)
            for n in range(4):
                hi(96 + n, n)
            for s in range(4):
                act.wait_ge(ln_dve.sem, ln_dve.at(f"c{s}"))
                if s >= 2:
                    act.wait_ge(ln_pe.sem, ln_pe.at(f"var{s - 2}"))
                nc.scalar.activation(scr[:, s % 2].rearrange("p (k n) -> p k n", k=2),
                                     z[:, Z_AGT + 2 * s:Z_AGT + 2 * s + 2, :], ACT.Square).then_inc(ln_act.sem, 1)
                if s == 1:
                    for n in range(4):
                        hi(100 + n, n)
            act.wait_ge(ln_pe.sem, ln_pe.at("var3"))
            nc.scalar.activation(scr[:, 2, 0:T], ps[:, 1, 0:T], ACT.Sqrt, bias=eps[:, 0:1],
                                 scale=1.0 / CW).then_inc(ln_act.sem, 1)
            for s in range(4):
                act.wait_ge(ln_dve.sem, ln_dve.at(f"n{s}"))
                for k in range(2):
                    c = 2 * s + k
                    nc.scalar.activation(z[:, Z_AGT + c, :], z[:, Z_AGT + c, :], ACT.Silu,
                                         bias=vec[:, ROWS["even_conv_ln_b"] + c:ROWS["even_conv_ln_b"] + c + 1],
                                         scale=vec[:, ROWS["even_conv_ln_g"] + c:ROWS["even_conv_ln_g"] + c + 1]
                                         ).then_inc(ln_act.sem, 1)
            for n in range(4):
                hi(104 + n, n)
            for s in range(4):
                act.wait_ge(ln_act.sem, ln_act.at(f"silu{s}b"))
                nc.scalar.activation(b[:, 8 + 2 * s:8 + 2 * s + 2, 0, :], z[:, Z_AGT + 2 * s:Z_AGT + 2 * s + 2, :],
                                     ACT.Copy).then_inc(ln_act.sem, 1)
            nc.scalar.activation(z[:, Z_AGATE:Z_AGATE + 8, :], z[:, Z_AGATE:Z_AGATE + 8, :],
                                 ACT.Silu).then_inc(ln_act.sem, 1)
            for n in range(4):
                hi(108 + n, n)
            his(UNIT0["even_w_pw"], 8)
            act.wait_ge(group_free, 28)
            nc.scalar.activation(z[:, Z_BGATE:Z_BGATE + 8, :], z[:, Z_BGATE:Z_BGATE + 8, :],
                                 ACT.Silu).then_inc(ln_act.sem, 1)
            ahead(UNIT0["even_w_out"])
            act.wait_ge(ln_dve.sem, ln_dve.at("lo3"))
            with act.Fori(0, HE // 2) as i:
                for w in range(2):
                    act.wait_ge(at_dve[w].sem, at_dve[w].done(i))
                    nc.scalar.mul(e_q[w], z[:, bass.ds(i * 2 + (Z_Q + w), 1), :].rearrange("p a n -> p (a n)"),
                                  DH ** -0.5).then_inc(at_act[w].sem, 1)
                    nc.scalar.copy(e_v[w], z[:, bass.ds(i * 2 + (Z_V + w), 1), :].rearrange("p a n -> p (a n)")).then_inc(at_act[w].sem, 1)
                for w in range(2):
                    act.wait_ge(at_dve[w].sem, at_dve[w].at("neg", i))
                    for q in range(TT):
                        nc.scalar.activation(e_s[w][:, q, :], e_s[w][:, q, :], ACT.Exp, bias=stat[:, 8 * w + 2 + q:8 * w + 3 + q],
                                             accum_out=stat[:, 8 * w + 4 + q:8 * w + 5 + q]).then_inc(at_act[w].sem, 1)
            his(UNIT0["even_w_out"] + 4, 28)
            norm_squares(1, UNIT0["odd_w_in"])
            norm_hi(1)
            his(UNIT0["odd_w_in"] + 4, 12)
            act.wait_ge(group_free, GROUP0["odd_w_in"] + 3)
            nc.scalar.activation(scr[:, 0:2, :].rearrange("p a (k n) -> p (a k) n", k=2), z[:, Z_CQ:Z_CQ + 4, :],
                                 ACT.Square).then_inc(od_act.sem, 1)
            nc.scalar.activation(scr[:, 3, :].rearrange("p (k n) -> p k n", k=2), z[:, Z_CKV:Z_CKV + 2, :],
                                 ACT.Square).then_inc(od_act.sem, 1)
            his(UNIT0["odd_w_in"] + 16, 4)
            act.wait_ge(od_pe.sem, od_pe.at("cqs"))
            nc.scalar.activation(scr[:, 2, 0:T], ps[:, 0, 0:T], ACT.Sqrt, bias=eps[:, 0:1],
                                 scale=1.0 / QL).then_inc(od_act.sem, 1)
            act.wait_ge(od_pe.sem, od_pe.at("kvs"))
            nc.scalar.activation(scr[:, 3, 0:T], ps[:, 1, 0:T], ACT.Sqrt, bias=eps[:, 0:1],
                                 scale=1.0 / KVL).then_inc(od_act.sem, 1)
            act.wait_ge(od_dve.sem, od_dve.at("cq3"))
            nc.scalar.activation(b[:, 0:4, 0, :], z[:, Z_CQ:Z_CQ + 4, :], ACT.Copy).then_inc(od_act.sem, 1)
            act.wait_ge(od_dve.sem, od_dve.at("ag1"))
            nc.scalar.activation(stat[:, 20:22], stat[:, 16:20].rearrange("p (q s) -> p s q", s=2)[:, 1, :], ACT.Sqrt,
                                 bias=eps[:, 0:1]).then_inc(od_act.sem, 1)
            his(UNIT0["odd_w_iq"], 4)
            for n in range(2):
                hi(UNIT0["odd_gate"] + n, n)
            with act.Fori(0, 2) as i:
                for k in range(4):
                    c = i * 4 + k
                    act.wait_ge(group_free, GROUP0["odd_w_iq"] + 4)
                    act.wait_ge(ix_pe.sem, ix_pe.done(c))
                    nc.scalar.copy(iq_st, z[:, bass.ds(i * 4 + (Z_IQ + k), 1), :].rearrange("p a n -> p (a n)")).then_inc(ix_act.sem, 1)
                    act.wait_ge(ix_pe.sem, ix_pe.at("idx", c))
                    act.wait_ge(ix_dve.sem, ix_dve.done(c))
                    nc.scalar.activation(relu.rearrange("p a n -> p (a n)"), ps[:, 0:2, :].rearrange("p a n -> p (a n)"),
                                         ACT.Relu).then_inc(ix_act.sem, 1)
                    for n in (2 * k + 2, 2 * k + 3):
                        slot = n % SLOTS
                        act.wait_ge(raw_in[slot], i * 32 + 16 * ((UNIT0["odd_gate"] + n) // SLOTS + 1))
                        act.wait_ge(unit_used, i * 8 + (UNIT0["odd_gate"] + n - SLOTS + 1))
                        nc.scalar.activation(w_hi[:, slot], raw[:, slot], ACT.Copy).then_inc(hi_done, 1)
            for n in range(18, 24):
                hi(UNIT0["odd_gate"] + n, n % SLOTS)
            his(UNIT0["odd_w_qb"], 8)
            act.wait_ge(group_free, GROUP0["odd_gate"] + 6)
            nc.scalar.activation(z[:, Z_OGATE:Z_OGATE + 16, :], z[:, Z_OGATE:Z_OGATE + 16, :],
                                 ACT.Silu).then_inc(od_act.sem, 1)
            his(UNIT0["odd_w_uk"], 4)
            ahead(UNIT0["odd_w_uv"])
            for half in range(2):
                with act.Fori(0, 4) as i:
                    for w in range(2):
                        r = i + 4 * half
                        if half == 0:
                            act.wait_ge(group_free, GROUP0["odd_w_uk"] + 16)
                        act.wait_ge(da_pe[w].sem, da_pe[w].done(r))
                        nc.scalar.mul(o_q[w].rearrange("p (k n) -> p k n", k=2), z[:, bass.ds(i * 4 + (Z_QLAT + 2 * w + 16 * half), 2), :],
                                      DH ** -0.5).then_inc(da_act[w].sem, 1)
                    for w in range(2):
                        act.wait_ge(da_dve[w].sem, da_dve[w].at("neg", r))
                        for q in range(TT):
                            nc.scalar.activation(o_s[w][:, q, :], o_s[w][:, q, :], ACT.Exp, bias=stat[:, 8 * w + 2 + q:8 * w + 3 + q],
                                                 accum_out=stat[:, 8 * w + 4 + q:8 * w + 5 + q]).then_inc(da_act[w].sem, 1)
                    for w in range(2):
                        act.wait_ge(da_pe[w].sem, da_pe[w].at("o", r))
                        if half == 1:
                            act.wait_ge(unit_used, UNIT0["odd_w_uv"] + 2)
                        else:
                            act.wait_ge(unit_used, UNIT0["odd_w_uk"] + 4)
                        nc.scalar.activation(a[:, bass.ds(i * 4 + 2 * w, 2), 0, :], ps[:, 2 * w, :].rearrange("p (k n) -> p k n", k=2),
                                             ACT.Copy).then_inc(da_act[w].sem, 1)
            his(UNIT0["odd_w_out"], 32)
            norm_squares(2, UNIT0["w_in_2"])
            norm_squares(3)
            norm_hi(3)
            his(UNIT0["w_in_2"] + 4, 12)
            ahead(UNIT0["w_in_2"] + 16)
            act.wait_ge(sc_pe.sem, sc_pe.at("scal"))
            act.wait_ge(sc_dve.sem, sc_dve.at("a1"))
            for c in range(TT):
                nc.scalar.activation(dsc[:, BETA, :, c, :],
                                     ps[:, 0, c * 32:c * 32 + 16].rearrange("p (d h) -> p d h", d=2),
                                     ACT.Sigmoid).then_inc(sc_act.sem, 1)
            act.wait_ge(sc_dve.sem, sc_dve.at("abs"))
            nc.scalar.activation(stat[:, 0:32], stat[:, 0:32], ACT.Exp, scale=-1.0).then_inc(sc_act.sem, 1)
            act.wait_ge(sc_act.sem, sc_act.at("e"))
            nc.scalar.activation(stat[:, 0:32], stat[:, 0:32], ACT.Ln, bias=one[:, 0:1]).then_inc(sc_act.sem, 1)
            act.wait_ge(small_in, 16 * 4)
            nc.scalar.activation(dtb[:, 1, :], dtb[:, 1, :], ACT.Exp).then_inc(sc_act.sem, 1)
            for n in (20, 21):
                hi(UNIT0["w_in_2"] + n, n % SLOTS)
            act.wait_ge(sc_dve.sem, sc_dve.at("rem"))
            nc.scalar.activation(flat(dsc[:, EG]), flat(dsc[:, GC]), ACT.Exp).then_inc(sc_act.sem, 1)
            nc.scalar.activation(flat(dsc[:, ER]), flat(dsc[:, REM]), ACT.Exp).then_inc(sc_act.sem, 1)
            def fourier(g, units):
                act.wait_ge(group_free, GROUP0["w_in_2"] + 4)
                act.wait_ge(table_in, 64)
                act.wait_ge(fo_pe.sem, fo_pe.done(g))
                nc.scalar.copy(z[:, 46, :], z[:, bass.ds(g + Z_F, 1), :].rearrange("p a n -> p (a n)")).then_inc(fo_act.sem, 1)
                act.wait_ge(fo_pe.sem, fo_pe.at("ab", g))
                nc.scalar.activation(z[:, 48:50, :], ps[:, 2, :].rearrange("p (a n) -> p a n", a=2), ACT.Copy).then_inc(fo_act.sem, 1)
                for n in range(max(units, 3)):
                    if n == 2:
                        act.wait_ge(fo_pe.sem, fo_pe.at("o", g))
                        nc.scalar.activation(b[:, bass.ds(g + 8, 1), 0, :].rearrange("p a n -> p (a n)"), ps[:, 3, 0:T],
                                             ACT.Copy).then_inc(fo_act.sem, 1)
                    if n >= units:
                        continue
                    u, slot = UNIT0["w_in_2"] + 22 + n, (n + 2) % SLOTS
                    act.wait_ge(raw_in[slot], g * 32 + 16 * (u // SLOTS + 1))
                    act.wait_ge(unit_used, g * 8 + (u - SLOTS + 1))
                    nc.scalar.activation(w_hi[:, slot], raw[:, slot], ACT.Copy).then_inc(hi_done, 1)

            with act.Fori(0, FG - 1) as g:
                fourier(g, 8)
            fourier(FG - 1, 2)
            u0 = UNIT0["gates"]
            for n in range(2):
                hi(u0 + n, n)
            with act.Fori(0, HN // 2) as i:
                def fill(n):
                    u, slot = u0 + n + 2, (n + 2) % SLOTS
                    act.wait_ge(raw_in[slot], i * 64 + 16 * (u // SLOTS + 1))
                    act.wait_ge(unit_used, i * 16 + (u - SLOTS + 1))
                    nc.scalar.activation(w_hi[:, slot], raw[:, slot], ACT.Copy).then_inc(hi_done, 1)

                for w in ways:
                    own, dve_sem = dn_act[w.w], dn_dve[w.w]
                    for y, v in enumerate((w.qk_feat[:, 0, :], w.qk_feat[:, 1, :], w.v_feat)):
                        act.wait_ge(dve_sem.sem, dve_sem.at(f"cv{y}{NT - 1}", i))
                        nc.scalar.activation(v, v, ACT.Silu).then_inc(own.sem, 1)
                    act.wait_ge(own.sem, own.at("sl1", i))
                    nc.scalar.activation(w.sq, w.qk_feat, ACT.Square).then_inc(own.sem, 1)
                    fill(w.w)
                fill(2)
                for w in ways:
                    own, pe_sem = dn_act[w.w], dn_pe[w.w]
                    act.wait_ge(pe_sem.sem, pe_sem.at("l2", i))
                    nc.scalar.activation(w.root, w.x_ps.rearrange("p (a n) -> p a n", a=2), ACT.Sqrt,
                                         bias=eps[:, 0:1]).then_inc(own.sem, 1)
                fill(3)
                for w in ways:
                    own, pe_sem = dn_act[w.w], dn_pe[w.w]
                    act.wait_ge(pe_sem.sem, pe_sem.at("tok", i))
                    nc.scalar.activation(w.tok, four1(w.y_ps), ACT.Copy).then_inc(own.sem, 1)
                fill(4)
                for w in ways:
                    own, dve_sem = dn_act[w.w], dn_dve[w.w]
                    act.wait_ge(dve_sem.sem, dve_sem.at("dmin", i))
                    nc.scalar.activation(w.decay, w.decay, ACT.Exp).then_inc(own.sem, 1)
                fill(5)
                for l in range(LEVELS):
                    for w in ways:
                        own, pe_sem = dn_act[w.w], dn_pe[w.w]
                        act.wait_ge(pe_sem.sem, pe_sem.at(f"x{l}", i))
                        nc.scalar.activation(w.x, four1(w.x_ps), ACT.Copy).then_inc(own.sem, 1)
                    fill(6 + l)
                fill(13)
                for w in ways:
                    own, pe_sem = dn_act[w.w], dn_pe[w.w]
                    act.wait_ge(pe_sem.sem, pe_sem.at("s", i))
                    nc.scalar.activation(w.x[:, 0:2, :], four1(w.y_ps)[:, 0:2, :], ACT.Copy).then_inc(own.sem, 1)
                fill(14)
                for w in ways:
                    own, pe_sem = dn_act[w.w], dn_pe[w.w]
                    act.wait_ge(pe_sem.sem, pe_sem.at("qs", i))
                    for d in range(2):
                        nc.scalar.activation(w.x[:, 2 + 1 - d, :], four1(w.y_ps)[:, d, :], ACT.Copy,
                                             scale=dsc[:, EG, d, 1 - d, bass.ds(i * 2 + w.w, 1)]).then_inc(own.sem, 1)
                fill(15)
                for w in ways:
                    own, dve_sem = dn_act[w.w], dn_dve[w.w]
                    act.wait_ge(dve_sem.sem, dve_sem.at("o", i))
                    for c in range(TT):
                        nc.scalar.activation(w.v_dec[:, c, :], w.u[:, c, :], ACT.Square,
                                             accum_out=w.norm[:, c:c + 1]).then_inc(own.sem, 1)
                    act.wait_ge(own.sem, own.at("os1", i))
                    nc.scalar.activation(w.norm[:, 2:4], w.norm[:, 0:2], ACT.Sqrt, bias=eps[:, 0:1],
                                         scale=1.0 / P).then_inc(own.sem, 1)
                for w in ways:
                    nc.scalar.activation(w.x[:, 0:2, :].rearrange("p a n -> p (a n)"),
                                         z[:, bass.ds(i * 2 + (Z_DZ + w.w), 1), :].rearrange("p a n -> p (a n)"),
                                         ACT.Silu).then_inc(dn_act[w.w].sem, 1)
            act.wait_ge(group_free, GROUP0["gates"] + 16)
            for n in range(4):
                gate = z[:, 8 * n:8 * n + 8, :]
                nc.scalar.activation(gate, gate, ACT.Sigmoid).then_inc(mx_act.sem, 1)
            for n in (2, 3):
                hi(UNIT0["mix"] + n, n)
            his(UNIT0["mix"] + 4, 28)
            his(UNIT0["w_o_2"], 32)
            norm_squares(4, UNIT0["mlp"])
            norm_hi(4)
            his(UNIT0["mlp"] + 4, 252)
            norm_squares(5)

        @block.vector
        def _(dve):
            nc.vector.memset(ones[:], 1.0).then_inc(bld, 1)
            nc.vector.memset(eps[:], EPS).then_inc(bld, 1)
            nc.vector.memset(one[:], 1.0).then_inc(bld, 1)
            for s in range(8):
                dve.wait_ge(tp_pe, 1 + s)
                nc.vector.tensor_copy(x[:, 2 * s:2 * s + 2, :],
                                      ps[:, 1 + s % 3, :].rearrange("p (k n) -> p k n", k=2)).then_inc(x_done, 1)
            dve.wait_ge(tp_pe, 9)
            nc.vector.tensor_copy(vec[:, 0:4 * P], ps[:, 0, :]).then_inc(tp_ev, 1)
            nc.vector.tensor_copy(vec[:, 4 * P:N_ROWS], lin_ps[:, 0, 0:N_ROWS - 4 * P]).then_inc(tp_ev, 1)

            def norm(r, last=False):
                g0 = ROWS[NORMS[r]]
                dve.wait_ge(nr_act.sem, nr_act.at("root", r))
                dve.wait_ge(x_done, XB[r] + 8)
                dve.wait_ge(tp_ev, 2)
                nc.vector.reciprocal(rstd[:], scr[:, 0, 0:T]).then_inc(nr_rs.sem, 1)
                dve.wait_ge(nr_rs.sem, nr_rs.at("rstd", r))
                R = SPLIT_ROUND[r]
                for s in range(8):
                    pair = x[:, 2 * s:2 * s + 2, :]
                    t2 = pair if R is None else scr[:, 2 + s % 2].rearrange("p (k n) -> p k n", k=2)
                    if R is not None and s >= 2:
                        dve.wait_ge(nr_lo.sem, nr_lo.at(f"{s - 2}", R))
                    for k in range(2):
                        c = 2 * s + k
                        m = nc.vector.scalar_tensor_tensor(out=t2[:, k, :], in0=x[:, c, :], scalar=vec[:, g0 + c:g0 + c + 1],
                                                           in1=rstd[:], op0=ALU.mult, op1=ALU.mult)
                    if R is None:
                        m.then_inc(x_done, 1)
                        continue
                    m.then_inc(nr_n.sem, 1)
                    if last:
                        dve.wait_ge(nr_n.sem, nr_n.at(f"{s}", R))
                        nc.vector.tensor_copy(z[:, 2 * s:2 * s + 2, :], t2).then_inc(nr_lo.sem, 1)
                    else:
                        dve.wait_ge(nr_hi.sem, nr_hi.at(f"{s}", R))
                        nc.vector.tensor_tensor(a[:, 2 * s:2 * s + 2, 1, :], t2, a[:, 2 * s:2 * s + 2, 0, :].bitcast(F32),
                                                ALU.subtract).then_inc(nr_lo.sem, 1)

            def halves(parity):
                return lin_ps[:, 2 * parity:2 * parity + 2, :].rearrange("p m (s n) -> p m n s", s=2)

            def to_z(name, n, z0, per=2, u=0, g=0):
                kus, u0, g0 = KUS[name], UNIT0[name] + u, GROUP0[name] + g

                def turn(used, zb):
                    for k in range(per):
                        dve.wait_ge(unit_used, used + (k + 1) * kus)
                        nc.vector.tensor_reduce(z[:, bass.ds(zb + 2 * k, 2), :], halves((g0 + k) % 2), AX.X,
                                                ALU.add).then_inc(group_free, 1)
                if n <= per:
                    turn(u0, z0)
                else:
                    with dve.Fori(0, n // per) as i:
                        turn(i * (per * kus) + u0, i * (2 * per) + z0)

            def to_x(name, u=0, g=0):
                u0, g0 = UNIT0[name] + u, GROUP0[name] + g
                with dve.Fori(0, 4) as i:
                    for k in range(2):
                        dve.wait_ge(unit_used, i * 8 + (u0 + 4 * (k + 1)))
                        tmp = scr[:, 2 + k].rearrange("p (m n) -> p m n", m=2)
                        nc.vector.tensor_reduce(tmp, halves((g0 + k) % 2), AX.X, ALU.add).then_inc(group_free, 1)
                        dve.wait_ge(group_free, i * 2 + (g0 + k + 1))
                        xs = x[:, bass.ds(i * 4 + 2 * k, 2), :]
                        nc.vector.tensor_tensor(xs, xs, tmp, ALU.add).then_inc(x_done, 1)

            norm(0)
            to_z("even_w_in", 8, 0)

            def even_out(g):
                dve.wait_ge(unit_used, 4 * g + 4)
                nc.vector.tensor_reduce(z[:, 2 * g:2 * g + 2, :], halves(g % 2), AX.X, ALU.add).then_inc(group_free, 1)

            with dve.Fori(0, 4) as i:
                dve.wait_ge(cv_act.sem, cv_act.at("sig1", i))
                dve.wait_ge(group_free, 8)
                u = [z[:, bass.ds(i * 2 + (Z_AVAL + c), 1), :] for c in range(2)]
                y = [z[:, bass.ds(i * 2 + (Z_AGT + c), 1), :] for c in range(2)]
                per_channel = lambda row: vec[:, bass.ds(i * 2 + row, 1)]
                w = ROWS["even_w_dw"]
                for c in range(2):
                    nc.vector.scalar_tensor_tensor(out=u[c], in0=u[c], scalar=per_channel(ROWS["even_b_glu"] + c), in1=y[c],
                                                   op0=ALU.add, op1=ALU.mult).then_inc(cv_dve.sem, 1)
                for c in range(2):
                    dve.wait_ge(cv_dve.sem, cv_dve.at(f"glu{c}", i))
                    nc.vector.tensor_scalar(y[c], u[c], per_channel(w + 8 * (TAPS - 1) + c),
                                            per_channel(ROWS["even_b_dw"] + c), ALU.mult, ALU.add).then_inc(cv_dve.sem, 1)
                for k in range(1, TAPS):
                    if k in (6, 14, 21, 29):
                        n = (6, 14, 21, 29).index(k)
                        dve.wait_ge(unit_used, i * 16 + (32 + 4 * n + 4))
                        nc.vector.tensor_reduce(z[:, bass.ds(i * 8 + (16 + 2 * n), 2), :], halves(n % 2), AX.X, ALU.add).then_inc(group_free, 1)
                    for c in range(2):
                        dve.wait_ge(cv_dve.sem, cv_dve.at(f"tap{k - 1}{c}", i))
                        nc.vector.scalar_tensor_tensor(out=y[c][:, :, k:T], in0=u[c][:, :, 0:T - k],
                                                       scalar=per_channel(w + 8 * (TAPS - 1 - k) + c), in1=y[c][:, :, k:T],
                                                       op0=ALU.mult, op1=ALU.add).then_inc(cv_dve.sem, 1)
            mean = ps[:, 0, 0:T].unsqueeze(1).broadcast_to([P, 2, T])
            dve.wait_ge(ln_pe.sem, ln_pe.at("mean"))
            dve.wait_ge(cv_dve.sem, cv_dve.at(f"tap{TAPS - 1}1", 3))
            for s in range(4):
                yy = z[:, Z_AGT + 2 * s:Z_AGT + 2 * s + 2, :]
                nc.vector.scalar_tensor_tensor(out=yy, in0=mean, scalar=-1.0 / CW, in1=yy,
                                               op0=ALU.mult, op1=ALU.add).then_inc(ln_dve.sem, 1)
            even_out(24)
            dve.wait_ge(ln_act.sem, ln_act.at("root"))
            nc.vector.reciprocal(scr[:, 3, 0:T], scr[:, 2, 0:T]).then_inc(ln_dve.sem, 1)
            dve.wait_ge(ln_dve.sem, ln_dve.at("rstd"))
            for s in range(4):
                yy = z[:, Z_AGT + 2 * s:Z_AGT + 2 * s + 2, :]
                nc.vector.tensor_tensor(yy, yy, scr[:, 3, 0:T].unsqueeze(1).broadcast_to([P, 2, T]),
                                        ALU.mult).then_inc(ln_dve.sem, 1)
            even_out(25)
            for s in range(4):
                dve.wait_ge(ln_act.sem, ln_act.at(f"hi{s}"))
                nc.vector.tensor_tensor(b[:, 8 + 2 * s:8 + 2 * s + 2, 1, :], z[:, Z_AGT + 2 * s:Z_AGT + 2 * s + 2, :],
                                        b[:, 8 + 2 * s:8 + 2 * s + 2, 0, :].bitcast(F32), ALU.subtract).then_inc(ln_dve.sem, 1)
            even_out(26)
            even_out(27)
            for g in range(4):
                G = GROUP0["even_w_pw"] + g
                dve.wait_ge(unit_used, UNIT0["even_w_pw"] + 2 * g + 2)
                dve.wait_ge(ln_act.sem, ln_act.at("agate"))
                if g >= 1:
                    dve.wait_ge(pw_dve.sem, pw_dve.at("lo", g - 1))
                tmp = scr[:, 0].rearrange("p (m n) -> p m n", m=2)
                nc.vector.tensor_reduce(tmp, halves(G % 2), AX.X, ALU.add).then_inc(group_free, 1)
                dve.wait_ge(group_free, G + 1)
                for k in range(2):
                    c = 2 * g + k
                    nc.vector.scalar_tensor_tensor(out=tmp[:, k, :], in0=tmp[:, k, :],
                                                   scalar=vec[:, ROWS["even_b_pw"] + c:ROWS["even_b_pw"] + c + 1],
                                                   in1=z[:, Z_AGATE + c, :], op0=ALU.add, op1=ALU.mult).then_inc(pw_dve.sem, 1)
                dve.wait_ge(pw_dve.sem, pw_dve.at("g1", g))
                nc.vector.tensor_copy(b[:, 2 * g:2 * g + 2, 0, :], tmp).then_inc(pw_dve.sem, 1)
                dve.wait_ge(pw_dve.sem, pw_dve.at("hi", g))
                nc.vector.tensor_tensor(b[:, 2 * g:2 * g + 2, 1, :], tmp, b[:, 2 * g:2 * g + 2, 0, :].bitcast(F32),
                                        ALU.subtract).then_inc(pw_dve.sem, 1)
            with dve.Fori(0, HE // 2) as i:
                for w in range(2):
                    own, at = at_dve[w].sem, at_dve[w].at
                    dve.wait_ge(at_pe[w].sem, at_pe[w].at("vt", i))
                    nc.vector.tensor_copy(e_vt[w], ps[:, 2 * w, 0:T]).then_inc(own, 1)
                    dve.wait_ge(at_pe[w].sem, at_pe[w].at("s", i))
                    nc.vector.tensor_tensor(e_s[w], ps[:, 2 * w + 1, :].rearrange("p (q n) -> p q n", q=2), causal[:], ALU.add).then_inc(own, 1)
                    dve.wait_ge(own, at("mask", i))
                    nc.vector.tensor_reduce(stat[:, 8 * w:8 * w + 2], e_s[w], AX.X, ALU.max).then_inc(own, 1)
                    dve.wait_ge(own, at("max", i))
                    nc.vector.tensor_scalar(stat[:, 8 * w + 2:8 * w + 4], stat[:, 8 * w:8 * w + 2], -1.0, None, ALU.mult).then_inc(own, 1)
                for w in range(2):
                    own, at = at_dve[w].sem, at_dve[w].at
                    dve.wait_ge(at_act[w].sem, at_act[w].at("p1", i))
                    nc.vector.reciprocal(stat[:, 8 * w + 6:8 * w + 8], stat[:, 8 * w + 4:8 * w + 6]).then_inc(own, 1)
                    dve.wait_ge(own, at("rsum", i))
                    for q in range(TT):
                        nc.vector.tensor_scalar(e_s[w][:, q, :], e_s[w][:, q, :], stat[:, 8 * w + 6 + q:8 * w + 7 + q], None, ALU.mult).then_inc(own, 1)
                for w in range(2):
                    own, at = at_dve[w].sem, at_dve[w].at
                    dve.wait_ge(at_pe[w].sem, at_pe[w].at("pt", i))
                    nc.vector.tensor_copy(e_pt[w], ps[:, 2 * w, :].rearrange("p (q n) -> p q n", q=2)).then_inc(own, 1)
                for w in range(2):
                    own, at = at_dve[w].sem, at_dve[w].at
                    dve.wait_ge(at_pe[w].sem, at_pe[w].at("o", i))
                    tmp = scr[:, 1 + w, 0:T]
                    nc.vector.tensor_tensor(tmp, ps[:, 2 * w + 1, 0:T], z[:, bass.ds(i * 2 + (Z_BGATE + w), 1), :].rearrange("p a n -> p (a n)"),
                                            ALU.mult).then_inc(own, 1)
                    dve.wait_ge(unit_used, UNIT0["even_w_out"])
                    dve.wait_ge(own, at("o", i))
                    bh = b[:, bass.ds(i * 2 + (8 + w), 1), :, :].rearrange("p a s n -> p (a s) n")
                    nc.vector.tensor_copy(bh[:, 0, :], tmp).then_inc(own, 1)
                    dve.wait_ge(own, at("hi", i))
                    nc.vector.tensor_tensor(bh[:, 1, :], tmp, bh[:, 0, :].bitcast(F32), ALU.subtract).then_inc(own, 1)
            to_x("even_w_out")
            norm(1)
            to_z("odd_w_in", 3, Z_CQ, per=3)
            rg = lambda c: vec[:, c:c + 1]
            dve.wait_ge(od_act.sem, od_act.at("cqroot"))
            dve.wait_ge(group_free, GROUP0["odd_w_in"] + 3)
            nc.vector.reciprocal(scr[:, 2, T:2 * T], scr[:, 2, 0:T]).then_inc(od_dve.sem, 1)
            dve.wait_ge(od_dve.sem, od_dve.at("cqr"))
            for c in range(4):
                nc.vector.scalar_tensor_tensor(out=z[:, Z_CQ + c, :], in0=z[:, Z_CQ + c, :], scalar=rg(ROWS["odd_q_norm"] + c),
                                               in1=scr[:, 2, T:2 * T], op0=ALU.mult, op1=ALU.mult).then_inc(od_dve.sem, 1)
            dve.wait_ge(od_act.sem, od_act.at("cqhi"))
            nc.vector.tensor_tensor(b[:, 0:4, 1, :], z[:, Z_CQ:Z_CQ + 4, :], b[:, 0:4, 0, :].bitcast(F32),
                                    ALU.subtract).then_inc(od_dve.sem, 1)
            dve.wait_ge(od_act.sem, od_act.at("kvroot"))
            nc.vector.reciprocal(scr[:, 3, T:2 * T], scr[:, 3, 0:T]).then_inc(od_dve.sem, 1)
            dve.wait_ge(od_dve.sem, od_dve.at("kvr"))
            for c in range(2):
                nc.vector.scalar_tensor_tensor(out=ckvn[:, c, :], in0=z[:, Z_CKV + c, :], scalar=rg(ROWS["odd_kv_norm"] + c),
                                               in1=scr[:, 3, T:2 * T], op0=ALU.mult, op1=ALU.mult).then_inc(od_dve.sem, 1)
            to_z("odd_w_in", 1, Z_OGATE, per=1, u=12, g=3)
            dve.wait_ge(od_pe.sem, od_pe.at("ik"))
            for q in range(TT):
                nc.vector.bn_stats(stat[:, 24 + 6 * q:30 + 6 * q], ps[:, 3, P * q:P * q + ID]).then_inc(od_dve.sem, 1)
            for q in range(TT):
                dve.wait_ge(od_dve.sem, od_dve.at(f"bn{q}"))
                nc.vector.bn_aggr(stat[:, 16 + 2 * q:18 + 2 * q], stat[:, 24 + 6 * q:30 + 6 * q]).then_inc(od_dve.sem, 1)
            dve.wait_ge(od_act.sem, od_act.at("ikroot"))
            nc.vector.reciprocal(stat[:, 22:24], stat[:, 20:22]).then_inc(od_dve.sem, 1)
            dve.wait_ge(od_dve.sem, od_dve.at("ikr"))
            for q in range(TT):
                for k in range(2):
                    nc.vector.tensor_scalar(ikn[:, P * q + ID * k:P * q + ID * k + ID], ps[:, 3, P * q:P * q + ID],
                                            stat[:, 16 + 2 * q:17 + 2 * q], stat[:, 22 + q:23 + q],
                                            ALU.subtract, ALU.mult).then_inc(od_dve.sem, 1)
            to_z("odd_w_in", 1, Z_OGATE + 2, per=1, u=16, g=4)
            dve.wait_ge(od_pe.sem, od_pe.at("kvt"))
            nc.vector.tensor_copy(ckvt[:], ps[:, 2, :].rearrange("p (a n) -> p a n", a=2)).then_inc(od_dve.sem, 1)
            dve.wait_ge(od_pe.sem, od_pe.at("ikt"))
            nc.vector.tensor_scalar(ikt[:], ps[:, 0, 0:T], rg(ROWS["ik_g"]), rg(ROWS["ik_b"]), ALU.mult, ALU.add).then_inc(od_dve.sem, 1)
            nc.vector.tensor_scalar(iw[:], ps[:, 3, 0:2 * P].rearrange("p (q n) -> p q n", q=2)[:, :, ID:ID + IH],
                                    IH ** -0.5 * ID ** -0.5, None, ALU.mult).then_inc(od_dve.sem, 1)
            to_z("odd_w_iq", 4, Z_IQ, per=4)
            dve.wait_ge(od_pe.sem, od_pe.at("ik"))
            nc.vector.memset(score, 0.0).then_inc(od_dve.sem, 1)
            with dve.Fori(0, 2) as i:
                for k2 in range(4):
                    c = i * 4 + k2
                    dve.wait_ge(ix_act.sem, ix_act.at("relu", c))
                    dve.wait_ge(od_dve.sem, od_dve.at("zero"))
                    for k in range(2):
                        for q in range(TT):
                            if k == 0:
                                dve.wait_ge(ix_dve.sem, ix_dve.done(c))
                            else:
                                dve.wait_ge(ix_dve.sem, ix_dve.at(f"s{q}", c))
                            nc.vector.scalar_tensor_tensor(out=score[:, q, :], in0=relu[:, 2 * k + q, :],
                                                           scalar=iw[:, q, bass.ds(i * 8 + (2 * k2 + k), 1)], in1=score[:, q, :],
                                                           op0=ALU.mult, op1=ALU.add).then_inc(ix_dve.sem, 1)
                    if k2 % 2:
                        n = k2 // 2
                        dve.wait_ge(unit_used, i * 8 + (UNIT0["odd_gate"] + 4 * n + 4))
                        nc.vector.tensor_reduce(z[:, bass.ds(i * 4 + (Z_OGATE + 4 + 2 * n), 2), :],
                                                halves((GROUP0["odd_gate"] + n) % 2), AX.X, ALU.add).then_inc(group_free, 1)
            dve.wait_ge(ix_dve.sem, ix_dve.done(8))
            nc.vector.scalar_tensor_tensor(out=work, in0=causal[:], scalar=3.0e8, in1=score, op0=ALU.mult, op1=ALU.add).then_inc(tk_dve.sem, 1)
            prev = ["fill", "fill"]
            for r in range(8):
                for q in range(TT):
                    dve.wait_ge(tk_dve.sem, tk_dve.at(prev[q]))
                    nc.vector.max(stat[:, 40 + 8 * q:48 + 8 * q], work[:, q, :]).then_inc(tk_dve.sem, 1)
                for q in range(TT):
                    dve.wait_ge(tk_dve.sem, tk_dve.at(f"max{r}{q}"))
                    nc.vector.match_replace(work[:, q, :], stat[:, 40 + 8 * q:48 + 8 * q], work[:, q, :],
                                            -3.4e38).then_inc(tk_dve.sem, 1)
                    prev[q] = f"rep{r}{q}"
                if r in (3, 7):
                    n = r // 4
                    to_z("odd_gate", 1, Z_OGATE + 12 + 2 * n, per=1, u=16 + 4 * n, g=4 + n)
            dve.wait_ge(tk_dve.sem, tk_dve.at("rep71"))
            nc.vector.tensor_scalar(work, work, -3.2e38, -1.0e30, ALU.is_ge, ALU.mult).then_inc(tk_dve.sem, 1)
            dve.wait_ge(tk_dve.sem, tk_dve.at("sel"))
            nc.vector.tensor_tensor(addm, work, causal[:], ALU.add).then_inc(tk_dve.sem, 1)
            with dve.Fori(0, 4) as i:
                for k in range(2):
                    g = i * 2 + k
                    G = g + GROUP0["odd_w_qb"]
                    dve.wait_ge(unit_used, g + (UNIT0["odd_w_qb"] + 1))
                    tmp = scr[:, 2 + k].rearrange("p (m n) -> p m n", m=2)
                    nc.vector.tensor_reduce(tmp, halves((GROUP0["odd_w_qb"] + k) % 2), AX.X, ALU.add).then_inc(group_free, 1)
                    dve.wait_ge(group_free, G + 1)
                    nc.vector.tensor_copy(a[:, bass.ds(i * 4 + 2 * k, 2), 0, :], tmp).then_inc(qb_dve.sem, 1)
                    dve.wait_ge(qb_dve.sem, qb_dve.at("hi", g))
                    nc.vector.tensor_tensor(a[:, bass.ds(i * 4 + 2 * k, 2), 1, :], tmp,
                                            a[:, bass.ds(i * 4 + 2 * k, 2), 0, :].bitcast(F32), ALU.subtract).then_inc(qb_dve.sem, 1)
            with dve.Fori(0, 4) as i:
                for k in range(4):
                    if k < 3:
                        dve.wait_ge(part_done, i * 3 + (k + 1))
                    else:
                        dve.wait_ge(unit_used, i + (UNIT0["odd_w_uk"] + 1))
                    nc.vector.tensor_reduce(z[:, bass.ds(i * 8 + (Z_QLAT + 2 * k), 2), :],
                                            halves((GROUP0["odd_w_uk"] + k) % 2), AX.X, ALU.add).then_inc(group_free, 1)
            for half in range(2):
                with dve.Fori(0, 4) as i:
                    r = i + 4 * half
                    for w in range(2):
                        own, at = da_dve[w].sem, da_dve[w].at
                        dve.wait_ge(da_pe[w].sem, da_pe[w].at("s", r))
                        dve.wait_ge(tk_dve.sem, tk_dve.at("am"))
                        nc.vector.tensor_tensor(o_s[w], ps[:, 2 * w, :].rearrange("p (q n) -> p q n", q=2), addm, ALU.add).then_inc(own, 1)
                        dve.wait_ge(own, at("mask", r))
                        nc.vector.tensor_reduce(stat[:, 8 * w:8 * w + 2], o_s[w], AX.X, ALU.max).then_inc(own, 1)
                        dve.wait_ge(own, at("max", r))
                        nc.vector.tensor_scalar(stat[:, 8 * w + 2:8 * w + 4], stat[:, 8 * w:8 * w + 2], -1.0, None, ALU.mult).then_inc(own, 1)
                    for w in range(2):
                        own, at = da_dve[w].sem, da_dve[w].at
                        dve.wait_ge(da_act[w].sem, da_act[w].at("p1", r))
                        nc.vector.reciprocal(stat[:, 8 * w + 6:8 * w + 8], stat[:, 8 * w + 4:8 * w + 6]).then_inc(own, 1)
                        dve.wait_ge(own, at("rsum", r))
                        for q in range(TT):
                            nc.vector.tensor_scalar(o_s[w][:, q, :], o_s[w][:, q, :], stat[:, 8 * w + 6 + q:8 * w + 7 + q], None,
                                                    ALU.mult).then_inc(own, 1)
                    for w in range(2):
                        dve.wait_ge(da_pe[w].sem, da_pe[w].at("pt", r))
                        nc.vector.tensor_copy(o_pt[w], ps[:, 2 * w + 1, :].rearrange("p (q n) -> p q n", q=2)).then_inc(da_dve[w].sem, 1)
                    for w in range(2):
                        dve.wait_ge(da_act[w].sem, da_act[w].at("ohi", r))
                        ah = a[:, bass.ds(i * 4 + 2 * w, 2), :, :]
                        nc.vector.tensor_tensor(ah[:, :, 1, :], ps[:, 2 * w, :].rearrange("p (k n) -> p k n", k=2),
                                                ah[:, :, 0, :].bitcast(F32), ALU.subtract).then_inc(da_dve[w].sem, 1)
                for g4 in range(4):
                    g = 4 * half + g4
                    G = GROUP0["odd_w_uv"] + g
                    if g % 2 == 0:
                        dve.wait_ge(part_done, 12 + g // 2 + 1)
                    else:
                        dve.wait_ge(unit_used, UNIT0["odd_w_uv"] + g // 2 + 1)
                    if g:
                        dve.wait_ge(uv_dve.sem, uv_dve.at("lo", g - 1))
                    tmp = scr[:, 2].rearrange("p (m n) -> p m n", m=2)
                    nc.vector.tensor_reduce(tmp, halves(G % 2), AX.X, ALU.add).then_inc(group_free, 1)
                    dve.wait_ge(group_free, G + 1)
                    dve.wait_ge(od_act.sem, od_act.at("ogate"))
                    nc.vector.tensor_tensor(tmp, tmp, z[:, Z_OGATE + 2 * g:Z_OGATE + 2 * g + 2, :], ALU.mult).then_inc(uv_dve.sem, 1)
                    dve.wait_ge(uv_dve.sem, uv_dve.at("gate", g))
                    nc.vector.tensor_copy(b[:, 2 * g:2 * g + 2, 0, :], tmp).then_inc(uv_dve.sem, 1)
                    dve.wait_ge(uv_dve.sem, uv_dve.at("hi", g))
                    nc.vector.tensor_tensor(b[:, 2 * g:2 * g + 2, 1, :], tmp, b[:, 2 * g:2 * g + 2, 0, :].bitcast(F32),
                                            ALU.subtract).then_inc(uv_dve.sem, 1)
            to_x("odd_w_out")
            norm(2)
            norm(3)
            to_z("w_in_2", 4, Z_F, per=4)
            soft = stat[:, 0:32]
            dve.wait_ge(sc_pe.sem, sc_pe.at("scal"))
            dve.wait_ge(small_in, 16 * 4)
            aa = flat(dsc[:, AA])
            for c in range(TT):
                nc.vector.tensor_tensor(aa[:, 16 * c:16 * c + 16], ps[:, 0, c * 32 + 16:c * 32 + 32], dtb[:, 0, :], ALU.add).then_inc(sc_dve.sem, 1)
            dve.wait_ge(sc_dve.sem, sc_dve.at("a1"))
            nc.vector.tensor_scalar(flat(dsc[:, NEG]), aa, -1.0, None, ALU.mult).then_inc(sc_dve.sem, 1)
            dve.wait_ge(sc_dve.sem, sc_dve.at("neg"))
            nc.vector.tensor_tensor(soft, flat(dsc[:, NEG]), aa, ALU.max).then_inc(sc_dve.sem, 1)
            nc.vector.tensor_scalar(aa, aa, 0.0, None, ALU.max).then_inc(sc_dve.sem, 1)
            dve.wait_ge(sc_act.sem, sc_act.at("ea"))
            dve.wait_ge(sc_dve.sem, sc_dve.at("pos"))
            nc.vector.tensor_tensor(aa, aa, soft, ALU.add).then_inc(sc_dve.sem, 1)
            dve.wait_ge(sc_dve.sem, sc_dve.at("sp"))
            nc.vector.tensor_scalar(dtb[:, 1, :], dtb[:, 1, :], -1.0, None, ALU.mult).then_inc(sc_dve.sem, 1)
            dve.wait_ge(sc_dve.sem, sc_dve.at("nea"))
            for c in range(TT):
                nc.vector.tensor_tensor(dsc[:, GG, :, c, :], aa[:, 16 * c:16 * c + 16].rearrange("p (d h) -> p d h", d=2),
                                        dtb[:, 1, :].rearrange("p (d h) -> p d h", d=2), ALU.mult).then_inc(sc_dve.sem, 1)
            dve.wait_ge(sc_pe.sem, sc_pe.at("cum"))
            nc.vector.tensor_copy(flat(dsc[:, GC]), ps[:, 1, 0:32]).then_inc(sc_dve.sem, 1)
            nc.vector.tensor_copy(flat(dsc[:, REM]), ps[:, 1, 32:64]).then_inc(sc_dve.sem, 1)
            dve.wait_ge(sc_act.sem, sc_act.at("er"))
            nc.vector.tensor_scalar(flat(dsc[:, NEG]), flat(dsc[:, EG]), -1.0, None, ALU.mult).then_inc(sc_dve.sem, 1)
            with dve.Fori(0, FG) as g:
                for n in range(2):
                    dve.wait_ge(unit_used, g * 8 + (UNIT0["w_in_2"] + 16 + 4 * n + 4))
                    nc.vector.tensor_reduce(z[:, bass.ds(g * 4 + 2 * n, 2), :], halves((GROUP0["w_in_2"] + n) % 2), AX.X,
                                            ALU.add).then_inc(group_free, 1)
                    if n == 0:
                        dve.wait_ge(fo_act.sem, fo_act.at("hi", g))
                        bg = b[:, bass.ds(g + 8, 1), :, :].rearrange("p a s n -> p (a s) n")
                        nc.vector.tensor_tensor(bg[:, 1, :], ps[:, 3, 0:T], bg[:, 0, :].bitcast(F32), ALU.subtract).then_inc(fo_dve.sem, 1)
            two = lambda v: v.rearrange("p (c i) -> p c i", c=2).unsqueeze(1).broadcast_to([P, 2, 2, P])
            dc = lambda v: v.rearrange("p (d c) i -> p d c i", d=2)
            idb = ident[:].unsqueeze(1).broadcast_to([P, 4, P])
            with dve.Fori(0, HN // 2) as i:
                h = [i * 2 + w.w for w in ways]

                def per(n, w):
                    return dsc[:, n, :, :, bass.ds(h[w.w], 1)].rearrange("p d c h -> p (d c) h").broadcast_to([P, 4, P])

                def col(n, d, c, w):
                    return dsc[:, n, d, c, bass.ds(h[w.w], 1)]

                def gates_out(n):
                    G = GROUP0["gates"] + n
                    dve.wait_ge(unit_used, i * 16 + (UNIT0["gates"] + 4 * n + 4))
                    place, parts = z[:, bass.ds(i * 2 + 8 * n, 2), :], halves(G % 2)
                    nc.vector.tensor_scalar(place, parts[:, :, :, 0], 0.0, None, ALU.add).then_inc(gate_half, 1)
                    dve.wait_ge(gate_half, i * 4 + (n + 1))
                    nc.vector.tensor_tensor(place, place, parts[:, :, :, 1], ALU.add).then_inc(group_free, 1)

                for w in ways:
                    own = dn_dve[w.w]
                    if w.w == 0:
                        dve.wait_ge(group_free, i * 4 + (GROUP0["w_in_2"] + 20))
                        dve.wait_ge(fo_dve.sem, fo_dve.done(FG))
                    dve.wait_ge(own.sem, own.done(i))
                    dve.wait_ge(dn_act[w.w].sem, dn_act[w.w].done(i))
                    src = [z[:, bass.ds(h[w.w] + 8 * y, 1), :].rearrange("p a n -> p (a n)") for y in range(3)]
                    dst = (w.qk_feat[:, 0, :], w.qk_feat[:, 1, :], w.v_feat)
                    tap = lambda k, y: vec[:, bass.ds(h[w.w] + (ROWS["conv_w_2"] + 24 * k + 8 * y), 1)]
                    for y in range(3):
                        nc.vector.tensor_scalar(dst[y], src[y], tap(2, y), None, ALU.mult).then_inc(own.sem, 1)
                    for n, (k, o0, i0, m) in enumerate(((0, 2, 0, T - 2), (1, 1, 0, T - 1), (3, 0, 1, T - 1), (4, 0, 2, T - 2))):
                        for y in range(3):
                            dve.wait_ge(own.sem, own.at(f"cv{y}{n}", i))
                            nc.vector.scalar_tensor_tensor(out=dst[y][:, o0:o0 + m], in0=src[y][:, i0:i0 + m], scalar=tap(k, y),
                                                           in1=dst[y][:, o0:o0 + m], op0=ALU.mult, op1=ALU.add).then_inc(own.sem, 1)
                for w in ways:
                    own = dn_dve[w.w]
                    dve.wait_ge(dn_act[w.w].sem, dn_act[w.w].at("root", i))
                    nc.vector.reciprocal(w.root, w.root).then_inc(own.sem, 1)
                    dve.wait_ge(own.sem, own.at("rn", i))
                    nc.vector.scalar_tensor_tensor(out=w.qk_feat[:, 0, :], in0=w.qk_feat[:, 0, :], scalar=DH ** -0.5,
                                                   in1=w.root[:, 0, :], op0=ALU.mult, op1=ALU.mult).then_inc(own.sem, 1)
                    nc.vector.tensor_tensor(w.qk_feat[:, 1, :], w.qk_feat[:, 1, :], w.root[:, 1, :], ALU.mult).then_inc(own.sem, 1)
                    nc.vector.tensor_copy(w.gate, per(GG, w)).then_inc(own.sem, 1)
                for w in ways:
                    own = dn_dve[w.w]
                    dve.wait_ge(dn_pe[w.w].sem, dn_pe[w.w].at("gc", i))
                    dve.wait_ge(own.sem, own.at("kn", i))
                    nc.vector.tensor_tensor(w.decay, four1(w.x_ps), per(GC, w), ALU.subtract).then_inc(own.sem, 1)
                    dve.wait_ge(own.sem, own.at("dsub", i))
                    nc.vector.scalar_tensor_tensor(out=w.decay, in0=w.decay, scalar=0.0, in1=dmask[:], op0=ALU.min,
                                                   op1=ALU.add).then_inc(own.sem, 1)
                for w in ways:
                    own = dn_dve[w.w]
                    dve.wait_ge(dn_act[w.w].sem, dn_act[w.w].at("dexp", i))
                    dve.wait_ge(dn_pe[w.w].sem, dn_pe[w.w].at("gram", i))
                    nc.vector.tensor_tensor(dc(w.m), two(w.y_ps[:, 0:T]), dc(w.decay), ALU.mult).then_inc(own.sem, 1)
                    dve.wait_ge(own.sem, own.at("mt1", i))
                    nc.vector.tensor_tensor(w.m, w.m, per(BETA, w), ALU.mult).then_inc(own.sem, 1)
                    nc.vector.tensor_tensor(dc(w.qk), two(w.y_ps[:, T:2 * T]), dc(w.decay), ALU.mult).then_inc(own.sem, 1)
                    nc.vector.tensor_copy(w.t, idb).then_inc(own.sem, 1)
                    nc.vector.tensor_copy(w.u, idb).then_inc(own.sem, 1)
                    dve.wait_ge(own.sem, own.at("mt2", i))
                    nc.vector.tensor_tensor(dc(w.mm), dc(w.m), lmask[:, 0, :, :].unsqueeze(2).broadcast_to([P, 2, 2, P]),
                                            ALU.mult).then_inc(own.sem, 1)
                gates_out(0)
                for l in range(LEVELS):
                    if l < LEVELS - 1:
                        for w in ways:
                            dve.wait_ge(dn_pe[w.w].sem, dn_pe[w.w].at(f"x{l}", i))
                            nc.vector.tensor_tensor(dc(w.mm), dc(w.m), lmask[:, l + 1, :, :].unsqueeze(2).broadcast_to([P, 2, 2, P]),
                                                    ALU.mult).then_inc(dn_dve[w.w].sem, 1)
                    if l in (2, 6):
                        gates_out(l // 4 + 1)
                    for w in ways:
                        own = dn_dve[w.w]
                        dve.wait_ge(dn_pe[w.w].sem, dn_pe[w.w].at(f"tu{l}", i))
                        dve.wait_ge(own.sem, own.at(f"u{l}", i))
                        if l < LEVELS - 1:
                            nc.vector.tensor_tensor(w.t, w.t, four1(w.x_ps), ALU.subtract).then_inc(own.sem, 1)
                        nc.vector.tensor_tensor(w.u, w.u, four1(w.y_ps), ALU.subtract).then_inc(own.sem, 1)
                for w in ways:
                    own = dn_dve[w.w]
                    dve.wait_ge(dn_pe[w.w].sem, dn_pe[w.w].at("y1", i))
                    for d in range(2):
                        nc.vector.tensor_scalar(w.v_new[:, 2 * d + d, :], four1(w.x_ps)[:, d, :], col(BETA, d, d, w), None, ALU.mult).then_inc(own.sem, 1)
                    for d in range(2):
                        dve.wait_ge(own.sem, own.at(("vn1a", "vn1b")[d], i))
                        nc.vector.tensor_scalar(w.v_dec[:, d, :], w.v_new[:, 2 * d + d, :], col(ER, d, d, w), None, ALU.mult).then_inc(own.sem, 1)
                for w in ways:
                    own = dn_dve[w.w]
                    dve.wait_ge(dn_pe[w.w].sem, dn_pe[w.w].at("ks", i))
                    for d in range(2):
                        nc.vector.scalar_tensor_tensor(out=w.r[:, d, :], in0=four1(w.x_ps)[:, d, :], scalar=col(NEG, d, 1 - d, w),
                                                       in1=w.tok[:, 2 + 1 - d, :], op0=ALU.mult, op1=ALU.add).then_inc(own.sem, 1)
                for w in ways:
                    own = dn_dve[w.w]
                    dve.wait_ge(dn_pe[w.w].sem, dn_pe[w.w].at("y2", i))
                    for d in range(2):
                        nc.vector.tensor_scalar(w.v_new[:, 2 * d + 1 - d, :], four1(w.x_ps)[:, d, :], col(BETA, d, 1 - d, w), None, ALU.mult).then_inc(own.sem, 1)
                for w in ways:
                    own = dn_dve[w.w]
                    dve.wait_ge(dn_pe[w.w].sem, dn_pe[w.w].at("o", i))
                    dve.wait_ge(dn_act[w.w].sem, dn_act[w.w].at("qs1", i))
                    nc.vector.tensor_tensor(w.u[:, 0:2, :], four1(w.y_ps)[:, 0:2, :], w.x[:, 2:4, :], ALU.add).then_inc(own.sem, 1)
                for w in ways:
                    own = dn_dve[w.w]
                    dve.wait_ge(dn_act[w.w].sem, dn_act[w.w].at("oroot", i))
                    nc.vector.reciprocal(w.norm[:, 4:6], w.norm[:, 2:4]).then_inc(own.sem, 1)
                    dve.wait_ge(own.sem, own.at("orn", i))
                    for c in range(TT):
                        nc.vector.tensor_scalar(w.u[:, c, :], w.u[:, c, :], w.norm[:, 4 + c:5 + c], None, ALU.mult).then_inc(own.sem, 1)
                for w in ways:
                    own = dn_dve[w.w]
                    dve.wait_ge(dn_pe[w.w].sem, dn_pe[w.w].at("ot", i))
                    dve.wait_ge(dn_act[w.w].sem, dn_act[w.w].at("sz", i))
                    tmp = w.v_dec[:, 2:4, :].rearrange("p a n -> p (a n)")
                    nc.vector.scalar_tensor_tensor(out=tmp, in0=w.x_ps[:, 0:T], scalar=vec[:, ROWS["g_dn_head_2"]:ROWS["g_dn_head_2"] + 1],
                                                   in1=w.x[:, 0:2, :].rearrange("p a n -> p (a n)"), op0=ALU.mult, op1=ALU.mult).then_inc(own.sem, 1)
                    dve.wait_ge(own.sem, own.at("ot", i))
                    bh = b[:, bass.ds(h[w.w], 1), :, :].rearrange("p a s n -> p (a s) n")
                    nc.vector.tensor_copy(bh[:, 0, :], tmp).then_inc(own.sem, 1)
                    dve.wait_ge(own.sem, own.at("hi", i))
                    nc.vector.tensor_tensor(bh[:, 1, :], tmp, bh[:, 0, :].bitcast(F32), ALU.subtract).then_inc(own.sem, 1)
                gates_out(3)
            own, at = mx_dve.sem, mx_dve.at
            with dve.Fori(0, 4) as i:
                for k in range(2):
                    r = i * 2 + k
                    up, fr = (scr[:, 2 * k + n].rearrange("p (m n) -> p m n", m=2) for n in range(2))
                    for n, (v, y) in enumerate(((up, "dn"), (fr, "fr"))):
                        dve.wait_ge(unit_used, i * 8 + (UNIT0["mix"] + 4 * k + 2 * n + 2))
                        if k == 0 and n == 0:
                            dve.wait_ge(mx_act.sem, mx_act.at("sigd"))
                            dve.wait_ge(dn_dve[1].sem, dn_dve[1].done(HN // 2))
                        nc.vector.tensor_reduce(v, halves((GROUP0["mix"] + n) % 2), AX.X, ALU.add).then_inc(group_free, 1)
                        dve.wait_ge(group_free, i * 4 + (GROUP0["mix"] + 2 * k + n + 1))
                        nc.vector.tensor_tensor(v, v, z[:, bass.ds(i * 2 + (16 * k + 8 * n), 2), :], ALU.mult).then_inc(own, 1)
                    dve.wait_ge(own, at("frg", r))
                    nc.vector.tensor_tensor(fr, up, fr, ALU.add).then_inc(own, 1)
                    dve.wait_ge(own, at("sum", r))
                    aa = a[:, bass.ds(i * 4 + 2 * k, 2), :, :]
                    nc.vector.tensor_copy(aa[:, :, 0, :], fr).then_inc(own, 1)
                    dve.wait_ge(own, at("hi", r))
                    nc.vector.tensor_tensor(aa[:, :, 1, :], fr, aa[:, :, 0, :].bitcast(F32), ALU.subtract).then_inc(own, 1)
            to_x("w_o_2")
            norm(4)
            for ph in range(4):
                g0 = GROUP0["mlp"] + 16 * ph
                with dve.Fori(0, 4) as i:
                    for k in range(2):
                        r = i * 2 + (k + 8 * ph)
                        dve.wait_ge(unit_used, i * 8 + (UNIT0["mlp"] + 64 * ph + 4 * (k + 1)))
                        tmp = scr[:, 2 * k].rearrange("p (m n) -> p m n", m=2)
                        tm2 = scr[:, 2 * k + 1].rearrange("p (m n) -> p m n", m=2)
                        bb = b[:, bass.ds(i * 4 + 2 * k, 2), :, :]
                        if k == 0:
                            dve.wait_ge(ml_dve.sem, ml_dve.done(r))
                        nc.vector.tensor_reduce(tmp, halves((g0 + k) % 2), AX.X, ALU.add).then_inc(group_free, 1)
                        dve.wait_ge(group_free, i * 2 + (g0 + k + 1))
                        nc.vector.scalar_tensor_tensor(out=tm2, in0=tmp, scalar=0.0, in1=tmp, op0=ALU.max, op1=ALU.mult).then_inc(ml_dve.sem, 1)
                        dve.wait_ge(ml_dve.sem, ml_dve.at("sq", r))
                        nc.vector.tensor_copy(bb[:, :, 0, :], tm2).then_inc(ml_dve.sem, 1)
                        dve.wait_ge(ml_dve.sem, ml_dve.at("hi", r))
                        nc.vector.tensor_tensor(bb[:, :, 1, :], tm2, bb[:, :, 0, :].bitcast(F32), ALU.subtract).then_inc(ml_dve.sem, 1)
                to_x("mlp", u=64 * ph + 32, g=16 * ph + 8)
            norm(5, last=True)
            for s in range(8):
                dve.wait_ge(fin_pe, s + 1)
                nc.vector.tensor_copy(z[:, 16 + 2 * s:18 + 2 * s, :], ps[:, 2 + s % 2, :].rearrange("p (q n) -> p q n", q=2)).then_inc(fin_dve, 1)

        @block.tensor
        def _(pe):
            pe.wait_ge(x_in, 48)
            for s in range(8):
                if s >= 3:
                    pe.wait_ge(x_done, s - 2)
                for k in range(2):
                    for tt in range(TT):
                        c = 2 * s + k
                        m = nc.tensor.transpose(ps[:, 1 + s % 3, k * T + tt * P:k * T + (tt + 1) * P],
                                                z[:, 8 * tt:8 * tt + 8, :].rearrange("p a b -> p (a b)")[:, c * P:(c + 1) * P],
                                                ident[:])
                m.then_inc(tp_pe, 1)
            pe.wait_ge(consts_in, 16 * N_CONST)
            for k in range(N_PACKS):
                rows = min(P, N_ROWS - k * P)
                dst = (ps, lin_ps)[k // 4][:, 0, (k % 4) * P:(k % 4) * P + rows]
                m = nc.tensor.transpose(dst, pk[0:rows, k * P:(k + 1) * P], ident[0:rows, 0:rows])
            m.then_inc(tp_pe, 1)
            pe.wait_ge(tp_ev, 2)
            pe.wait_ge(bld, 3)

            def norm_sums(r):
                for s in range(8):
                    pe.wait_ge(nr_act.sem, nr_act.at(f"sq{s}", r))
                    for k in range(2):
                        m = nc.tensor.matmul(ps[:, 0, 0:T], ones[:], scr[:, s % 2, k * T:(k + 1) * T],
                                             start=(s == 0 and k == 0), stop=(s == 7 and k == 1))
                    m.then_inc(nr_pe.sem, 1)

            def linear(u0, g0, n, kus, src, k0=0, waits=None, per=2):
                slots = lambda j: [(u0 + j * kus + q) % SLOTS for q in range(kus)]

                def turn(u, g, w=None, first=False):
                    for j in range(per):
                        run(u + j * kus, slots(j), g + j, (g0 + j) % 2, src, k0, w if j == 0 else None, not (first and g0 == 0))

                turn(u0, g0, waits, first=True)
                if n > per:
                    with pe.Fori(1, n // per) as i:
                        turn(i * (per * kus) + u0, i * per + g0)

            def product(u, g, parity, q, n, slot, src, k0, wait, free):
                if q == 0 and free:
                    pe.wait_ge(group_free, g - 1)
                pe.wait_ge(lo_done, u + 1)
                hi = w_hi[:, slot].rearrange("p (k n) -> p k n", k=UK)
                lo = w_lo[:, slot].rearrange("p (k n) -> p k n", k=UK)
                for k in range(UK):
                    kk = k0 + q * UK + k
                    if wait:
                        wait(q * UK + k)
                    for m in range(2):
                        acc = lin_ps[:, 2 * parity + m, :]
                        nc.tensor.matmul(acc, hi[:, k, m * P:(m + 1) * P], src[:, kk].rearrange("p s n -> p (s n)"),
                                         start=(q == 0 and k == 0), stop=False)
                        last = nc.tensor.matmul(acc[:, 0:T], lo[:, k, m * P:(m + 1) * P], src[:, kk, 0, :],
                                                start=False, stop=(q == n - 1 and k == UK - 1))
                last.then_inc(unit_used, 1)

            def run(u, slots, g, parity, src, k0, wait, free):
                for q, slot in enumerate(slots):
                    product(u + q, g, parity, q, len(slots), slot, src, k0, wait, free)

            def normed(r):
                def wait(c):
                    if c % 2 == 0:
                        pe.wait_ge(nr_lo.sem, nr_lo.at(f"{c // 2}", SPLIT_ROUND[r]))
                return wait

            norm_sums(0)
            linear(0, 0, 24, 4, a, waits=normed(0))
            for c in range(8):
                pe.wait_ge(cv_dve.sem, cv_dve.at(f"tap{TAPS - 1}{c % 2}", c // 2))
                m = nc.tensor.matmul(ps[:, 0, 0:T], ones[:], z[:, Z_AGT + c, :], start=(c == 0), stop=(c == 7))
            m.then_inc(ln_pe.sem, 1)
            run(96, range(4), 24, 0, a, 0, None, True)
            for s in range(4):
                pe.wait_ge(ln_act.sem, ln_act.at(f"sq{s}"))
                for k in range(2):
                    m = nc.tensor.matmul(ps[:, 1, 0:T], ones[:], scr[:, s % 2, k * T:(k + 1) * T],
                                         start=(s == 0 and k == 0), stop=(s == 3 and k == 1))
                m.then_inc(ln_pe.sem, 1)
            for g in range(25, 28):
                run(4 * g, range(4), g, g % 2, a, 0, None, True)
            def ln_ready(c):
                if c % 2 == 0:
                    pe.wait_ge(ln_dve.sem, ln_dve.at(f"lo{c // 2}"))
            linear(UNIT0["even_w_pw"], GROUP0["even_w_pw"], 4, 2, b, k0=8, waits=ln_ready, per=4)
            with pe.Fori(0, HE // 2) as i:
                for w in range(2):
                    own = at_pe[w].sem
                    pe.wait_ge(at_act[w].sem, at_act[w].at("vs", i))
                    for c in range(TT):
                        m = nc.tensor.transpose(ps[:, 2 * w, c * P:(c + 1) * P], e_v[w][:, c * P:(c + 1) * P], ident[:])
                    m.then_inc(own, 1)
                    for q in range(TT):
                        m = nc.tensor.matmul(ps[:, 2 * w + 1, q * T:(q + 1) * T], e_q[w][:, q * P:(q + 1) * P],
                                             z[:, bass.ds(i * 2 + (Z_K + w), 1), :].rearrange("p a n -> p (a n)"), start=True, stop=True)
                    m.then_inc(own, 1)
                for w in range(2):
                    pe.wait_ge(at_dve[w].sem, at_dve[w].at("n1", i))
                    for kt in range(TT):
                        for q in range(TT):
                            m = nc.tensor.transpose(ps[:, 2 * w, kt * T + q * P:kt * T + (q + 1) * P], e_s[w][:, q, kt * P:(kt + 1) * P], ident[:])
                    m.then_inc(at_pe[w].sem, 1)
                for w in range(2):
                    pe.wait_ge(at_dve[w].sem, at_dve[w].at("ptc", i))
                    for kt in range(TT):
                        m = nc.tensor.matmul(ps[:, 2 * w + 1, 0:T], e_vt[w][:, kt * P:(kt + 1) * P], e_pt[w][:, kt, :],
                                             start=(kt == 0), stop=(kt == TT - 1))
                    m.then_inc(at_pe[w].sem, 1)

            def cat_ready(c):
                if c == 0:
                    pe.wait_ge(pw_dve.sem, pw_dve.at("lo", 3))
                if c >= 8:
                    pe.wait_ge(at_dve[c % 2].sem, at_dve[c % 2].at("lo", (c - 8) // 2))
            linear(UNIT0["even_w_out"], GROUP0["even_w_out"], 8, 4, b, waits=cat_ready)
            norm_sums(1)
            linear(UNIT0["odd_w_in"], GROUP0["odd_w_in"], 3, 4, a, waits=normed(1), per=3)
            pe.wait_ge(sw_in, 16)
            for q in range(TT):
                for c in range(DC):
                    for s in range(2):
                        m = nc.tensor.matmul(ps[:, 3, q * P:q * P + ID + IH], a[:, c, s, q * P:(q + 1) * P].bitcast(F32),
                                             small_w[:, c * (ID + IH):(c + 1) * (ID + IH)],
                                             start=(c == 0 and s == 0), stop=(c == DC - 1 and s == 1))
            m.then_inc(od_pe.sem, 1)
            gate_group = lambda u, g: run(u, range(4), g, g % 2, a, 0, None, True)
            gate_group(UNIT0["odd_w_in"] + 12, GROUP0["odd_w_in"] + 3)
            pe.wait_ge(od_act.sem, od_act.at("cqsq"))
            for c in range(4):
                m = nc.tensor.matmul(ps[:, 0, 0:T], ones[:], scr[:, 0:2, :].rearrange("p a (k n) -> p (a k) n", k=2)[:, c, :],
                                     start=(c == 0), stop=(c == 3))
            m.then_inc(od_pe.sem, 1)
            pe.wait_ge(od_act.sem, od_act.at("kvsq"))
            for c in range(2):
                m = nc.tensor.matmul(ps[:, 1, 0:T], ones[:], scr[:, 3, c * T:(c + 1) * T], start=(c == 0), stop=(c == 1))
            m.then_inc(od_pe.sem, 1)
            gate_group(UNIT0["odd_w_in"] + 16, GROUP0["odd_w_in"] + 4)
            pe.wait_ge(od_dve.sem, od_dve.at("kv1"))
            for q in range(TT):
                for c in range(2):
                    m = nc.tensor.transpose(ps[:, 2, q * T + c * P:q * T + (c + 1) * P], ckvn[:, c, q * P:(q + 1) * P], ident[:])
            m.then_inc(od_pe.sem, 1)
            pe.wait_ge(od_dve.sem, od_dve.at("ikn3"))
            for q in range(TT):
                m = nc.tensor.transpose(ps[:, 0, q * P:(q + 1) * P], ikn[:, q * P:(q + 1) * P], ident[:])
            m.then_inc(od_pe.sem, 1)

            def cq_ready(c):
                if c == 0:
                    pe.wait_ge(od_dve.sem, od_dve.at("cqlo"))
            linear(UNIT0["odd_w_iq"], GROUP0["odd_w_iq"], 4, 1, b, waits=cq_ready, per=4)
            with pe.Fori(0, 2) as i:
                for k4 in range(4):
                    c = i * 4 + k4
                    pe.wait_ge(ix_act.sem, ix_act.at("stage", c))
                    pe.wait_ge(od_dve.sem, od_dve.at("iw"))
                    for k in range(2):
                        for q in range(TT):
                            m = nc.tensor.matmul(ps[:, k, q * T:(q + 1) * T], iq_st[ID * k:ID * k + ID, q * P:(q + 1) * P],
                                                 ikt[ID * k:ID * k + ID, :], start=True, stop=True)
                    m.then_inc(ix_pe.sem, 1)
                    for n in (2 * k4, 2 * k4 + 1):
                        g = n // 4
                        product(i * 8 + (UNIT0["odd_gate"] + n), i * 2 + (GROUP0["odd_gate"] + g), (GROUP0["odd_gate"] + g) % 2,
                                n % 4, 4, n % 4, a, 0, None, True)
            for n in (4, 5):
                gate_group(UNIT0["odd_gate"] + 4 * n, GROUP0["odd_gate"] + n)
            linear(UNIT0["odd_w_qb"], GROUP0["odd_w_qb"], 8, 1, b, per=4)
            for n in range(4):
                u = UNIT0["odd_w_uk"] + n
                hi = w_hi[:, n].rearrange("p (k n) -> p k n", k=UK)
                lo = w_lo[:, n].rearrange("p (k n) -> p k n", k=UK)
                pe.wait_ge(lo_done, u + 1)
                for j in range(4):
                    h = 4 * n + j
                    G = GROUP0["odd_w_uk"] + h
                    pe.wait_ge(group_free, G - 1)
                    pe.wait_ge(qb_dve.sem, qb_dve.at("lo", h // 2))
                    for m in range(2):
                        acc = lin_ps[:, 2 * (G % 2) + m, :]
                        nc.tensor.matmul(acc, hi[:, j, m * P:(m + 1) * P], a[:, h].rearrange("p s n -> p (s n)"), start=True, stop=False)
                        last = nc.tensor.matmul(acc[:, 0:T], lo[:, j, m * P:(m + 1) * P], a[:, h, 0, :], start=False, stop=True)
                    last.then_inc(unit_used if j == 3 else part_done, 1)
            for half in range(2):
                with pe.Fori(0, 4) as i:
                    r = i + 4 * half
                    for w in range(2):
                        pe.wait_ge(da_act[w].sem, da_act[w].at("stage", r))
                        pe.wait_ge(da_dve[w].sem, da_dve[w].done(r))
                        for q in range(TT):
                            for c in range(2):
                                m = nc.tensor.matmul(ps[:, 2 * w, q * T:(q + 1) * T], o_q[w][:, c * T + q * P:c * T + (q + 1) * P], ckvn[:, c, :],
                                                     start=(c == 0), stop=(c == 1))
                        m.then_inc(da_pe[w].sem, 1)
                    for w in range(2):
                        pe.wait_ge(da_dve[w].sem, da_dve[w].at("n1", r))
                        for kt in range(TT):
                            for q in range(TT):
                                m = nc.tensor.transpose(ps[:, 2 * w + 1, kt * T + q * P:kt * T + (q + 1) * P], o_s[w][:, q, kt * P:(kt + 1) * P], ident[:])
                        m.then_inc(da_pe[w].sem, 1)
                    for w in range(2):
                        pe.wait_ge(da_dve[w].sem, da_dve[w].at("ptc", r))
                        for c in range(2):
                            for kt in range(TT):
                                m = nc.tensor.matmul(ps[:, 2 * w, c * T:(c + 1) * T], ckvt[:, kt, c * P:(c + 1) * P], o_pt[w][:, kt, :],
                                                     start=(kt == 0), stop=(kt == TT - 1))
                        m.then_inc(da_pe[w].sem, 1)
                for n in range(2 * half, 2 * half + 2):
                    u = UNIT0["odd_w_uv"] + n
                    hi = w_hi[:, n].rearrange("p (k n) -> p k n", k=UK)
                    lo = w_lo[:, n].rearrange("p (k n) -> p k n", k=UK)
                    pe.wait_ge(lo_done, u + 1)
                    for w in range(2):
                        pe.wait_ge(da_dve[w].sem, da_dve[w].at("olo", 4 * half + 3))
                    for j in range(2):
                        G = GROUP0["odd_w_uv"] + 2 * n + j
                        pe.wait_ge(group_free, G - 1)
                        for m in range(2):
                            h = 2 * j + m
                            acc = lin_ps[:, 2 * (G % 2) + m, :]
                            for k in range(2):
                                src = a[:, 2 * (4 * (n % 2) + h) + k]
                                nc.tensor.matmul(acc, hi[:, h, k * P:(k + 1) * P], src.rearrange("p s n -> p (s n)"), start=(k == 0), stop=False)
                                last = nc.tensor.matmul(acc[:, 0:T], lo[:, h, k * P:(k + 1) * P], src[:, 0, :], start=False, stop=(k == 1))
                        last.then_inc(unit_used if j == 1 else part_done, 1)

            def o_ready(c):
                if c == 0:
                    pe.wait_ge(uv_dve.sem, uv_dve.at("lo", 7))
            linear(UNIT0["odd_w_out"], GROUP0["odd_w_out"], 8, 4, b, waits=o_ready)
            norm_sums(2)
            norm_sums(3)
            linear(UNIT0["w_in_2"], GROUP0["w_in_2"], 4, 4, a, waits=normed(3), per=4)
            pe.wait_ge(table_in, 64)
            for q in range(TT):
                for c in range(DC):
                    for s in range(2):
                        m = nc.tensor.matmul(ps[:, 0, q * 32:q * 32 + 32], a[:, c, s, q * P:(q + 1) * P].bitcast(F32),
                                             scw[:, c * 32:c * 32 + 32], start=(c == 0 and s == 0), stop=(c == DC - 1 and s == 1))
            m.then_inc(sc_pe.sem, 1)
            run(UNIT0["w_in_2"] + 16, range(4), GROUP0["w_in_2"] + 4, GROUP0["w_in_2"] % 2, a, 0, None, True)
            pe.wait_ge(sc_dve.sem, sc_dve.at("g1"))
            for n in range(4):
                d = n % 2
                m = nc.tensor.matmul(ps[:, 1, 16 * n:16 * n + 16], tri[:, n, :], flat(dsc[:, GG])[:, 16 * d:16 * d + 16], start=True, stop=True)
            m.then_inc(sc_pe.sem, 1)
            def fourier(g, groups):
                def unit(n):
                    product(g * 8 + (UNIT0["w_in_2"] + 20 + n), g * 2 + (GROUP0["w_in_2"] + 5 + n // 4),
                            (GROUP0["w_in_2"] + 5 + n // 4) % 2, n % 4, 4, n % 4, a, 0, None, True)

                pe.wait_ge(fo_act.sem, fo_act.at("stage", g))
                for q in range(TT):
                    m = nc.tensor.matmul(ps[:, 2, q * T:(q + 1) * T], z[:, 46, q * P:(q + 1) * P], z[:, 40, :], start=True, stop=True)
                m.then_inc(fo_pe.sem, 1)
                unit(0)
                pe.wait_ge(fo_act.sem, fo_act.at("ab", g))
                pe.wait_ge(fo_dve.sem, fo_dve.done(g))
                for q in range(TT):
                    for s in range(2):
                        m = nc.tensor.matmul(ps[:, 3, 0:T], z[:, 48 + q, s * P:(s + 1) * P], z[:, 41 + 2 * s + q, :],
                                             start=(q == 0 and s == 0), stop=(q == 1 and s == 1))
                m.then_inc(fo_pe.sem, 1)
                for n in range(1, 4 * groups):
                    unit(n)

            with pe.Fori(0, FG - 1) as g:
                fourier(g, 2)
            fourier(FG - 1, 1)
            with pe.Fori(0, HN // 2) as i:
                def fill(n):
                    g, q = n // 4, n % 4
                    product(i * 16 + (UNIT0["gates"] + n), i * 4 + (GROUP0["gates"] + g), (GROUP0["gates"] + g) % 2,
                            q, 4, q, a, 0, None, True)

                def after(w, engine, name):
                    st = (dn_act if engine == "act" else dn_dve)[w.w]
                    pe.wait_ge(st.sem, st.at(name, i))

                blk = lambda v, n: v[:, n * P:(n + 1) * P]
                for n in range(3):
                    fill(n)
                for w in ways:
                    after(w, "act", "sq")
                    nc.tensor.matmul(w.x_ps, ones[:], w.sq.rearrange("p a n -> p (a n)"), start=True, stop=True).then_inc(dn_pe[w.w].sem, 1)
                fill(3)
                for w in ways:
                    after(w, "dve", "kn")
                    after(w, "act", "sl2")
                    for n in range(4):
                        src = w.qk_feat[:, 1, :] if n < 2 else w.v_feat
                        m = nc.tensor.transpose(blk(w.y_ps, n), blk(src, n % 2), ident[:])
                    m.then_inc(dn_pe[w.w].sem, 1)
                    after(w, "dve", "gb")
                    for n in range(4):
                        m = nc.tensor.matmul(blk(w.x_ps, n), w.gate[:, n, :], tri[:, n // 2, :], start=True, stop=True)
                    m.then_inc(dn_pe[w.w].sem, 1)
                fill(4)
                for w in ways:
                    after(w, "act", "tok")
                    for y in (1, 0):
                        for c in range(TT):
                            m = nc.tensor.matmul(blk(w.y_ps, 2 * (1 - y) + c), blk(w.qk_feat[:, 1, :], c), blk(w.qk_feat[:, y, :], c),
                                                 start=True, stop=True)
                    m.then_inc(dn_pe[w.w].sem, 1)
                fill(5)
                for l in range(LEVELS):
                    fill(6 + l)
                    for w in ways:
                        after(w, "dve", f"u{l}" if l else "mm0")
                        for n in range(4):
                            m = nc.tensor.matmul(blk(w.x_ps, n), w.mm[:, n, :], w.t[:, n, :], start=True, stop=True)
                        m.then_inc(dn_pe[w.w].sem, 1)
                    for w in ways:
                        after(w, "act", f"x{l}")
                        for n in range(4):
                            if l < LEVELS - 1:
                                nc.tensor.matmul(blk(w.x_ps, n), w.u[:, n, :], w.x[:, n, :], start=True, stop=True)
                            m = nc.tensor.matmul(blk(w.y_ps, n), w.x[:, n, :], w.u[:, n, :], start=True, stop=True)
                        m.then_inc(dn_pe[w.w].sem, 1)
                fill(13)
                for w in ways:
                    after(w, "dve", f"u{LEVELS}")
                    for d in range(2):
                        m = nc.tensor.matmul(blk(w.x_ps, d), w.u[:, 3 * d, :], w.tok[:, 2 + d, :], start=True, stop=True)
                    m.then_inc(dn_pe[w.w].sem, 1)
                for w in ways:
                    after(w, "dve", "vkb")
                    for d in range(2):
                        m = nc.tensor.matmul(blk(w.y_ps, d), w.tok[:, d, :], w.v_dec[:, d, :], start=True, stop=True)
                    m.then_inc(dn_pe[w.w].sem, 1)
                fill(14)
                for w in ways:
                    after(w, "act", "s")
                    for y, bank in ((1, w.x_ps), (0, w.y_ps)):
                        for d in range(2):
                            m = nc.tensor.matmul(blk(bank, d), blk(w.qk_feat[:, y, :], 1 - d), w.x[:, d, :], start=True, stop=True)
                        m.then_inc(dn_pe[w.w].sem, 1)
                for w in ways:
                    after(w, "dve", "r2b")
                    for d in range(2):
                        m = nc.tensor.matmul(blk(w.x_ps, d), w.u[:, 2 * d + 1 - d, :], w.r[:, d, :], start=True, stop=True)
                    m.then_inc(dn_pe[w.w].sem, 1)
                fill(15)
                for w in ways:
                    after(w, "dve", "vn2b")
                    after(w, "act", "qs1")
                    for c in range(TT):
                        for d in range(2):
                            m = nc.tensor.matmul(blk(w.y_ps, c), w.qk[:, 2 * d + c, :], w.v_new[:, 2 * d + c, :], start=(d == 0), stop=(d == 1))
                    m.then_inc(dn_pe[w.w].sem, 1)
                for w in ways:
                    after(w, "dve", "on1")
                    for c in range(TT):
                        m = nc.tensor.transpose(blk(w.x_ps, c), w.u[:, c, :], ident[:])
                    m.then_inc(dn_pe[w.w].sem, 1)
            u0, g0 = UNIT0["mix"], GROUP0["mix"]
            for w in range(2):
                pe.wait_ge(dn_dve[w].sem, dn_dve[w].done(HN // 2))
            pe.wait_ge(fo_dve.sem, fo_dve.done(FG))
            with pe.Fori(0, 8) as g:
                run(g * 4 + u0, [0, 1], g * 2 + g0, g0 % 2, b, 0, None, True)
                run(g * 4 + (u0 + 2), [2, 3], g * 2 + (g0 + 1), (g0 + 1) % 2, b, 8, None, True)

            def mix_ready(c):
                if c % 2 == 0:
                    pe.wait_ge(mx_dve.sem, mx_dve.at("lo", c // 2))
            linear(UNIT0["w_o_2"], GROUP0["w_o_2"], 8, 4, a, waits=mix_ready)
            norm_sums(4)
            for ph in range(4):
                def hid_ready(c):
                    if c % 2 == 0:
                        pe.wait_ge(ml_dve.sem, ml_dve.at("lo", 8 * ph + c // 2))
                linear(UNIT0["mlp"] + 64 * ph, GROUP0["mlp"] + 16 * ph, 8, 4, a, waits=normed(4) if ph == 0 else None)
                linear(UNIT0["mlp"] + 64 * ph + 32, GROUP0["mlp"] + 16 * ph + 8, 8, 4, b, waits=hid_ready)
            norm_sums(5)
            for s in range(8):
                pe.wait_ge(nr_lo.sem, nr_lo.at(f"{s}", SPLIT_ROUND[5]))
                if s >= 2:
                    pe.wait_ge(fin_dve, s - 1)
                for q in range(TT):
                    for k in range(2):
                        m = nc.tensor.transpose(ps[:, 2 + s % 2, q * T + k * P:q * T + (k + 1) * P], z[:, 2 * s + k, q * P:(q + 1) * P], ident[:])
                m.then_inc(fin_pe, 1)


def _bfloat16(v):
    return (v.astype(np.float32).view(np.uint32) >> 16).astype(np.uint16)


def _tables():
    i = np.arange(P)
    upto = (i[:, None] <= i[None, :])
    tri = np.stack([upto, upto.T, i[:, None] > i[None, :], i[:, None] < i[None, :]], 1).astype(np.float32)
    q = np.arange(T).reshape(TT, P)
    causal = np.where(np.arange(T)[None, None, :] <= q.T[:, :, None], 0.0, -1.0e30)
    dm = np.where(upto, 0.0, -1.0e30)
    dmask = np.stack([dm, dm, dm.T, dm.T], 1)
    lmask = np.zeros((P, LEVELS, 2, P), np.float32)
    for level in range(LEVELS):
        w = 2 ** level
        same = (i[:, None] // (2 * w)) == (i[None, :] // (2 * w))
        low = same & (i[:, None] // w % 2 == 0) & (i[None, :] // w % 2 == 1)
        lmask[:, level, 0] = low
        lmask[:, level, 1] = low.T
    scale = (T * P) ** -0.5
    ang = 2 * np.pi * np.outer(i, i) / P
    angt = 2 * np.pi * (np.outer(np.arange(T), np.arange(T)) % T) / T
    dft = np.zeros((P, 5, T))
    dft[:, 0, 0:P], dft[:, 0, P:] = np.cos(ang), np.sin(ang)
    for k in range(TT):
        dft[:, 1 + k] = scale * np.cos(angt[k * P:(k + 1) * P])
        dft[:, 3 + k] = -scale * np.sin(angt[k * P:(k + 1) * P])
    return {"c_ident": np.eye(P, dtype=np.float32), "c_tri": tri, "c_causal": _bfloat16(causal), "c_dmask": _bfloat16(dmask),
            "c_lmask": _bfloat16(lmask), "c_dft": dft.astype(np.float32)}


def kernel(**inputs):
    import concourse.bacc as bacc
    from concourse.bass_utils import run_bass_kernel_spmd

    nc = bacc.Bacc("TRN2", target_bir_lowering=False, num_devices=1)
    arrays, t = {}, {}
    for name, a in {**inputs, **_tables()}.items():
        a = np.ascontiguousarray(a)
        if a.shape[0] == 1:
            a = a[0]
        arrays[f"in_{name}"] = a
        t[name] = nc.dram_tensor(f"in_{name}", a.shape, mybir.dt.from_np(a.dtype), kind="ExternalInput").ap()
    out = nc.dram_tensor("out_x", (T, D), F32, kind="ExternalOutput").ap()
    build(nc, t, out)
    r = run_bass_kernel_spmd(nc, [arrays], core_ids=[0])
    return r.results[0]["out_x"].reshape(1, T, D)
```
